# Optimizing a Trainium2 kernel written in Bass

```python
import jax
import jax.numpy as jnp
from jax import lax
import numpy as np

D_MODEL = 1024
BATCH = 1
SEQ = 512
DEPTH = 1
DEC_BATCH = 8
DEC_SEQ = 1
PAST_LEN = 1024
PAGE_SIZE = 128

MIX_WIDTH = D_MODEL
RWKV_WIDTH = MIX_WIDTH // 2
RWKV_HEAD = 64
RWKV_HEADS = RWKV_WIDTH // RWKV_HEAD
W_LORA = 64
A_LORA = 64
G_LORA = 128
RWKV_COLS = 3 * RWKV_WIDTH + W_LORA + A_LORA + G_LORA
SWA_WIDTH = MIX_WIDTH - RWKV_WIDTH
SWA_HEAD = 64
SWA_HEADS = SWA_WIDTH // SWA_HEAD
SWA_KV_HEADS = 2
KV_WIDTH = SWA_KV_HEADS * SWA_HEAD
SWA_COLS = SWA_WIDTH + 2 * KV_WIDTH
IN_COLS = RWKV_COLS + SWA_COLS
WINDOW = 128
BLOCK = 128
ROPE_THETA = 10000.0
MEM_TOKENS = 256
X_HEADS = 4
X_HEAD = 128
X_WIDTH = X_HEADS * X_HEAD
N_GROUPS = 4
EXPERTS_PER_GROUP = 8
TOP_K = 2
EXPERT_HIDDEN = 128
NORM_EPS = 1e-5
GN_EPS = 64e-5
L2_EPS = 1e-12

kernel_name = 'hymba_rwkv7_swa_sink_hmoe_step'

F32 = jnp.float32

def rms_norm(x, gain):
    xf = x.astype(F32)
    y = xf * lax.rsqrt(jnp.mean(xf * xf, axis=-1, keepdims=True) + NORM_EPS)
    return (y * gain.astype(F32)).astype(x.dtype)

def rope(x, pos):
    dh = x.shape[-1]
    half = dh // 2
    inv_freq = ROPE_THETA ** (-jnp.arange(half, dtype=F32) * 2.0 / dh)
    ang = pos.astype(F32)[:, None] * inv_freq[None, :]
    cos = jnp.cos(ang)[None, :, None, :]
    sin = jnp.sin(ang)[None, :, None, :]
    xf = x.astype(F32)
    x1, x2 = xf[..., :half], xf[..., half:]
    return jnp.concatenate([x1 * cos - x2 * sin, x2 * cos + x1 * sin], axis=-1).astype(x.dtype)

def rwkv7_time_mix(p, shift_prev, wkv0, lp):
    B, T, _ = p.shape
    C = RWKV_WIDTH
    pf = p.astype(F32)
    prev = jnp.concatenate([shift_prev.astype(F32)[:, None, :], pf[:, :-1]], axis=1)
    xm = pf + (prev - pf) * lp['mu_shift'].astype(F32)
    r = xm[..., :C]
    k = xm[..., C:2 * C]
    v = xm[..., 2 * C:3 * C]
    o = 3 * C
    xw = xm[..., o:o + W_LORA]
    xa = xm[..., o + W_LORA:o + W_LORA + A_LORA]
    xg = xm[..., o + W_LORA + A_LORA:]
    w = -jax.nn.softplus(-(lp['w_decay0'].astype(F32) + jnp.tanh(xw) @ lp['w_decay_up'].astype(F32))) - 0.5
    decay = jnp.exp(-jnp.exp(w))
    a = jax.nn.sigmoid(lp['a0'].astype(F32) + xa @ lp['w_a_up'].astype(F32))
    g = jax.nn.sigmoid(xg) @ lp['w_g_up'].astype(F32)

    def heads(t):
        return t.reshape(B, T, RWKV_HEADS, RWKV_HEAD)

    kk = heads(k * lp['k_k'].astype(F32))
    kk = kk / jnp.maximum(jnp.sqrt(jnp.sum(kk * kk, axis=-1, keepdims=True)), L2_EPS)
    k = k * (1.0 + (a - 1.0) * lp['k_a'].astype(F32))
    rh, wh, kh, vh, ah = heads(r), heads(decay), heads(k), heads(v), heads(a)
    seq = (jnp.moveaxis(rh, 1, 0), jnp.moveaxis(wh, 1, 0), jnp.moveaxis(kh, 1, 0),
           jnp.moveaxis(vh, 1, 0), jnp.moveaxis(-kk, 1, 0), jnp.moveaxis(kk * ah, 1, 0))

    def step(S, inp):
        r_t, w_t, k_t, v_t, a_t, b_t = inp
        sa = jnp.einsum('bhij,bhj->bhi', S, a_t)
        S = S * w_t[:, :, None, :] + sa[..., None] * b_t[:, :, None, :] + v_t[..., None] * k_t[:, :, None, :]
        return S, jnp.einsum('bhij,bhj->bhi', S, r_t)

    S_final, y = lax.scan(step, wkv0.astype(F32), seq)
    y = jnp.moveaxis(y, 0, 1)
    mu = jnp.mean(y, axis=-1, keepdims=True)
    var = jnp.mean(jnp.square(y - mu), axis=-1, keepdims=True)
    yn = ((y - mu) * lax.rsqrt(var + GN_EPS)).reshape(B, T, C)
    yn = yn * lp['ln_x_w'].astype(F32) + lp['ln_x_b'].astype(F32)
    bonus = jnp.sum(rh * kh * lp['r_k'].astype(F32), axis=-1, keepdims=True) * vh
    out = (yn + bonus.reshape(B, T, C)) * g
    return out.astype(p.dtype), p[:, -1], S_final.astype(wkv0.dtype)

def sink_softmax(s, sink):
    hkv, gq = s.shape[-4], s.shape[-3]
    col = jnp.broadcast_to(sink.astype(F32).reshape(hkv, gq, 1, 1), s.shape[:-1] + (1,))
    return jax.nn.softmax(jnp.concatenate([s, col], axis=-1), axis=-1)[..., :-1]

def swa_banded(q, k, v, sink):
    B, T, Hq, Dh = q.shape
    Hkv = k.shape[2]
    G = Hq // Hkv
    NB = T // BLOCK
    qb = q.reshape(B, NB, BLOCK, Hkv, G, Dh).astype(F32)

    def band(t):
        tb = t.reshape(B, NB, BLOCK, Hkv, Dh)
        prev = jnp.concatenate([jnp.zeros_like(tb[:, :1]), tb[:, :-1]], axis=1)
        return jnp.concatenate([prev, tb], axis=2)

    kc, vc = band(k), band(v)
    s = jnp.einsum('bnqkgd,bnskd->bnkgqs', qb, kc.astype(F32)) * (Dh ** -0.5)
    i = jnp.arange(BLOCK)[:, None]
    j = jnp.arange(2 * BLOCK)[None, :]
    diff = i + BLOCK - j
    blk = jnp.arange(NB)[:, None, None]
    valid = (diff >= 0) & (diff < WINDOW) & ((blk > 0) | (j >= BLOCK))
    s = jnp.where(valid[None, :, None, None], s, -jnp.inf)
    pr = sink_softmax(s, sink)
    o = jnp.einsum('bnkgqs,bnskd->bnqkgd', pr.astype(v.dtype), vc)
    return o.reshape(B, T, Hq * Dh)

def swa_with_buffer(q, k, v, pos, k_past, v_past, sink):
    B, T, Hq, Dh = q.shape
    Hkv = k.shape[2]
    G = Hq // Hkv
    WB = k_past.shape[1]
    kc = jnp.concatenate([k_past.astype(k.dtype), k], axis=1)
    vc = jnp.concatenate([v_past.astype(v.dtype), v], axis=1)
    kpos = jnp.concatenate([pos[0] - WB + jnp.arange(WB, dtype=jnp.int32), pos])
    diff = pos[:, None] - kpos[None, :]
    valid = (diff >= 0) & (diff < WINDOW)
    qg = q.reshape(B, T, Hkv, G, Dh).astype(F32)
    s = jnp.einsum('btkgd,bskd->bkgts', qg, kc.astype(F32)) * (Dh ** -0.5)
    s = jnp.where(valid, s, -jnp.inf)
    pr = sink_softmax(s, sink)
    o = jnp.einsum('bkgts,bskd->btkgd', pr.astype(vc.dtype), vc)
    return o.reshape(B, T, Hq * Dh), kc[:, -WB:], vc[:, -WB:]

def hybrid_mixer(h, pos, shift_prev, wkv0, k_past, v_past, lp):
    B, T, _ = h.shape
    proj = h @ lp['w_in']
    p_rwkv = proj[..., :RWKV_COLS]
    p_swa = proj[..., RWKV_COLS:]
    y_rwkv, new_shift, new_wkv = rwkv7_time_mix(p_rwkv, shift_prev, wkv0, lp)
    q = rope(p_swa[..., :SWA_WIDTH].reshape(B, T, SWA_HEADS, SWA_HEAD), pos)
    k = rope(p_swa[..., SWA_WIDTH:SWA_WIDTH + KV_WIDTH].reshape(B, T, SWA_KV_HEADS, SWA_HEAD), pos)
    v = p_swa[..., SWA_WIDTH + KV_WIDTH:].reshape(B, T, SWA_KV_HEADS, SWA_HEAD)
    if k_past is None:
        y_swa = swa_banded(q, k, v, lp['attn_sink'])
        wb = min(WINDOW, T)
        new_k, new_v = k[:, T - wb:], v[:, T - wb:]
    else:
        y_swa, new_k, new_v = swa_with_buffer(q, k, v, pos, k_past, v_past, lp['attn_sink'])
    y = jnp.concatenate([y_rwkv, y_swa.astype(y_rwkv.dtype)], axis=-1) @ lp['w_out']
    return y, new_shift, new_wkv, new_k, new_v

def memory_kv(mem, lp):
    B, M, _ = mem.shape
    mn = rms_norm(mem, lp['norm_mem'])
    mk = (mn @ lp['w_ck']).reshape(B, M, X_HEADS, X_HEAD)
    mv = (mn @ lp['w_cv']).reshape(B, M, X_HEADS, X_HEAD)
    return mk, mv

def memory_cross_attention(h, mk, mv, lp):
    B, T, _ = h.shape
    q = (h @ lp['w_cq']).reshape(B, T, X_HEADS, X_HEAD)
    s = jnp.einsum('bthd,bshd->bhts', q.astype(F32), mk.astype(F32)) * (X_HEAD ** -0.5)
    pr = jax.nn.softmax(s, axis=-1)
    o = jnp.einsum('bhts,bshd->bthd', pr.astype(mv.dtype), mv).reshape(B, T, X_WIDTH)
    return o @ lp['w_co']

def hierarchical_moe(h, lp):
    B, T, D = h.shape
    hf = h.reshape(B * T, D)
    lg = (hf @ lp['w_group_router'] + lp['b_group_router']).astype(F32)
    pg = jax.nn.softmax(lg, axis=-1)
    gsel = jnp.argmax(lg, axis=-1)
    onehot_g = jax.nn.one_hot(gsel, N_GROUPS, dtype=F32)
    p_sel = jnp.sum(pg * onehot_g, axis=-1)
    le = (hf @ lp['w_expert_router'] + lp['b_expert_router']).astype(F32)
    le = le.reshape(-1, N_GROUPS, EXPERTS_PER_GROUP)
    le_sel = jnp.take_along_axis(le, gsel[:, None, None], axis=1)[:, 0]
    top_v, top_i = lax.top_k(le_sel, TOP_K)
    top_w = jax.nn.softmax(top_v, axis=-1)
    gate_e = jnp.sum(jax.nn.one_hot(top_i, EXPERTS_PER_GROUP, dtype=F32) * top_w[..., None], axis=1)
    gate = onehot_g[:, :, None] * (p_sel[:, None] * gate_e)[:, None, :]
    out = jnp.zeros((B * T, D), h.dtype)
    for gi in range(N_GROUPS):
        hg = jnp.einsum('nd,edf->nef', hf, lp['w_exp_gate'][gi])
        hu = jnp.einsum('nd,edf->nef', hf, lp['w_exp_up'][gi])
        act = jax.nn.silu(hg) * hu * gate[:, gi, :, None].astype(hf.dtype)
        out = out + jnp.einsum('nef,efd->nd', act, lp['w_exp_down'][gi])
    return out.reshape(B, T, D)

def decoder_layer(x, pos, shift_prev, wkv0, k_past, v_past, mem_k, mem_v, lp):
    y, new_shift, new_wkv, new_k, new_v = hybrid_mixer(rms_norm(x, lp['norm_mix']), pos, shift_prev, wkv0, k_past, v_past, lp)
    x = x + y
    x = x + memory_cross_attention(rms_norm(x, lp['norm_cross']), mem_k, mem_v, lp)
    x = x + hierarchical_moe(rms_norm(x, lp['norm_ffn']), lp)
    return x, new_shift, new_wkv, new_k, new_v

def setup_inputs(seed: int = 0) -> dict:
    key = jax.random.key(seed)
    ks = iter(jax.random.split(key, 64))
    L = DEPTH
    G, E, FH = N_GROUPS, EXPERTS_PER_GROUP, EXPERT_HIDDEN
    wb = min(WINDOW, PAST_LEN)

    def nrm(shape, scale=1.0):
        return jax.random.normal(next(ks), shape, F32) * scale

    def gain(shape):
        return 1.0 + 0.1 * jax.random.normal(next(ks), shape, F32)

    def unif(shape, lo, hi):
        return jax.random.uniform(next(ks), shape, F32, lo, hi)

    return {
        'x_prompt': nrm((BATCH, SEQ, D_MODEL)),
        'x_sample': nrm((DEC_BATCH, DEC_SEQ, D_MODEL)),
        'mem_prompt': nrm((BATCH, MEM_TOKENS, D_MODEL)),
        'state_rwkv_shift': nrm((L, DEC_BATCH, RWKV_COLS)),
        'state_rwkv_wkv': nrm((L, DEC_BATCH, RWKV_HEADS, RWKV_HEAD, RWKV_HEAD), 0.5),
        'cache_swa_k': nrm((L, DEC_BATCH, wb, SWA_KV_HEADS, SWA_HEAD)),
        'cache_swa_v': nrm((L, DEC_BATCH, wb, SWA_KV_HEADS, SWA_HEAD)),
        'cache_mem_k': nrm((L, DEC_BATCH, MEM_TOKENS, X_HEADS, X_HEAD)),
        'cache_mem_v': nrm((L, DEC_BATCH, MEM_TOKENS, X_HEADS, X_HEAD)),
        'norm_mix': gain((L, D_MODEL)),
        'w_in': nrm((L, D_MODEL, IN_COLS), D_MODEL ** -0.5),
        'mu_shift': unif((L, RWKV_COLS), 0.0, 1.0),
        'w_decay0': unif((L, RWKV_WIDTH), -6.0, -1.0),
        'w_decay_up': nrm((L, W_LORA, RWKV_WIDTH), 0.5 * W_LORA ** -0.5),
        'a0': nrm((L, RWKV_WIDTH), 0.1),
        'w_a_up': nrm((L, A_LORA, RWKV_WIDTH), A_LORA ** -0.5),
        'w_g_up': nrm((L, G_LORA, RWKV_WIDTH), G_LORA ** -0.5),
        'k_k': 0.85 + nrm((L, RWKV_WIDTH), 0.1),
        'k_a': gain((L, RWKV_WIDTH)),
        'r_k': nrm((L, RWKV_HEADS, RWKV_HEAD), 0.1),
        'ln_x_w': gain((L, RWKV_WIDTH)),
        'ln_x_b': nrm((L, RWKV_WIDTH), 0.01),
        'attn_sink': nrm((L, SWA_HEADS), 0.5),
        'w_out': nrm((L, MIX_WIDTH, D_MODEL), MIX_WIDTH ** -0.5),
        'norm_cross': gain((L, D_MODEL)),
        'norm_mem': gain((L, D_MODEL)),
        'w_cq': nrm((L, D_MODEL, X_WIDTH), D_MODEL ** -0.5),
        'w_ck': nrm((L, D_MODEL, X_WIDTH), D_MODEL ** -0.5),
        'w_cv': nrm((L, D_MODEL, X_WIDTH), D_MODEL ** -0.5),
        'w_co': nrm((L, X_WIDTH, D_MODEL), X_WIDTH ** -0.5),
        'norm_ffn': gain((L, D_MODEL)),
        'w_group_router': nrm((L, D_MODEL, G), D_MODEL ** -0.5),
        'b_group_router': nrm((L, G), 0.01),
        'w_expert_router': nrm((L, D_MODEL, G * E), D_MODEL ** -0.5),
        'b_expert_router': nrm((L, G * E), 0.01),
        'w_exp_gate': nrm((L, G, E, D_MODEL, FH), D_MODEL ** -0.5),
        'w_exp_up': nrm((L, G, E, D_MODEL, FH), D_MODEL ** -0.5),
        'w_exp_down': nrm((L, G, E, FH, D_MODEL), FH ** -0.5),
        'norm_final': gain((D_MODEL,)),
    }

def reference(x_prompt, x_sample, mem_prompt, state_rwkv_shift, state_rwkv_wkv, cache_swa_k, cache_swa_v,
              cache_mem_k, cache_mem_v, norm_mix, w_in, mu_shift, w_decay0, w_decay_up, a0, w_a_up, w_g_up,
              k_k, k_a, r_k, ln_x_w, ln_x_b, attn_sink, w_out, norm_cross, norm_mem, w_cq, w_ck, w_cv, w_co,
              norm_ffn, w_group_router, b_group_router, w_expert_router, b_expert_router, w_exp_gate,
              w_exp_up, w_exp_down, norm_final):
    bp = x_prompt.shape[0]
    pos_p = jnp.arange(x_prompt.shape[1], dtype=jnp.int32)
    pos_s = PAST_LEN + jnp.arange(x_sample.shape[1], dtype=jnp.int32)
    xp, xs = x_prompt, x_sample
    p_shift, p_wkv, p_k, p_v, p_mk, p_mv = [], [], [], [], [], []
    s_shift, s_wkv, s_k, s_v = [], [], [], []
    for l in range(DEPTH):
        lp = dict(norm_mix=norm_mix[l], w_in=w_in[l], mu_shift=mu_shift[l], w_decay0=w_decay0[l],
                  w_decay_up=w_decay_up[l], a0=a0[l], w_a_up=w_a_up[l], w_g_up=w_g_up[l], k_k=k_k[l],
                  k_a=k_a[l], r_k=r_k[l], ln_x_w=ln_x_w[l], ln_x_b=ln_x_b[l], attn_sink=attn_sink[l],
                  w_out=w_out[l], norm_cross=norm_cross[l], norm_mem=norm_mem[l], w_cq=w_cq[l], w_ck=w_ck[l],
                  w_cv=w_cv[l], w_co=w_co[l], norm_ffn=norm_ffn[l], w_group_router=w_group_router[l],
                  b_group_router=b_group_router[l], w_expert_router=w_expert_router[l],
                  b_expert_router=b_expert_router[l], w_exp_gate=w_exp_gate[l], w_exp_up=w_exp_up[l],
                  w_exp_down=w_exp_down[l])
        mk_p, mv_p = memory_kv(mem_prompt, lp)
        shift0 = jnp.zeros((bp, RWKV_COLS), xp.dtype)
        wkv_init = jnp.zeros((bp, RWKV_HEADS, RWKV_HEAD, RWKV_HEAD), state_rwkv_wkv.dtype)
        xp, sh, wk, kn, vn = decoder_layer(xp, pos_p, shift0, wkv_init, None, None, mk_p, mv_p, lp)
        p_shift.append(sh); p_wkv.append(wk); p_k.append(kn); p_v.append(vn); p_mk.append(mk_p); p_mv.append(mv_p)
        xs, sh, wk, kn, vn = decoder_layer(xs, pos_s, state_rwkv_shift[l], state_rwkv_wkv[l], cache_swa_k[l],
                                           cache_swa_v[l], cache_mem_k[l], cache_mem_v[l], lp)
        s_shift.append(sh); s_wkv.append(wk); s_k.append(kn); s_v.append(vn)
    y_prompt = rms_norm(xp, norm_final)
    y_sample = rms_norm(xs, norm_final)
    prompt_shift = jnp.stack(p_shift)
    prompt_wkv = jnp.stack(p_wkv)
    prompt_swa_k = jnp.stack(p_k)
    prompt_swa_v = jnp.stack(p_v)
    prompt_mem_k = jnp.stack(p_mk)
    prompt_mem_v = jnp.stack(p_mv)
    sample_shift = jnp.stack(s_shift)
    sample_wkv = jnp.stack(s_wkv)
    sample_swa_k = jnp.stack(s_k)
    sample_swa_v = jnp.stack(s_v)
    return (y_prompt, y_sample, prompt_shift, prompt_wkv, prompt_swa_k, prompt_swa_v, prompt_mem_k,
            prompt_mem_v, sample_shift, sample_wkv, sample_swa_k, sample_swa_v)


_drawn_inputs = setup_inputs


def setup_inputs(seed=0):
    import zlib

    import numpy as np

    out = dict(_drawn_inputs(seed))
    spreads = {}
    factors = {'ln_x_b': 3.876, 'attn_sink': 5.949, 'b_group_router': 32.1, 'b_expert_router': 3.473}
    for name, (base, spread) in spreads.items():
        noise = np.random.default_rng([zlib.crc32(name.encode()), seed]).standard_normal(out[name].shape)
        drawn = base * np.exp(spread * noise) if base else spread * noise
        out[name] = jnp.asarray(drawn.astype(out[name].dtype))
    for name, factor in factors.items():
        out[name] = (out[name] * factor).astype(out[name].dtype)
    return out
```

```python
from contextlib import ExitStack

import numpy as np

import concourse.bass as bass
from concourse import mybir

F32 = mybir.dt.float32
I32 = mybir.dt.int32
U32 = mybir.dt.uint32
ALU = mybir.AluOpType
ACT = mybir.ActivationFunctionType
X = mybir.AxisListType.X

P = 128
D = 1024
KD = D // P
SEQ = 512
NS = 8
NT = SEQ + NS
HALF = NT // 2
TILES = SEQ // P
H = 8
HD = 64
PAIRS = H // 2
CH = 64
NCH = SEQ // CH
RW = 14
SW = 6
RCOLS = RW * P
MT = 256
XH = 4
EPS = 1e-5
GN_EPS = 64e-5
L2_EPS = 1e-12
KAPPA = float(np.exp(-0.5))
NEG = -1e30
NE = 32
FH = 128
PAIRS_E = 2 * NT
NBLK = NE + (PAIRS_E - NE) // P
BANKS = 8

PAR_ROWS = (("mu_shift", 14), ("w_decay0", 4), ("a0", 4), ("k_k", 4), ("k_a", 4), ("r_k", 4), ("ln_x_w", 4),
            ("ln_x_b", 4))


CROSS_ORDER = (("xs", 0), ("ckT", 0), ("xs", 1), ("ckT", 1), ("xp", 0), ("cs", 0), ("xs", 2), ("ckT", 2), ("cs", 1),
               ("ckT", 3), ("xp", 1), ("cs", 2), ("xs", 3), ("ckT", 4), ("cs", 3), ("ckT", 5), ("cs", 4),
               ("xp", 2), ("ckT", 6), ("cs", 5), ("ckT", 7), ("cs", 6), ("xp", 3), ("cs", 7))


def tile_rows(t):
    return P if t < TILES else NS


def bank_plan():
    g = [(("par",), "v"), (("shift_in",), "v")]
    for t in range(TILES + 1):
        g += [(("xT", t, i), "v") for i in range(2)]
    for j in (12, 13, 14, 15, 4, 5, 6, 7, 0, 1, 2, 3, 8, 9, 10, 11, 16, 17, 18, 19):
        g += [(("proj", j, s), "a") for s in range(2)]
        if j == 15:
            for t in range(2):
                g += [(("mT", t, i), "v") for i in range(2)]
    g += [(("lora_w", c, s), "a") for c in range(4) for s in range(2)]
    g += [(("lora_a", c, s), "a") for c in range(4) for s in range(2)]
    g += [(("mk", t), "a") for t in range(2)]
    g += [(("mv", t), "a") for t in range(2)]
    g += [(("mkT", t), "a") for t in range(2)]
    g += [(("shift_out", i), "a") for i in range(4)]
    g += [(("tokV", t), "a") for t in range(TILES)]
    for c in range(4):
        g += [(("norm_k", c, s), "a") for s in range(2)]
        g += [(("bonus", c, s), "v") for s in range(2)]
    g += [(("svec", i), "a") for i in range(6)]
    for t in range(TILES):
        g += [(("tok", t, i), "a") for i in range(3)]
        g += [(("AB", t, h), "v") for h in range(H)]
        g += [(("N0", t, q), "a") for q in range(2)]
        for k in range(6):
            for q in range(2):
                if k > 0:
                    g += [(("XM", t, q, k), "v")]
                if k < 4:
                    g += [(("MM", t, q, k), "a")]
                if k < 5:
                    g += [(("NN", t, q, k), "v" if k % 2 else "a")]
        g += [(("akv", t), "v"), (("G", t), "v"), (("WT", t), "a")]
        for u in range(2):
            g += [(("U", t, u, 0), "v"), (("U", t, u, 1), "v"), (("S", t, u), "v")]
        g += [(("Y", t), "a")]
    g += [(("wkvT",), "a"), (("ysT",), "v")]
    g += [(("mean", c, s), "v") for c in range(4) for s in range(2)]
    g += [(("var", c, s), "a") for c in range(4) for s in range(2)]
    g += [(("gate", c, s), "v") for c in range(4) for s in range(2)]
    for s in range(2):
        for i in range(2):
            g += [(("rka", i, s), "v"), (("rkb", i, s), "v")]
        g += [(("rq", c, s), "v") for c in range(4)]
    g += [(("vtok",), "a"), (("kvout",), "a")]
    for t in range(-1, TILES):
        if t < TILES - 1:
            g += [(("s", t + 1, e, i), "v") for e in range(2) for i in range(2)]
        if t >= 0:
            g += [(("pT", t, i), "a") for i in range(4)]
            g += [(("o", t), "a")]
    g += [(("qd", e), "v") for e in range(2)]
    g += [(("kT", i), "a") for i in range(2)]
    g += [(("ss", e), "v") for e in range(2)]
    g += [(("ssT",), "v"), (("spT",), "v"), (("so",), "v")]
    g += [(("wo", t, n), "v") for t in range(TILES + 1) for n in range(2)]
    for t in range(TILES + 1):
        g += [(("xT2", t, i), "v") for i in range(2)]
    g += [(("q", h, s), "a") for h in range(XH) for s in range(2)]
    for step in CROSS_ORDER:
        what, n = step
        g += {"xs": [(("xs", n, i), "v") for i in range(2)],
              "xp": [(("xpT", n, i), "a") for i in range(2)] + [(("xo", n), "a")],
              "ckT": [(("ckT", n, i), "a") for i in range(2)],
              "cs": [(("cs", n), "v")]}[what]
    g += [(("csT",), "v"), (("cpT",), "v"), (("co",), "v")]
    g += [(("wc", t, n), "v") for t in range(TILES + 1) for n in range(2)]
    for t in range(TILES + 1):
        g += [(("xT3", t, i), "v") for i in range(2)]
    g += [(("route", t), "v") for t in range(TILES + 1)]
    g += [(("ranks",), "v"), (("slots",), "v")]
    return g


def small_kernel(nc, A, O):
    plan = bank_plan()
    place = {key: n for n, (key, _) in enumerate(plan)}
    rank, count = {}, {"v": 0, "a": 0}
    for key, e in plan:
        count[e] += 1
        rank[key] = (e, count[e])

    with ExitStack() as ctx:
        def sem(name):
            return ctx.enter_context(nc.semaphore(name))

        arena = ctx.enter_context(nc.sbuf_tensor("arena", [P, 53150], F32))
        at = {}

        def region(name, words, start=None):
            if start is None:
                start = at["_end"]
                at["_end"] = start + words
            at[name] = start
            return arena[:, start:start + words]

        at["_end"] = 0
        ident = region("ident", P)
        bones = region("bones", P)
        maskAB = region("maskAB", 4 * P).rearrange("p (a t) -> p a t", a=4)
        swamask = region("swamask", 2 * P)
        tri = region("tri", P)
        sel = region("sel", 5 * P).rearrange("p (a t) -> p a t", a=5)
        cosT = region("cosT", NT)
        sinT = region("sinT", NT)
        misc = region("misc", 64)
        gains = region("gains", 4 * KD).rearrange("p (a k) -> p a k", a=4)
        par = region("par", 48)
        small = region("small", 64)
        lora = region("lora", 512)
        gup = region("gup", 512)
        mkT = region("mkT", XH * MT).rearrange("p (h s) -> p h s", h=XH)
        mv = region("mv", 2 * 512).rearrange("p (t n) -> p t n", t=2)
        stat = region("stat", 64)
        stats = [stat[:, 32 * i:32 * i + 32] for i in range(2)]
        sinks = region("sinks", 2 * H)
        saved = region("saved", RW * 9).rearrange("p (j n) -> p j n", j=RW)
        shiftS = region("shiftS", RW * NS).rearrange("p (j n) -> p j n", j=RW)
        PC = region("PC", 32).rearrange("p (c n) -> p c n", c=4)
        wS = region("wS", 32).rearrange("p (c n) -> p c n", c=4)
        hA = region("hA", KD * NT).rearrange("p (k n) -> p k n", k=KD)
        hB = region("hB", KD * NT).rearrange("p (k n) -> p k n", k=KD)
        ring = [region(f"ring{i}", 4096) for i in range(3)]
        PR = region("PR", RW * (NT + 1)).rearrange("p (j n) -> p j n", j=RW)
        SQ = region("SQ", SW * NT).rearrange("p (j n) -> p j n", j=SW)
        B0 = region("B0", 4 * NT).rearrange("p (c n) -> p c n", c=4)
        B1 = region("B1", 4 * NT).rearrange("p (c n) -> p c n", c=4)
        xreg = region("x", 5 * D)
        x = xreg.rearrange("p (t n) -> p t n", t=5)
        tokV = region("tokV", TILES * 512).rearrange("p (t n) -> p t n", t=TILES)
        STr = region("ST", 9 * 256)
        ST = STr.rearrange("p (s c i) -> p s c i", s=9, c=4)
        assert at["_end"] <= 53150, at["_end"]
        memT = arena[:, at["hB"]:at["hB"] + KD * MT].rearrange("p (k n) -> p k n", k=KD)
        memX = arena[:, at["hB"] + 2080:at["hB"] + 2080 + 2048].rearrange("p (t n) -> p t n", t=2)
        mkS = arena[:, at["hB"] + 2080:at["hB"] + 2080 + 1024].rearrange("p (t n) -> p t n", t=2)
        junk = arena[:, at["B0"]:at["B0"] + D]
        prow = arena[:, at["B0"] + 1100:at["B0"] + 1100 + P]
        srow = arena[:, at["B1"]:at["B1"] + RCOLS]
        sg = arena[:, at["x"]:at["x"] + 2080].rearrange("p (c n) -> p c n", c=4)
        aa = arena[:, at["x"] + 2080:at["x"] + 4160].rearrange("p (c n) -> p c n", c=4)
        reset = arena[:, at["x"] + 4160:at["x"] + 4160 + SEQ]
        tmp = [STr[:, i * NT:(i + 1) * NT] for i in range(4)]
        Bt = hA[:, 0:4, :]
        Kt = hA[:, 4:8, :]
        Xi = arena[:, at["x"]:at["x"] + 1024].rearrange("p (h t) -> p h t", h=H)
        Mi = [arena[:, at["x"] + 1024 * (1 + i):at["x"] + 1024 * (2 + i)].rearrange("p (h t) -> p h t", h=H)
              for i in range(2)]
        Ni = [arena[:, at["x"] + 1024 * (3 + i):at["x"] + 1024 * (4 + i)].rearrange("p (h t) -> p h t", h=H)
              for i in range(2)]
        AB = ring[1].rearrange("p (h a t) -> p h a t", h=H, a=4)
        tokX = ring[2][:, 0:1536].rearrange("p (i n) -> p i n", i=3)
        akv = ring[2][:, 1536:2048]
        Gt = ring[2][:, 2048:2560]
        WT = ring[2][:, 2560:3072].rearrange("p (c t) -> p c t", c=4)
        Ut = ring[2][:, 3072:3584]
        yT = hB
        SS = arena[:, at["hB"] + 2080:at["hB"] + 2080 + 2048].rearrange("p (i j) -> p i j", i=32)
        Stmp = ring[0][:, 0:2048].rearrange("p (i j) -> p i j", i=32)
        sv = ring[0][:, 3072:3072 + 5 * HD].rearrange("p (a j) -> p a j", a=5)
        svv = ring[0][:, 3400:3432]
        ssa = ring[0][:, 3432:3464]
        sy = ring[0][:, 3464:3496]
        svt6 = ring[0][0:NS, 0:3072].rearrange("p (a n) -> p a n", a=6)
        shiftO = arena[0:9, at["tokV"]:at["tokV"] + RCOLS]
        wkvO = ring[1][0:64, 0:512]
        RK = [hA.rearrange("p k n -> p (k n)")[:, i * NT:(i + 1) * NT] for i in range(2)]
        hAf = arena[:, at["hA"]:at["hA"] + KD * NT]
        vtok = hAf[:, 1040:1552].rearrange("p (t n) -> p t n", t=4)
        PTa = hAf[:, 1552:3600].rearrange("p (h a q) -> p h a q", h=H, a=2)
        PTc = arena[:, at["tokV"]:at["tokV"] + 1024].rearrange("p (h a q) -> p h a q", h=XH, a=2)
        kvO = hAf[:, 3600:3984]
        Sm = [ring[2][:, 2048 * i:2048 * (i + 1)] for i in range(2)]
        ropeT = arena[:, at["B0"]:at["B0"] + HALF]
        Kc = arena[:, at["tokV"]:at["tokV"] + 1024].rearrange("p (b n) -> p b n", b=NS)
        Vc = arena[:, at["tokV"] + 1024:at["tokV"] + 2048].rearrange("p (b n) -> p b n", b=NS)
        kTs = STr[:, 0:1024].rearrange("p (b s) -> p b s", b=NS)
        QD = STr[:, 1024:1088].rearrange("p (b c e) -> p b c e", b=NS, c=4)
        sT = STr[:, 2048:2048 + 64]
        pTs = STr[:, 2112:2112 + 64]
        xn = [arena[:, at["PR"] + i * D:at["PR"] + (i + 1) * D] for i in range(2)]
        kv_ring = [arena[:, at["PR"] + (2 + i) * 1024:at["PR"] + (3 + i) * 1024].rearrange("p (a n) -> p a n", a=2)
                   for i in range(4)]
        late = [hAf[:, i * 1024:(i + 1) * 1024].rearrange("p (a n) -> p a n", a=2) for i in range(4)]

        def values_of(b):
            return kv_ring[b] if b < 4 else late[b - 4]

        KT = [arena[:, at["B1"] + i * 1024:at["B1"] + (i + 1) * 1024].rearrange("p (h a s) -> p h a s", h=XH, a=2)
              for i in range(2)]
        csS = STr[:, 0:64].rearrange("p (a n) -> p a n", a=2)
        cpS = STr[:, 64:128].rearrange("p (a n) -> p a n", a=2)
        qT = SQ[:, 0:4, :]
        iota = misc[:, 0:NBLK]
        pair_no = misc[:, NBLK:NBLK + 10].rearrange("p (t j) -> p t j", j=2)
        valid = misc[:, NBLK + 10:NBLK + 15]
        NB3 = 3
        we = [arena[:, at["ring0"] + i * 3072:at["ring0"] + (i + 1) * 3072].rearrange("p (a n) -> p a n", a=3)
              for i in range(NB3)]
        xg = [arena[:, at["ring0"] + 9216 + i * D:at["ring0"] + 9216 + (i + 1) * D] for i in range(NB3)]
        yb = [arena[:, at["PR"] + (2 + i) * D:at["PR"] + (3 + i) * D] for i in range(NB3)]
        xTe = arena[:, at["PR"] + 5 * D:at["PR"] + 6 * D].rearrange("p (k n) -> p k n", k=KD)
        silu, act_e, actT = [arena[:, at["PR"] + 6 * D + i * P:at["PR"] + 6 * D + (i + 1) * P] for i in range(3)]
        gfin = arena[:, at["tokV"] + 1024:at["tokV"] + 2048]
        wrG = STr[:, 256:288].rearrange("p (k n) -> p k n", k=KD)
        wrE = STr[:, 288:544].rearrange("p (k n) -> p k n", k=KD)
        rbias = STr[:, 544:580]
        ydt = [arena[:, at["ring0"] + i * 2048:at["ring0"] + (i + 1) * 2048].rearrange("p (j n) -> p j n", j=2)
               for i in range(2)]
        hBf = arena[:, at["hB"]:at["hB"] + KD * NT]
        off = [0]

        def route_region(n, dt=None):
            v = hBf[:, off[0]:off[0] + n]
            off[0] += n
            return v if dt is None else v.bitcast(dt)

        T5 = TILES + 1
        Lg = route_region(T5 * 36).rearrange("p (t n) -> p t n", t=T5)
        Le = route_region(T5 * NE).rearrange("p (t n) -> p t n", t=T5)
        Ta = route_region(T5 * NE).rearrange("p (t n) -> p t n", t=T5)
        oh = [route_region(T5 * NE).rearrange("p (t n) -> p t n", t=T5) for _ in range(2)]
        ohg = route_region(T5 * 4).rearrange("p (t n) -> p t n", t=T5)
        Mk = route_region(T5 * NE).rearrange("p (t n) -> p t n", t=T5)
        RC = route_region(6 * NE)
        slot_all = route_region(T5 * NE).rearrange("p (t n) -> p t n", t=T5)
        gmx, psel, m1, m2, mi, ee = [route_region(T5) for _ in range(6)]
        cw = [route_region(T5) for _ in range(2)]
        sl = [route_region(T5) for _ in range(2)]
        slI = [route_region(T5, I32) for _ in range(2)]
        nb, nb1, cum, zer = [route_region(NE) for _ in range(4)]
        big = route_region(NBLK * NE).rearrange("p (b e) -> p b e", b=NBLK)
        eid = route_region(NBLK)
        eidI = route_region(NBLK, I32)
        slot_rows = route_region(P)
        pidI = route_region(NBLK, I32)
        tokI = route_region(NBLK, I32)
        idg = [route_region(1, I32) for _ in range(NB3)]
        ids = [route_region(1, I32) for _ in range(NB3)]
        onesm = route_region(P)
        scrap = route_region(2)
        assert off[0] <= KD * NT
        banks = [ctx.enter_context(nc.psum_tensor(f"bank{i}", [P, 512], F32)) for i in range(BANKS)]

        vec_d = nc.dram_tensor("vec_d", (6, NS, 512), F32, kind="Internal").ap()
        hn_d = nc.dram_tensor("hn_d", (NT, D), F32, kind="Internal").ap()
        slot_d = nc.dram_tensor("slot_d", (NBLK * P, 1), F32, kind="Internal").ap()
        pair_d = nc.dram_tensor("pair_d", (PAIRS_E, D), F32, kind="Internal").ap()
        ys_d = nc.dram_tensor("ys_d", (NS, 512), F32, kind="Internal").ap()

        full = sem("psum_full")
        evac = {"v": sem("emptied_by_vector"), "a": sem("emptied_by_scalar")}
        s_const = sem("constants_loaded")
        s_par = sem("params_loaded")
        s_x = [sem(f"x_loaded{t}") for t in range(5)]
        s_mem = sem("mem_loaded")
        s_w = [sem(f"weights_loaded{i}") for i in range(3)]
        s_sq = sem("row_norms_ready")
        s_eps = sem("eps_set")
        s_xn = sem("rows_normed")
        s_vz = sem("vector_zeroed")
        v_ch = sem("vector_chain")
        a_ch = sem("scalar_chain")
        s_mix = sem("chunks_mixed")
        s_act = sem("lora_inputs_ready")
        s_kk = sem("key_squares_ready")
        s_rk = sem("bonus_products_ready")
        s_cs = sem("decay_sums_ready")
        s_ep = sem("decay_factors_ready")
        s_up = sem("decay_factors_used")
        s_prep = sem("rwkv_operands_ready")
        s_bv = sem("bonus_applied")
        s_st = sem("state_ready")
        s_svd = sem("sample_vectors_out")
        s_svl = sem("sample_vectors_in")
        s_ss = sem("sample_states_done")
        s_ysl = sem("sample_outputs_in")
        s_yc = sem("y_centred")
        s_fin = sem("y_final")
        s_mout = sem("mem_rows_written")
        s_shout = sem("shift_rows_written")
        s_out = sem("outputs_written")
        s_wkvo = sem("prompt_states_written")
        s_sink = sem("sinks_loaded")
        s_sso = sem("sample_states_written")
        s_cache = sem("window_rows_loaded")
        s_newkv = sem("new_window_rows_written")
        s_xr = [sem(f"x_reloaded{t}") for t in range(5)]
        s_kvr = [sem(f"memory_cache_loaded{i}") for i in range(4)]
        s_late = sem("late_memory_values_loaded")
        s_max = sem("row_maxima_ready")
        s_exp = sem("exponentials_ready")
        s_prob = sem("probabilities_ready")
        s_sq2 = sem("row_norms2_ready")
        s_xn2 = sem("rows_normed2")
        s_rope = sem("keys_rotated")
        s_rw = sem("router_weights_loaded")
        s_hn = [sem(f"normed_rows_written{i}") for i in range(2)]
        s_mk = sem("choices_ready")
        s_exp1 = sem("router_exponents_ready")
        s_exp2 = sem("router_exponentials_done")
        s_init = sem("slot_table_cleared")
        s_sinit = sem("slot_table_written")
        s_slot = sem("slots_ready")
        s_scat = sem("slots_scattered")
        s_srow = sem("slot_rows_loaded")
        s_eid = sem("expert_ids_ready")
        s_idx = sem("row_indices_ready")
        s_wgu = [sem(f"gate_up_loaded{i}") for i in range(NB3)]
        s_wd = [sem(f"down_loaded{i}") for i in range(NB3)]
        s_gx = [sem(f"rows_gathered{i}") for i in range(NB3)]
        s_ys = [sem(f"rows_scattered{i}") for i in range(NB3)]
        s_idc = sem("pool_index_copied")
        s_pX = sem("rows_transposed")
        s_pG = sem("gate_up_products")
        s_pA = sem("activation_transposed")
        s_pY = sem("down_products")
        s_vx = sem("rows_in_sbuf")
        s_as = sem("silu_done")
        s_vm = sem("activation_done")
        s_aa = sem("activation_in_sbuf")
        s_vy = sem("left_half_out")
        s_ay = sem("right_half_out")
        s_yl = [sem(f"pair_rows_loaded{i}") for i in range(2)]
        s_comb = sem("experts_added")
        s_sq3 = sem("row_norms3_ready")
        s_res = sem("results_ready")
        s_kvw = sem("prompt_window_rows_written")
        outs = [0]

        def bank(key):
            return banks[place[key] % BANKS]

        def reuse(pe, key):
            n = place[key]
            if n >= BANKS:
                e, k = rank[plan[n - BANKS][0]]
                pe.wait_ge(evac[e], k)
            return bank(key)

        def filled(eng, key):
            eng.wait_ge(full, place[key] + 1)
            return bank(key)

        def done(eng, key):
            e, k = rank[key]
            eng.wait_ge(evac[e], k)

        PARC = {}
        r = 0
        for name, n in PAR_ROWS:
            PARC[name] = r
            r += n

        def pcol(name, c):
            return par[:, PARC[name] + c:PARC[name] + c + 1]

        block = ctx.enter_context(nc.Block())

        w_in = A["w_in"][0].rearrange("(p k) n -> p k n", k=KD)
        loads = []
        for i, grp in enumerate((3, 1, 0, 2, 4)):
            loads.append((("w_in", grp), i % 3, w_in[:, :, grp * 512:(grp + 1) * 512], KD))
        loads.append((("w_ck",), 2, A["w_ck"][0].rearrange("(p k) n -> p k n", k=KD), KD))
        loads.append((("w_cv",), 0, A["w_cv"][0].rearrange("(p k) n -> p k n", k=KD), KD))
        n_early = len(loads)
        w_o = A["w_out"][0].rearrange("(c p) n -> p c n", p=P)
        loads.append((("wo", 0), 0, w_o[:, 0:4, :], 4))
        loads.append((("wo", 1), 1, w_o[:, 4:8, :], 4))
        loads.append((("w_cq",), 1, A["w_cq"][0].rearrange("(p k) n -> p k n", k=KD), KD))
        loads.append((("w_co",), 0, A["w_co"][0].rearrange("(c p) n -> p c n", p=P), 4))
        slot_of, loaded_at, cnt = {}, {}, [0, 0, 0]
        for key, s, _, _ in loads:
            cnt[s] += 16
            slot_of[key], loaded_at[key] = s, cnt[s]

        def weights(key, k=KD):
            return ring[slot_of[key]].rearrange("p (k n) -> p k n", k=k)

        def weights_in(pe, key):
            pe.wait_ge(s_w[slot_of[key]], loaded_at[key])

        last_use = {("w_in", 3): ("proj", 15, 1), ("w_in", 1): ("proj", 7, 1), ("w_in", 0): ("proj", 3, 1),
                    ("w_in", 2): ("proj", 11, 1), ("w_in", 4): ("proj", 19, 1), ("w_ck",): ("mk", 1),
                    ("w_cv",): ("mv", 1), ("wo", 0): ("wo", 4, 1), ("wo", 1): ("wo", 4, 1), ("w_cq",): ("q", 3, 1)}

        @block.sync
        def _(sp):
            c = A["c_tables"]
            sp.dma_start(ident, c[:, 0:P]).then_inc(s_par, 16)
            r = 0
            for name, n in PAR_ROWS:
                src = A[name][0]
                if name == "r_k":
                    src = src.rearrange("h d -> (h d)")
                sp.dma_start(prow[r:r + n, :], src.rearrange("(r c) -> r c", c=P)).then_inc(s_par, 16)
                r += n
            sp.dma_start(srow[0:NS, :], A["state_rwkv_shift"][0]).then_inc(s_par, 16)
            for i, name in enumerate(("norm_mix", "norm_mem", "norm_cross", "norm_ffn")):
                sp.dma_start(gains[:, i, :], A[name][0].rearrange("(p k) -> p k", k=KD)).then_inc(s_par, 16)
            for t in range(TILES):
                sp.dma_start(x[:, t, :], A["x_prompt"][0, t * P:(t + 1) * P, :]).then_inc(s_x[t], 16)
            sp.dma_start(x[0:NS, 4, :], A["x_sample"][:, 0, :]).then_inc(s_x[4], 16)
            for i in range(3):
                key, s, src, k = loads[i]
                sp.dma_start(weights(key, k), src).then_inc(s_w[s], 16)
                if i == 0:
                    sp.dma_start(arena[:, P:at["gains"]], c[:, P:at["gains"]]).then_inc(s_const, 16)
                    sp.dma_start(memX, A["mem_prompt"][0].rearrange("(t p) n -> p t n", p=P)).then_inc(s_mem, 16)
                    sp.dma_start(lora[0:64, :], A["w_decay_up"][0]).then_inc(s_const, 16)
                    sp.dma_start(lora[64:128, :], A["w_a_up"][0]).then_inc(s_const, 16)
                    sp.dma_start(gup, A["w_g_up"][0]).then_inc(s_const, 16)
            row = A["attn_sink"]
            sp.dma_start(sinks[:, 0:H], bass.AP(row.tensor, row.offset, [[0, P], [1, H]])).then_inc(s_sink, 16)
            sp.dma_start(sinks[0:64, H:H + 1], bass.AP(row.tensor, row.offset, [[0, NS], [1, H], [1, 1]])) \
                .then_inc(s_sink, 16)
            for i in range(3, n_early):
                key, s, src, k = loads[i]
                prev = [l[0] for l in loads[:i] if l[1] == s][-1]
                sp.wait_ge(full, place[last_use[prev]] + 1)
                sp.dma_start(weights(key, k), src).then_inc(s_w[s], 16)
            done(sp, ("mk", 1))
            sp.dma_start(O["prompt_mem_k"][0, 0].rearrange("(t p) h d -> p t (h d)", p=P), mkS).then_inc(s_mout, 16)
            done(sp, ("mv", 1))
            sp.dma_start(O["prompt_mem_v"][0, 0].rearrange("(t p) h d -> p t (h d)", p=P), mv).then_inc(s_mout, 16)
            done(sp, ("shift_out", 3))
            sp.dma_start(O["prompt_shift"][0], shiftO[0:1, :]).then_inc(s_shout, 16)
            sp.dma_start(O["sample_shift"][0], shiftO[1:9, :]).then_inc(s_shout, 16)
            for kv in "kv":
                sp.dma_start(O[f"sample_swa_{kv}"][0, :, 0:P - 1], A[f"cache_swa_{kv}"][0, :, 1:P]) \
                    .then_inc(s_out, 16)
            sp.wait_ge(s_mout, 32)
            done(sp, ("mkT", 1))
            sp.dma_start(SS.rearrange("p i j -> p (i j)"),
                         A["state_rwkv_wkv"][0].rearrange("b h (u i) j -> (b h u) (i j)", u=2)).then_inc(s_svl, 16)
            done(sp, ("svec", 5))
            sp.dma_start(vec_d.rearrange("a b n -> b a n"), svt6).then_inc(s_svd, 16)
            sp.wait_ge(s_svd, 16)
            for a in range(5):
                src = vec_d[a].rearrange("b (h j) -> (b h) j", j=HD)
                src = bass.AP(src.tensor, src.offset, [[HD, NS * H], [0, 2], [1, HD]])
                sp.dma_start(sv[:, a, :], src).then_inc(s_svl, 16)
            sp.dma_start(svv, vec_d[5].rearrange("b (q i) -> (b q) i", i=32)).then_inc(s_svl, 16)
            sp.wait_ge(s_ss, 1)
            sp.dma_start(O["sample_wkv"][0].rearrange("b h (u i) j -> (b h u) (i j)", u=2),
                         SS.rearrange("p i j -> p (i j)")).then_inc(s_sso, 16)
            sp.wait_ge(s_ss, 2)
            sp.dma_start(ys_d.rearrange("b (q i) -> (b q) i", i=32), sy).then_inc(s_svd, 16)
            sp.wait_ge(s_svd, 32)
            sp.dma_start(svt6[:, 0, :], ys_d).then_inc(s_ysl, 16)
            sp.wait_ge(full, place[("WT", 3)] + 1)
            for t in range(TILES):
                sp.dma_start(x[:, t, :], A["x_prompt"][0, t * P:(t + 1) * P, :]).then_inc(s_xr[t], 16)
            sp.dma_start(x[0:NS, 4, :], A["x_sample"][:, 0, :]).then_inc(s_xr[4], 16)
            done(sp, ("wkvT",))
            for kv, dst in (("k", Kc), ("v", Vc)):
                sp.dma_start(dst[0:P - 1, :, :], A[f"cache_swa_{kv}"][0, :, 1:P].rearrange("b p h d -> p b (h d)")) \
                    .then_inc(s_cache, 16)
            sp.dma_start(O["prompt_wkv"][0, 0].rearrange("h i j -> i h j"),
                         wkvO.rearrange("i (h j) -> i h j", h=H)).then_inc(s_wkvo, 16)
            done(sp, ("ysT",))
            for i in range(n_early, n_early + 2):
                key, s, src, k = loads[i]
                if i == n_early + 1:
                    sp.wait_ge(s_wkvo, 16)
                sp.dma_start(weights(key, k), src).then_inc(s_w[s], 16)
            done(sp, ("kvout",))
            sp.dma_start(O["prompt_swa_k"][0, 0].rearrange("p h d -> p (h d)"), kvO[:, 0:P]).then_inc(s_kvw, 16)
            sp.dma_start(O["prompt_swa_v"][0, 0].rearrange("p h d -> p (h d)"), vtok[:, 3, :]).then_inc(s_kvw, 16)
            for i, kv in enumerate("kv"):
                sp.dma_start(O[f"sample_swa_{kv}"][0, :, P - 1].rearrange("b h d -> b (h d)"),
                             kvO[0:NS, (1 + i) * P:(2 + i) * P]).then_inc(s_newkv, 16)
            sp.wait_ge(s_newkv, 32)
            for kv, dst in (("k", Kc), ("v", Vc)):
                sp.dma_start(dst[P - 1:P, :, :],
                             O[f"sample_swa_{kv}"][0:1, :, P - 1].rearrange("a b h d -> a b (h d)")) \
                    .then_inc(s_cache, 16)
            def memory_load(kv, b, dst, signal):
                src = A[f"cache_mem_{kv}"][0, b]
                sp.dma_start(dst, src.rearrange("(a p) h d -> p a (h d)", p=P)).then_inc(signal, 16)

            sp.wait_ge(s_fin, 1)
            for b in range(4):
                memory_load("k", b, kv_ring[b], s_kvr[b])
            for i in range(n_early + 2, n_early + 4):
                key, s, src, k = loads[i]
                sp.wait_ge(full, place[("wo", 4, 1)] + 1)
                sp.dma_start(weights(key, k), src).then_inc(s_w[s], 16)
            sp.wait_ge(full, place[("q", 3, 1)] + 1)
            for b in range(4, NS):
                if b == 6:
                    for m in range(4, NS):
                        memory_load("v", m, late[m - 4], s_late)
                sp.wait_ge(full, place[("ckT", b - 4, 1)] + 1)
                memory_load("k", b, kv_ring[b % 4], s_kvr[b % 4])
            for b in range(4):
                sp.wait_ge(full, place[("ckT", b + 4, 1)] + 1)
                memory_load("v", b, kv_ring[b], s_kvr[b])
            sp.dma_start(wrG, A["w_group_router"][0].rearrange("(p k) n -> p k n", k=KD)).then_inc(s_rw, 16)
            sp.dma_start(wrE, A["w_expert_router"][0].rearrange("(p k) n -> p k n", k=KD)).then_inc(s_rw, 16)
            b1, b2, b3 = A["b_group_router"], A["b_expert_router"], A["norm_final"]
            sp.dma_start(rbias[:, 0:4], bass.AP(b1.tensor, b1.offset, [[0, P], [1, 4]])).then_inc(s_rw, 16)
            sp.dma_start(rbias[:, 4:36], bass.AP(b2.tensor, b2.offset, [[0, P], [1, NE]])).then_inc(s_rw, 16)
            sp.dma_start(gfin, bass.AP(b3.tensor, b3.offset, [[0, P], [1, D]])).then_inc(s_rw, 16)
            for t in range(T5):
                R = tile_rows(t)
                sp.wait_ge(s_xn2, 6 + t)
                sp.dma_start(hn_d[t * P:t * P + R, :], xn[t % 2][0:R, :]).then_inc(s_hn[t % 2], 16)
            sp.wait_ge(s_init, 1)
            sp.dma_start(slot_d.rearrange("(b p) a -> b (p a)", p=P), slot_rows[0:NBLK, :]).then_inc(s_sinit, 16)
            sp.wait_ge(s_scat, 16 * 2 * T5)
            sp.dma_start(slot_rows[0:NBLK, :], slot_d.rearrange("(b p) a -> b (p a)", p=P)).then_inc(s_srow, 16)
            wge = A["w_exp_gate"][0].rearrange("g e (p k) f -> (g e) p (k f)", k=KD)
            wue = A["w_exp_up"][0].rearrange("g e (p k) f -> (g e) p (k f)", k=KD)
            wde = A["w_exp_down"][0].rearrange("g e f d -> (g e) f d")
            def load_expert(i, b):
                e = sp.value_load(eidI[0:1, bass.ds(b, 1)], min_val=0, max_val=NE - 1)
                sp.dma_start(we[i][:, 0, :], wge[bass.ds(e, 1)].rearrange("a p n -> (a p) n")).then_inc(s_wgu[i], 16)
                sp.dma_start(we[i][:, 1, :], wue[bass.ds(e, 1)].rearrange("a p n -> (a p) n")).then_inc(s_wgu[i], 16)
                sp.dma_start(we[i][:, 2, :], wde[bass.ds(e, 1)].rearrange("a p n -> (a p) n")).then_inc(s_wd[i], 16)

            sp.wait_ge(full, place[("wc", 4, 1)] + 1)
            sp.wait_ge(s_eid, 1)
            for i in range(NB3):
                load_expert(i, i)
            with sp.Fori(1, NBLK // NB3) as it:
                for i in range(NB3):
                    sp.wait_ge(s_pY, it * NB3 + (i + 1 - NB3))
                    sp.wait_ge(s_eid, 1)
                    load_expert(i, it * NB3 + i)
            for i in range(NB3):
                sp.wait_ge(s_ys[i], 16 * (NBLK // NB3))
            sp.wait_ge(s_pY, NBLK)
            prow_d = pair_d.rearrange("(t j) d -> t j d", j=2)
            for t in range(T5):
                R = tile_rows(t)
                if t >= 2:
                    sp.wait_ge(s_comb, t - 1)
                sp.dma_start(ydt[t % 2][0:R, :, :], prow_d[t * P:t * P + R]).then_inc(s_yl[t % 2], 16)
            for t in range(T5):
                R = tile_rows(t)
                sp.wait_ge(s_res, t + 1)
                dst = O["y_prompt"][0, t * P:(t + 1) * P, :] if t < TILES else O["y_sample"][:, 0, :]
                sp.dma_start(dst, x[0:R, t, :]).then_inc(s_out, 16)
            sp.wait_ge(s_out, 16 * (2 + T5))

        @block.gpsimd
        def _(pool):
            pool.wait_ge(s_sinit, 16)
            pool.wait_ge(s_slot, 1)
            pool.wait_ge(s_const, 64)
            for t in range(T5):
                for j in range(2):
                    pool.indirect_dma_start(slot_d, bass.IndirectOffsetOnAxis(slI[j][:, t:t + 1].bitcast(U32), 0),
                                            pair_no[:, t, j:j + 1], None, bounds_check=NBLK * P - 1,
                                            oob_is_err=False).then_inc(s_scat, 16)
            pool.wait_ge(s_idx, 1)
            for i in range(2):
                pool.wait_ge(s_hn[i], 16 * (3 - i))

            def wait(sem, value):
                pool.wait_ge(sem, value)
                pool.wait_ge(s_idx, 1)

            def index_in(value):
                pool.wait_ge(s_idc, value)
                pool.tensor_tensor(scrap[:, 0:1], scrap[:, 1:2], scrap[:, 1:2], ALU.add)

            pool.memset(scrap, 0.0)

            def gather(i, b):
                pool.tensor_copy(idg[i], tokI[:, bass.ds(b, 1)]).then_inc(s_idc, 1)

            def scatter_index(i, b):
                pool.tensor_copy(ids[i], pidI[:, bass.ds(b, 1)]).then_inc(s_idc, 1)

            def start_gather(i):
                pool.indirect_dma_start(xg[i], None, hn_d, bass.IndirectOffsetOnAxis(idg[i].bitcast(U32), 0),
                                        bounds_check=NT - 1, oob_is_err=False).then_inc(s_gx[i], 16)

            def start_scatter(i):
                pool.indirect_dma_start(pair_d, bass.IndirectOffsetOnAxis(ids[i].bitcast(U32), 0), yb[i], None,
                                        bounds_check=PAIRS_E - 1, oob_is_err=False).then_inc(s_ys[i], 16)

            for i in range(NB3):
                gather(i, i)
                pool.wait_ge(s_idc, i + 1)
                start_gather(i)
            with pool.Fori(1, NBLK // NB3) as it:
                for i in range(NB3):
                    wait(s_pX, it * NB3 + (i - 2))
                    wait(s_gx[i], it * 16)
                    gather(i, it * NB3 + i)
                    index_in(it * (2 * NB3) + (2 * i + 1 - NB3))
                    start_gather(i)
                    wait(s_vy, it * NB3 + (i - 2))
                    wait(s_ay, it * NB3 + (i - 2))
                    scatter_index(i, it * NB3 + (i - NB3))
                    index_in(it * (2 * NB3) + (2 * i + 2 - NB3))
                    start_scatter(i)
            last = NBLK // NB3 - 1
            for i in range(NB3):
                pool.wait_ge(s_vy, NB3 * last + i + 1)
                pool.wait_ge(s_ay, NB3 * last + i + 1)
                pool.wait_ge(s_ys[i], 16 * last)
                scatter_index(i, NB3 * last + i)
                pool.wait_ge(s_idc, 2 * NB3 * last + NB3 + i + 1)
                start_scatter(i)

        @block.tensor
        def _(pe):
            last = [None]

            def mm(out, lhsT, rhs, start=True, stop=True):
                last[0] = pe.matmul(out, lhsT, rhs, start=start, stop=stop, skip_group_check=True)

            def tr(out, in_):
                n = in_.shape[0]
                last[0] = pe.transpose(out, in_, ident[0:n, 0:n])

            def close():
                last[0].then_inc(full, 1)

            pe.wait_ge(s_par, 16 * 14)
            o = reuse(pe, ("par",))
            tr(o[:, 0:42], prow[0:42, :])
            close()
            o = reuse(pe, ("shift_in",))
            for j in range(RW):
                tr(o[:, NS * j:NS * j + NS], srow[0:NS, j * P:(j + 1) * P])
            close()
            for t in range(TILES + 1):
                R = tile_rows(t)
                pe.wait_ge(s_xn, t + 1)
                for i in range(2):
                    o = reuse(pe, ("xT", t, i))
                    xk = x[0:R, t, :].rearrange("p (q k) -> p k q", k=KD)
                    for k in range(4):
                        tr(o[:, k * P:k * P + R], xk[:, 4 * i + k, :])
                    close()

            def project(j):
                grp = j // 4
                key = ("w_in", grp)
                weights_in(pe, key)
                w = weights(key)
                for s in range(2):
                    o = reuse(pe, ("proj", j, s))
                    for k in range(KD):
                        mm(o[:, 0:HALF], w[:, k, (j % 4) * P:(j % 4 + 1) * P], hA[:, k, s * HALF:(s + 1) * HALF],
                           k == 0, k == KD - 1)
                    close()

            done(pe, ("xT", 4, 1))
            for j in (12, 13, 14, 15):
                project(j)
            for t in range(2):
                pe.wait_ge(s_xn, 6 + t)
                for i in range(2):
                    o = reuse(pe, ("mT", t, i))
                    xk = memX[:, t, :].rearrange("p (q k) -> p k q", k=KD)
                    for k in range(4):
                        tr(o[:, k * P:(k + 1) * P], xk[:, 4 * i + k, :])
                    close()
            for j in (4, 5, 6, 7, 0, 1, 2, 3, 8, 9, 10, 11, 16, 17, 18, 19):
                project(j)
            pe.wait_ge(s_const, 64)
            pe.wait_ge(s_act, 1)
            for key, b in (("lora_w", 0), ("lora_a", 64)):
                for c in range(4):
                    for s in range(2):
                        o = reuse(pe, (key, c, s))
                        mm(o[:, 0:HALF], lora[b:b + 64, c * P:(c + 1) * P],
                           PR[b:b + 64, 12, 1 + s * HALF:1 + (s + 1) * HALF])
                        close()
            for key, wk in (("mk", ("w_ck",)), ("mv", ("w_cv",))):
                weights_in(pe, wk)
                for t in range(2):
                    o = reuse(pe, (key, t))
                    for k in range(KD):
                        mm(o[:, :], memT[:, k, t * P:(t + 1) * P], weights(wk)[:, k, :], k == 0, k == KD - 1)
                    close()
            for t in range(2):
                done(pe, ("mk", t))
                o = reuse(pe, ("mkT", t))
                for h in range(XH):
                    tr(o[:, h * P:(h + 1) * P], mkS[:, t, h * P:(h + 1) * P])
                close()
            pe.wait_ge(s_mix, 14)
            for i in range(4):
                o = reuse(pe, ("shift_out", i))
                for j in range(4 * i, min(4 * i + 4, RW)):
                    tr(o[0:9, (j % 4) * P:(j % 4 + 1) * P], saved[:, j, :])
                close()
            for t in range(TILES):
                o = reuse(pe, ("tokV", t))
                for c in range(4):
                    tr(o[:, c * P:(c + 1) * P], PR[:, 8 + c, 1 + t * P:1 + (t + 1) * P])
                close()
            for c in range(4):
                pe.wait_ge(s_kk, c + 1)
                for s in range(2):
                    o = reuse(pe, ("norm_k", c, s))
                    mm(o[:, 0:HALF], bones, tmp[0][:, s * HALF:(s + 1) * HALF])
                    close()
                pe.wait_ge(s_rk, c + 1)
                for s in range(2):
                    o = reuse(pe, ("bonus", c, s))
                    mm(o[:, 0:HALF], bones, tmp[1][:, s * HALF:(s + 1) * HALF])
                    close()
            pe.wait_ge(s_prep, 4)
            for i in range(6):
                o = reuse(pe, ("svec", i))
                for c in range(4):
                    src = (B0[:, c, SEQ:NT], B1[:, c, SEQ:NT], PR[:, 4 + c, 1 + SEQ:1 + NT], wS[:, c, :],
                           PR[:, c, 1 + SEQ:1 + NT], PR[:, 8 + c, 1 + SEQ:1 + NT])[i]
                    tr(o[0:NS, c * P:(c + 1) * P], src)
                close()
            for t in range(TILES):
                lo, hi = t * P, (t + 1) * P
                for i, src in enumerate((B0, B1, PR[:, 4:8, :])):
                    o = reuse(pe, ("tok", t, i))
                    off = 1 if i == 2 else 0
                    for c in range(4):
                        tr(o[:, c * P:(c + 1) * P], src[:, c, off + lo:off + hi])
                    close()
                for h in range(H):
                    c, b = h // 2, 64 * (h % 2)
                    o = reuse(pe, ("AB", t, h))
                    for i, src in enumerate((Bt, Kt)):
                        mm(o[:, i * 256:i * 256 + P], src[b:b + 64, c, lo:hi], B0[b:b + 64, c, lo:hi])
                        mm(o[:, i * 256 + P:i * 256 + 256], src[b:b + 64, c, lo:hi], PR[b:b + 64, c, 1 + lo:1 + hi])
                    close()
                for q in range(2):
                    o = reuse(pe, ("N0", t, q))
                    for h in range(4 * q, 4 * q + 4):
                        done(pe, ("AB", t, h))
                        tr(o[:, (h % 4) * P:(h % 4 + 1) * P], AB[:, h, 0, :])
                    close()

                def M(h, k):
                    return AB[:, h, 0, :] if k == 0 else Mi[k % 2][:, h, :]

                for k in range(6):
                    for q in range(2):
                        hs = range(4 * q, 4 * q + 4)
                        if k == 0:
                            done(pe, ("N0", t, q))
                        else:
                            done(pe, ("NN", t, q, k - 1))
                            if k < 5:
                                done(pe, ("MM", t, q, k - 1))
                            if k == 1:
                                pe.wait_ge(s_st, 2 * t + q + 1)
                            else:
                                done(pe, ("XM", t, q, k - 1))
                            o = reuse(pe, ("XM", t, q, k))
                            for h in hs:
                                mm(o[:, (h % 4) * P:(h % 4 + 1) * P], Ni[k % 2][:, h, :], Xi[:, h, :])
                            close()
                        if k < 4:
                            o = reuse(pe, ("MM", t, q, k))
                            for h in hs:
                                mm(o[:, (h % 4) * P:(h % 4 + 1) * P], Ni[k % 2][:, h, :], M(h, k))
                            close()
                        if k < 5:
                            o = reuse(pe, ("NN", t, q, k))
                            for h in hs:
                                mm(o[:, (h % 4) * P:(h % 4 + 1) * P], M(h, k), Ni[k % 2][:, h, :])
                            close()
                o = reuse(pe, ("akv", t))
                done(pe, ("tokV", t))
                for h in range(H):
                    mm(o[:, h * HD:(h + 1) * HD], AB[:, h, 2, :], tokV[:, t, h * HD:(h + 1) * HD])
                close()
                done(pe, ("akv", t))
                done(pe, ("XM", t, 1, 5))
                o = reuse(pe, ("G", t))
                for h in range(H):
                    mm(o[:, h * HD:(h + 1) * HD], Xi[:, h, :], akv[:, h * HD:(h + 1) * HD])
                close()
                o = reuse(pe, ("WT", t))
                done(pe, ("tok", t, 0))
                for h in range(H):
                    c, b = h // 2, 64 * (h % 2)
                    mm(o[b:b + 64, c * P:(c + 1) * P], tokX[:, 0, h * HD:(h + 1) * HD], Xi[:, h, :])
                close()
                done(pe, ("WT", t))
                done(pe, ("tok", t, 2))
                for u in range(2):
                    tk = 64 * u
                    n = 2 * t + u
                    if n == 0:
                        pe.wait_ge(s_vz, 1)
                    elif u == 0:
                        done(pe, ("S", t - 1, 1))
                    else:
                        done(pe, ("S", t, 0))
                    for e in range(2):
                        o = reuse(pe, ("U", t, u, e))
                        b = 64 * e
                        for c in range(4):
                            mm(o[tk:tk + 64, c * HD:(c + 1) * HD], WT[b:b + 64, c, tk:tk + 64],
                               ST[b:b + 64, n, c, :])
                        close()
                    done(pe, ("U", t, u, 1))
                    o = reuse(pe, ("S", t, u))
                    for h in range(H):
                        c, b = h // 2, 64 * (h % 2)
                        hc = slice(h * HD, (h + 1) * HD)
                        mm(o[b:b + 64, c * HD:(c + 1) * HD], tokX[tk:tk + 64, 2, hc], tokV[tk:tk + 64, t, hc],
                           True, False)
                        mm(o[b:b + 64, c * HD:(c + 1) * HD], tokX[tk:tk + 64, 1, hc], Ut[tk:tk + 64, hc], False, True)
                    close()
                o = reuse(pe, ("Y", t))
                for h in range(H):
                    c, b = h // 2, 64 * (h % 2)
                    hc = slice(h * HD, (h + 1) * HD)
                    yo = o[b:b + 64, c * P:(c + 1) * P]
                    mm(yo, tokV[:, t, hc], AB[:, h, 3, :], c == 0, False)
                    mm(yo, Ut[:, hc], AB[:, h, 1, :], False, False)
                    for u in range(2):
                        mm(o[b:b + 64, c * P + 64 * u:c * P + 64 * u + 64], ST[b:b + 64, 2 * t + u, c, :],
                           PR[b:b + 64, c, 1 + lo + 64 * u:1 + lo + 64 * u + 64], False, True)
                close()
            o = reuse(pe, ("wkvT",))
            done(pe, ("S", 3, 1))
            for c in range(4):
                tr(o[0:64, c * P:(c + 1) * P], ST[:, 8, c, :])
            close()
            pe.wait_ge(s_ysl, 16)
            o = reuse(pe, ("ysT",))
            for c in range(4):
                tr(o[:, c * NS:(c + 1) * NS], svt6[:, 0, c * P:(c + 1) * P])
            close()
            done(pe, ("ysT",))
            done(pe, ("Y", 3))
            for c in range(4):
                for s in range(2):
                    o = reuse(pe, ("mean", c, s))
                    mm(o[:, 0:HALF], bones, yT[:, c, s * HALF:(s + 1) * HALF])
                    close()
            for c in range(4):
                pe.wait_ge(s_yc, c + 1)
                for s in range(2):
                    o = reuse(pe, ("var", c, s))
                    mm(o[:, 0:HALF], bones, B0[:, c, s * HALF:(s + 1) * HALF])
                    close()
            for c in range(4):
                for s in range(2):
                    o = reuse(pe, ("gate", c, s))
                    mm(o[:, 0:HALF], gup[:, c * P:(c + 1) * P], PR[:, 13, 1 + s * HALF:1 + (s + 1) * HALF])
                    close()
            for s in range(2):
                cols = slice(s * HALF, (s + 1) * HALF)
                for i in range(2):
                    o = reuse(pe, ("rka", i, s))
                    mm(o[:, 0:HALF], sel[:, 1 + i, :], SQ[:, 4, cols])
                    close()
                    o = reuse(pe, ("rkb", i, s))
                    mm(o[:, 0:HALF], sel[:, 3 + i, :], SQ[:, 4, cols])
                    close()
                for c in range(4):
                    o = reuse(pe, ("rq", c, s))
                    mm(o[:, 0:HALF], sel[:, 0, :], SQ[:, c, cols])
                    close()
            o = reuse(pe, ("vtok",))
            for t in range(TILES):
                tr(o[:, t * P:(t + 1) * P], SQ[:, 5, t * P:(t + 1) * P])
            close()
            pe.wait_ge(s_rope, 1)
            o = reuse(pe, ("kvout",))
            for i in range(2):
                tr(o[:, i * HD:(i + 1) * HD], RK[i][0:HD, 3 * P:4 * P])
                tr(o[0:NS, P + i * HD:P + (i + 1) * HD], RK[i][0:HD, SEQ:NT])
            tr(o[0:NS, 2 * P:3 * P], SQ[:, 5, SEQ:NT])
            close()
            done(pe, ("vtok",))

            def window_scores(t):
                k0 = max(t - 1, 0) * P
                W = (t + 1) * P - k0
                for e in range(2):
                    b = 64 * e
                    for i in range(2):
                        o = reuse(pe, ("s", t, e, i))
                        for n in range(2):
                            mm(o[:, n * W:(n + 1) * W], SQ[b:b + 64, 2 * i + n, t * P:(t + 1) * P],
                               RK[i][b:b + 64, k0:k0 + W])
                        close()

            window_scores(0)
            for t in range(TILES):
                if t < TILES - 1:
                    window_scores(t + 1)
                pe.wait_ge(s_prob, t + 1)
                na = 1 if t == 0 else 2
                sm = Sm[t % 2].rearrange("p (h s) -> p h s", h=H)
                for i in range(4):
                    o = reuse(pe, ("pT", t, i))
                    for n in range(2):
                        for a in range(na):
                            tr(o[:, (2 * n + a) * P:(2 * n + a + 1) * P], sm[:, 2 * i + n, a * P:(a + 1) * P])
                    close()
                done(pe, ("pT", t, 3))
                o = reuse(pe, ("o", t))
                for h in range(H):
                    c, b, g = h // 2, 64 * (h % 2), h // 4
                    for a in range(na):
                        mm(o[b:b + 64, c * P:(c + 1) * P], vtok[:, t + 1 - na + a, g * HD:(g + 1) * HD],
                           PTa[:, h, a, :], a == 0, a == na - 1)
                close()
            pe.wait_ge(s_cache, 64)
            for e in range(2):
                o = reuse(pe, ("qd", e))
                mm(o[:, 0:32].rearrange("p (c b) -> p c b", c=4), sel[:, 1 + e, :], SQ[:, 0:4, SEQ:NT])
                close()
            for i in range(2):
                o = reuse(pe, ("kT", i))
                for m in range(4):
                    tr(o[:, m * P:(m + 1) * P], Kc[:, 4 * i + m, :])
                close()
            done(pe, ("kT", 1))
            done(pe, ("qd", 1))
            for g in range(2):
                o = reuse(pe, ("ss", g))
                for b in range(NS):
                    mm(o[:, 4 * b:4 * b + 4], kTs[64 * g:64 * g + 64, b, :],
                       QD[64 * g:64 * g + 64, b, 2 * g:2 * g + 2, :].rearrange("p c e -> p (c e)"))
                close()
            done(pe, ("ss", 1))
            o = reuse(pe, ("ssT",))
            tr(o[0:64, 0:P], sT)
            close()
            pe.wait_ge(s_prob, 5)
            o = reuse(pe, ("spT",))
            tr(o[:, 0:64], Sm[0][0:64, 0:P])
            close()
            done(pe, ("spT",))
            o = reuse(pe, ("so",))
            for e in range(2):
                for b in range(NS):
                    for g in range(2):
                        mm(o[64 * e:64 * e + 64, 0:32].rearrange("p (c b) -> p c b", c=4)[:, 2 * g:2 * g + 2, b],
                           Vc[:, b, g * HD:(g + 1) * HD],
                           pTs.rearrange("p (b g n e) -> p b g n e", b=NS, g=2, n=2)[:, b, g, :, e])
                close() if e else None
            done(pe, ("so",))
            pe.wait_ge(s_fin, 1)
            for i in range(2):
                weights_in(pe, ("wo", i))
            for t in range(TILES + 1):
                R = tile_rows(t)
                for n in range(2):
                    o = reuse(pe, ("wo", t, n))
                    for c in range(8):
                        mm(o[0:R, :], yT[:, c, t * P:t * P + R],
                           weights(("wo", c // 4), 4)[:, c % 4, n * 512:(n + 1) * 512], c == 0, c == 7)
                    close()

            def transpose_rows(key, first):
                for t in range(TILES + 1):
                    R = tile_rows(t)
                    pe.wait_ge(s_xn2, first + t + 1)
                    for i in range(2):
                        o = reuse(pe, (key, t, i))
                        xk = xn[t % 2][0:R, :].rearrange("p (q k) -> p k q", k=KD)
                        for k in range(4):
                            tr(o[:, k * P:k * P + R], xk[:, 4 * i + k, :])
                        close()

            transpose_rows("xT2", 0)
            weights_in(pe, ("w_cq",))
            done(pe, ("xT2", 4, 1))
            for h in range(XH):
                for s in range(2):
                    o = reuse(pe, ("q", h, s))
                    for k in range(KD):
                        mm(o[:, 0:HALF], weights(("w_cq",))[:, k, h * P:(h + 1) * P],
                           hA[:, k, s * HALF:(s + 1) * HALF], k == 0, k == KD - 1)
                    close()
            done(pe, ("q", 3, 1))

            def prompt_scores(t):
                for i in range(2):
                    o = reuse(pe, ("xs", t, i))
                    for n in range(2):
                        mm(o[:, n * MT:(n + 1) * MT], qT[:, 2 * i + n, t * P:(t + 1) * P], mkT[:, 2 * i + n, :])
                    close()

            def prompt_values(t):
                pe.wait_ge(s_prob, 6 + t)
                sm = Sm[(5 + t) % 2][:, 0:1024].rearrange("p (h s) -> p h s", h=XH)
                for i in range(2):
                    o = reuse(pe, ("xpT", t, i))
                    for n in range(2):
                        for a in range(2):
                            tr(o[:, (2 * n + a) * P:(2 * n + a + 1) * P], sm[:, 2 * i + n, a * P:(a + 1) * P])
                    close()
                done(pe, ("xpT", t, 1))
                o = reuse(pe, ("xo", t))
                for h in range(XH):
                    for a in range(2):
                        mm(o[:, h * P:(h + 1) * P], mv[:, a, h * P:(h + 1) * P], PTc[:, h, a, :], a == 0, a == 1)
                close()

            def keys_T(b):
                pe.wait_ge(s_kvr[b % 4], 16 * (b // 4 + 1))
                for st in range(2):
                    o = reuse(pe, ("ckT", b, st))
                    for h in range(XH):
                        tr(o[:, h * P:(h + 1) * P], kv_ring[b % 4][:, st, h * P:(h + 1) * P])
                    close()

            def sample_scores(b):
                done(pe, ("ckT", b, 1))
                o = reuse(pe, ("cs", b))
                for st in range(2):
                    for h in range(XH):
                        mm(o[:, 4 * st + h:4 * st + h + 1], KT[b % 2][:, h, st, :], qT[:, h, SEQ + b:SEQ + b + 1])
                close()

            for what, n in CROSS_ORDER:
                {"xs": prompt_scores, "xp": prompt_values, "ckT": keys_T, "cs": sample_scores}[what](n)
            done(pe, ("cs", 7))
            o = reuse(pe, ("csT",))
            for st in range(2):
                tr(o[0:32, st * P:(st + 1) * P], csS[:, st, :])
            close()
            pe.wait_ge(s_prob, 10)
            o = reuse(pe, ("cpT",))
            for st in range(2):
                tr(o[:, st * 32:(st + 1) * 32], Sm[1][0:32, st * P:(st + 1) * P])
            close()
            done(pe, ("cpT",))
            o = reuse(pe, ("co",))
            for b in range(NS):
                if b < 4:
                    pe.wait_ge(s_kvr[b], 48)
                elif b == 4:
                    pe.wait_ge(s_late, 64)
                for h in range(XH):
                    for st in range(2):
                        mm(o[:, 4 * b + h:4 * b + h + 1], values_of(b)[:, st, h * P:(h + 1) * P],
                           cpS[:, st, 4 * b + h:4 * b + h + 1], st == 0, st == 1)
            close()
            done(pe, ("co",))
            done(pe, ("xo", 3))
            weights_in(pe, ("w_co",))
            for t in range(TILES + 1):
                R = tile_rows(t)
                for n in range(2):
                    o = reuse(pe, ("wc", t, n))
                    for h in range(XH):
                        mm(o[0:R, :], yT[:, h, t * P:t * P + R], weights(("w_co",), 4)[:, h, n * 512:(n + 1) * 512],
                           h == 0, h == XH - 1)
                    close()
            transpose_rows("xT3", 5)
            done(pe, ("xT3", 4, 1))
            pe.wait_ge(s_rw, 16 * 5)
            for t in range(T5):
                R = tile_rows(t)
                o = reuse(pe, ("route", t))
                for w, lo, n in ((wrG, 0, 4), (wrE, 4, NE)):
                    for k in range(KD):
                        mm(o[0:R, lo:lo + n], hA[:, k, t * P:t * P + R], w[:, k, :], k == 0, k == KD - 1)
                close()
            pe.wait_ge(s_mk, 1)
            o = reuse(pe, ("ranks",))
            for t in range(T5 + 1):
                lhs = [(onesm, u) for u in range(min(t, T5))] + ([(tri, t)] if t < T5 else [])
                for n, (m, u) in enumerate(lhs):
                    mm(o[:, t * NE:(t + 1) * NE], m, Mk[:, u, :], n == 0, n == len(lhs) - 1)
            close()
            pe.wait_ge(s_srow, 16)
            o = reuse(pe, ("slots",))
            tr(o[:, 0:NBLK], slot_rows[0:NBLK, :])
            close()
            done(pe, ("slots",))
            bX = [banks[0], banks[1]]
            bG, bA = banks[2], banks[3]
            bY = [banks[4], banks[5]]

            def rows_T(i, b, r):
                pe.wait_ge(s_gx[i], r * 16 + 16)
                if b is not None:
                    pe.wait_ge(s_vx, b)
                xk = xg[i].rearrange("p (q k) -> p k q", k=KD)
                for k in range(KD):
                    ins = pe.transpose(bX[k // 4][:, (k % 4) * P:(k % 4 + 1) * P], xk[:, k, :], ident)
                ins.then_inc(s_pX, 1)

            def gate_up(i, b, r):
                pe.wait_ge(s_wgu[i], r * 32 + 32)
                pe.wait_ge(s_vx, b + 1)
                for k in range(KD):
                    ins = pe.matmul(bG[:, 0:2 * FH].rearrange("p (a f) -> p a f", a=2), xTe[:, k, :],
                                    we[i][:, 0:2, k * FH:(k + 1) * FH], start=k == 0, stop=k == KD - 1)
                ins.then_inc(s_pG, 1)

            def act_T(b):
                pe.wait_ge(s_vm, b + 1)
                pe.transpose(bA[:, 0:P], act_e, ident).then_inc(s_pA, 1)

            def down(i, b, r, first=False):
                pe.wait_ge(s_aa, b + 1)
                pe.wait_ge(s_wd[i], r * 16 + 16)
                if not first:
                    pe.wait_ge(s_vy, b)
                    pe.wait_ge(s_ay, b)
                for n in range(2):
                    ins = pe.matmul(bY[n][:, :], actT, we[i][:, 2, n * 512:(n + 1) * 512], start=True, stop=True)
                ins.then_inc(s_pY, 1)

            rows_T(0, None, 0)
            gate_up(0, 0, 0)
            rounds = NBLK // NB3

            def pe_round(it, first, final):
                for i in range(NB3):
                    b = it * NB3 + i
                    nxt = not (final and i == NB3 - 1)
                    if nxt:
                        rows_T((i + 1) % NB3, b + 1, it if i < NB3 - 1 else it + 1)
                    act_T(b)
                    if nxt:
                        gate_up((i + 1) % NB3, b + 1, it if i < NB3 - 1 else it + 1)
                    down(i, b, it, first and i == 0)

            pe_round(0, True, False)
            with pe.Fori(1, rounds - 1) as it:
                pe_round(it, False, False)
            pe_round(rounds - 1, False, True)

        @block.scalar
        def _(act):
            chain = [0]

            def link(ins):
                chain[0] += 1
                ins.then_inc(a_ch, 1)
                act.wait_ge(a_ch, chain[0])

            act.wait_ge(s_eps, 1)
            for t in range(TILES + 1):
                R = tile_rows(t)
                act.wait_ge(s_x[t], 16)
                ms = small[0:R, t:t + 1]
                link(act.activation(junk[0:R, :], x[0:R, t, :], ACT.Square, accum_out=ms))
                act.activation(ms, ms, ACT.Sqrt, scale=1.0 / D, bias=small[0:R, 41:42]).then_inc(s_sq, 1)
            act.wait_ge(s_mem, 16)
            for t in range(2):
                ms = small[:, 5 + t:6 + t]
                link(act.activation(junk, memX[:, t, :], ACT.Square, accum_out=ms))
                act.activation(ms, ms, ACT.Sqrt, scale=1.0 / D, bias=small[:, 41:42]).then_inc(s_sq, 1)
            for n, j in enumerate((12, 13, 14, 15, 4, 5, 6, 7, 0, 1, 2, 3, 8, 9, 10, 11, 16, 17, 18, 19)):
                for s in range(2):
                    o = filled(act, ("proj", j, s))
                    dst = PR[:, j, 1 + s * HALF:1 + (s + 1) * HALF] if j < RW else \
                        SQ[:, j - RW, s * HALF:(s + 1) * HALF]
                    act.copy(dst, o[:, 0:HALF]).then_inc(evac["a"], 1)
                if n == 7:
                    act.wait_ge(s_mix, 2)
                    link(act.activation(PR[0:64, 12, 1:1 + NT], PR[0:64, 12, 1:1 + NT], ACT.Tanh))
                    act.activation(PR[:, 13, 1:1 + NT], PR[:, 13, 1:1 + NT], ACT.Sigmoid).then_inc(s_act, 1)
            for key, dst, bias in (("lora_w", sg, "w_decay0"), ("lora_a", aa, "a0")):
                for c in range(4):
                    for s in range(2):
                        o = filled(act, (key, c, s))
                        act.activation(dst[:, c, s * HALF:(s + 1) * HALF], o[:, 0:HALF], ACT.Sigmoid,
                                       bias=pcol(bias, c)).then_inc(evac["a"], 1)
            for t in range(2):
                o = filled(act, ("mk", t))
                act.copy(mkS[:, t, :], o[:, :]).then_inc(evac["a"], 1)
            for t in range(2):
                o = filled(act, ("mv", t))
                act.copy(mv[:, t, :], o[:, :]).then_inc(evac["a"], 1)
            for t in range(2):
                o = filled(act, ("mkT", t))
                act.copy(mkT[:, :, t * P:(t + 1) * P], 
                         o[:, :].rearrange("p (h s) -> p h s", h=XH)).then_inc(evac["a"], 1)
            for i in range(4):
                o = filled(act, ("shift_out", i))
                n = min(4, RW - 4 * i) * P
                act.copy(shiftO[:, i * 512:i * 512 + n], o[0:9, 0:n]).then_inc(evac["a"], 1)
            act.wait_ge(s_shout, 32)
            for t in range(TILES):
                o = filled(act, ("tokV", t))
                act.copy(tokV[:, t, :], o[:, :]).then_inc(evac["a"], 1)
            for c in range(4):
                for s in range(2):
                    o = filled(act, ("norm_k", c, s))
                    if s == 0 and c > 0:
                        act.wait_ge(s_prep, c)
                    act.activation(tmp[2][:, s * HALF:(s + 1) * HALF], o[:, 0:HALF], ACT.Sqrt).then_inc(evac["a"], 1)
                act.wait_ge(s_cs, 3 * c + 1)
                link(act.activation(wS[:, c, :], sg[:, c, SEQ:NT], ACT.Exp, scale=-KAPPA))
                act.activation(tmp[1][:, 0:SEQ], tmp[0][:, 0:SEQ], ACT.Exp, scale=-KAPPA).then_inc(s_ep, 1)
                act.activation(tmp[2][:, 0:SEQ], tmp[0][:, 0:SEQ], ACT.Exp, scale=KAPPA).then_inc(s_ep, 1)
                act.wait_ge(s_cs, 3 * c + 2)
                act.activation(tmp[3][:, 0:SEQ], tmp[3][:, 0:SEQ], ACT.Exp, scale=-KAPPA).then_inc(s_ep, 1)
                act.wait_ge(s_cs, 3 * c + 3)
                act.activation(tmp[1][:, 0:SEQ], tmp[1][:, 0:SEQ], ACT.Exp, scale=-KAPPA).then_inc(s_ep, 1)
            for i in range(6):
                o = filled(act, ("svec", i))
                act.copy(svt6[:, i, :], o[0:NS, :]).then_inc(evac["a"], 1)
            for t in range(TILES):
                for i in range(3):
                    o = filled(act, ("tok", t, i))
                    act.copy(tokX[:, i, :], o[:, :]).then_inc(evac["a"], 1)
                for q in range(2):
                    o = filled(act, ("N0", t, q))
                    act.copy(Ni[0][:, 4 * q:4 * q + 4, :], o[:, :].rearrange("p (h t) -> p h t", h=4)) \
                        .then_inc(evac["a"], 1)
                for k in range(6):
                    for q in range(2):
                        for key, dst in (("MM", Mi), ("NN", Ni)):
                            if (key, t, q, k) in rank and rank[(key, t, q, k)][0] == "a":
                                o = filled(act, (key, t, q, k))
                                act.copy(dst[(k + 1) % 2][:, 4 * q:4 * q + 4, :],
                                         o[:, :].rearrange("p (h t) -> p h t", h=4)).then_inc(evac["a"], 1)
                o = filled(act, ("WT", t))
                act.copy(WT, o[:, :].rearrange("p (c t) -> p c t", c=4)).then_inc(evac["a"], 1)
                o = filled(act, ("Y", t))
                if t == 0:
                    act.wait_ge(s_bv, 4)
                act.copy(yT[:, 0:4, t * P:(t + 1) * P], o[:, :].rearrange("p (c t) -> p c t", c=4)) \
                    .then_inc(evac["a"], 1)
            o = filled(act, ("wkvT",))
            act.copy(wkvO, o[0:64, :]).then_inc(evac["a"], 1)
            for c in range(4):
                for s in range(2):
                    o = filled(act, ("var", c, s))
                    act.activation(B1[:, c, s * HALF:(s + 1) * HALF], o[:, 0:HALF], ACT.Sqrt, scale=1.0 / HD,
                                   bias=small[:, 40:41]).then_inc(evac["a"], 1)
            o = filled(act, ("vtok",))
            act.copy(vtok, o[:, :].rearrange("p (t n) -> p t n", t=4)).then_inc(evac["a"], 1)
            o = filled(act, ("kvout",))
            link(act.copy(kvO[:, 0:P], o[:, 0:P]))
            act.copy(kvO[0:NS, P:3 * P], o[0:NS, P:3 * P]).then_inc(evac["a"], 1)

            def exps(n, rows, heads, W, sink):
                act.wait_ge(s_max, n + 1)
                stat = stats[n % 2]
                sm = Sm[n % 2][0:rows, 0:heads * (2048 // H if heads == H else 256)] \
                    .rearrange("p (h s) -> p h s", h=heads)
                if sink:
                    link(act.activation(stat[0:rows, 24:24 + heads], stat[0:rows, 24:24 + heads], ACT.Exp))
                for h in range(heads):
                    ins = act.activation(sm[:, h, 0:W], sm[:, h, 0:W], ACT.Exp, bias=stat[0:rows, 8 + h:9 + h],
                                         accum_out=stat[0:rows, 16 + h:17 + h])
                ins.then_inc(s_exp, 1)

            act.wait_ge(s_sso, 16)
            exps(0, P, H, P, True)
            for t in range(TILES):
                if t < TILES - 1:
                    exps(t + 1, P, H, 2 * P, True)
                na = 1 if t == 0 else 2
                for i in range(4):
                    o = filled(act, ("pT", t, i))
                    act.copy(PTa[:, 2 * i:2 * i + 2, 0:na, :],
                             o[:, :].rearrange("p (n a q) -> p n a q", n=2, a=2)[:, :, 0:na, :]) \
                        .then_inc(evac["a"], 1)
                o = filled(act, ("o", t))
                act.copy(yT[:, 4:8, t * P:(t + 1) * P], o[:, :].rearrange("p (c q) -> p c q", c=4)) \
                    .then_inc(evac["a"], 1)
            for i in range(2):
                o = filled(act, ("kT", i))
                act.copy(kTs[:, 4 * i:4 * i + 4, :], o[:, :].rearrange("p (b s) -> p b s", b=4)) \
                    .then_inc(evac["a"], 1)
            exps(4, 64, 1, P, True)

            def row_norms(first, sem):
                for t in range(TILES + 1):
                    R = tile_rows(t)
                    act.wait_ge(evac["v"], sem[t])
                    ms = small[0:R, t:t + 1]
                    link(act.activation(junk[0:R, :], x[0:R, t, :], ACT.Square, accum_out=ms))
                    act.activation(ms, ms, ACT.Sqrt, scale=1.0 / D, bias=small[0:R, 41:42]).then_inc(s_sq2, 1)

            row_norms(0, [rank[("wo", t, 1)][1] for t in range(5)])
            for h in range(XH):
                for s in range(2):
                    o = filled(act, ("q", h, s))
                    act.copy(qT[:, h, s * HALF:(s + 1) * HALF], o[:, 0:HALF]).then_inc(evac["a"], 1)
            for what, n in CROSS_ORDER:
                if what == "xs":
                    exps(5 + n, P, XH, MT, False)
                elif what == "xp":
                    for i in range(2):
                        o = filled(act, ("xpT", n, i))
                        act.copy(PTc[:, 2 * i:2 * i + 2, :, :], o[:, :].rearrange("p (n a q) -> p n a q", n=2, a=2)) \
                            .then_inc(evac["a"], 1)
                    o = filled(act, ("xo", n))
                    act.copy(yT[:, 0:4, n * P:(n + 1) * P], o[:, :].rearrange("p (c q) -> p c q", c=4)) \
                        .then_inc(evac["a"], 1)
                elif what == "ckT":
                    for st in range(2):
                        o = filled(act, ("ckT", n, st))
                        act.copy(KT[n % 2][:, :, st, :], o[:, :].rearrange("p (h s) -> p h s", h=XH)) \
                            .then_inc(evac["a"], 1)
            exps(9, 32, 1, MT, False)
            row_norms(5, [rank[("wc", t, 1)][1] for t in range(5)])
            act.wait_ge(s_exp1, 1)
            act.activation(Ta[:, :, 0:4], Ta[:, :, 0:4], ACT.Exp).then_inc(s_exp2, 1)
            act.wait_ge(s_exp1, 2)
            act.activation(ee, ee, ACT.Exp).then_inc(s_exp2, 1)
            bG, bA, bY = banks[2], banks[3], banks[5]

            def act_block(i, b, r, first=False):
                act.wait_ge(s_pG, b + 1)
                act.activation(silu, bG[:, 0:FH], ACT.Silu).then_inc(s_as, 1)
                act.wait_ge(s_pA, b + 1)
                act.copy(actT, bA[:, 0:P]).then_inc(s_aa, 1)
                act.wait_ge(s_pY, b + 1)
                if not first:
                    act.wait_ge(s_ys[i], r * 16)
                act.copy(yb[i][:, 512:1024], bY[:, :]).then_inc(s_ay, 1)

            for i in range(NB3):
                act_block(i, i, 0, True)
            with act.Fori(1, NBLK // NB3) as it:
                for i in range(NB3):
                    act_block(i, it * NB3 + i, it)
            for t in range(T5):
                R = tile_rows(t)
                act.wait_ge(s_comb, t + 1)
                ms = small[0:R, t:t + 1]
                link(act.activation(junk[0:R, :], x[0:R, t, :], ACT.Square, accum_out=ms))
                act.activation(ms, ms, ACT.Sqrt, scale=1.0 / D, bias=small[0:R, 41:42]).then_inc(s_sq3, 1)

        @block.vector
        def _(dve):
            chain = [0]

            def link(ins):
                chain[0] += 1
                ins.then_inc(v_ch, 1)
                dve.wait_ge(v_ch, chain[0])

            tt, ts, stt = dve.tensor_tensor, dve.tensor_scalar, dve.scalar_tensor_tensor
            link(dve.memset(PR[:, :, 0:1], 0.0))
            link(dve.memset(small[:, 40:41], GN_EPS))
            dve.memset(small[:, 41:42], EPS).then_inc(s_eps, 1)
            o = filled(dve, ("par",))
            dve.tensor_copy(par[:, 0:42], o[:, 0:42]).then_inc(evac["v"], 1)
            o = filled(dve, ("shift_in",))
            dve.tensor_copy(shiftS, o[:, 0:RW * NS].rearrange("p (j n) -> p j n", j=RW)).then_inc(evac["v"], 1)

            for t in range(7):
                R = tile_rows(t) if t < 5 else P
                rows = x[0:R, t, :] if t < 5 else memX[:, t - 5, :]
                dve.wait_ge(s_sq, t + 1)
                ms = small[0:R, t:t + 1]
                link(dve.reciprocal(ms, ms))
                ts(rows, rows, ms, None, ALU.mult).then_inc(s_xn, 1)
                if t < 5:
                    for i in range(2):
                        o = filled(dve, ("xT", t, i))
                        g = gains[:, 0, 4 * i:4 * i + 4].unsqueeze(2).to_broadcast([P, 4, R])
                        tt(hA[:, 4 * i:4 * i + 4, t * P:t * P + R],
                           o[:, :].rearrange("p (k n) -> p k n", k=4)[:, :, 0:R], g, ALU.mult) \
                            .then_inc(evac["v"], 1)

            def mix(n, j):
                done(dve, ("proj", j, 1))
                link(dve.tensor_copy(saved[:, j, :], PR[:, j, SEQ:SEQ + 9]))
                d = tmp[n % 4]
                tt(d[:, 0:SEQ], PR[:, j, 0:SEQ], PR[:, j, 1:1 + SEQ], ALU.subtract)
                link(tt(d[:, SEQ:NT], shiftS[:, j, :], PR[:, j, 1 + SEQ:1 + NT], ALU.subtract))
                ins = stt(PR[:, j, 1:1 + NT], d, pcol("mu_shift", j), PR[:, j, 1:1 + NT], ALU.mult, ALU.add)
                ins.then_inc(s_mix, 1)

            dve.wait_ge(evac["v"], 2)
            mix(0, 12)
            mix(1, 13)
            for t in range(2):
                for i in range(2):
                    o = filled(dve, ("mT", t, i))
                    g = gains[:, 1, 4 * i:4 * i + 4].unsqueeze(2).to_broadcast([P, 4, P])
                    tt(memT[:, 4 * i:4 * i + 4, t * P:(t + 1) * P],
                       o[:, :].rearrange("p (k n) -> p k n", k=4), g, ALU.mult).then_inc(evac["v"], 1)
            for n, j in enumerate((4, 5, 6, 7, 0, 1, 2, 3, 8, 9, 10, 11)):
                mix(n, j)
            dve.wait_ge(s_mix, 14)
            link(dve.memset(reset, 1.0))
            link(dve.memset(reset.rearrange("p (n t) -> p n t", t=CH)[:, :, 0:1], 0.0))
            link(ts(small[:, 48:52], par[:, PARC["k_a"]:PARC["k_a"] + 4], -1.0, 1.0, ALU.mult, ALU.add))
            for c in range(4):
                R_, K_, V_ = PR[:, c, 1:1 + NT], PR[:, 4 + c, 1:1 + NT], PR[:, 8 + c, 1:1 + NT]
                kk, b = B0[:, c, :], B1[:, c, :]
                dve.wait_ge(s_act, 1)
                done(dve, ("lora_a", c, 1))
                link(ts(kk, K_, pcol("k_k", c), None, ALU.mult))
                tt(tmp[0], kk, kk, ALU.mult).then_inc(s_kk, 1)
                link(ts(tmp[3], aa[:, c, :], pcol("k_a", c), small[:, 48 + c:49 + c], ALU.mult, ALU.add))
                link(tt(K_, K_, tmp[3], ALU.mult))
                stt(tmp[1], R_, pcol("r_k", c), K_, ALU.mult, ALU.mult).then_inc(s_rk, 1)
                done(dve, ("norm_k", c, 1))
                link(ts(tmp[2], tmp[2], L2_EPS, None, ALU.max))
                link(dve.reciprocal(tmp[2], tmp[2]))
                link(tt(kk, kk, tmp[2], ALU.mult))
                link(tt(b, kk, aa[:, c, :], ALU.mult))
                for s in range(2):
                    o = filled(dve, ("bonus", c, s))
                    dve.tensor_copy(yT[:, c, s * HALF:(s + 1) * HALF], o[:, 0:HALF]).then_inc(evac["v"], 1)
                dve.tensor_tensor_scan(tmp[0][:, 0:SEQ], reset, sg[:, c, 0:SEQ], 0.0, ALU.mult, ALU.add) \
                    .then_inc(s_cs, 1)
                dve.wait_ge(s_cs, 3 * c + 1)
                tt(tmp[3][:, 0:SEQ], tmp[0][:, 0:SEQ], sg[:, c, 0:SEQ], ALU.subtract).then_inc(s_cs, 1)
                dve.wait_ge(s_ep, 4 * c + 1)
                link(dve.tensor_copy(PC[:, c, :], tmp[1][:, 0:SEQ].rearrange("p (n t) -> p n t", t=CH)[:, :, CH - 1]))
                link(tt(R_[:, 0:SEQ], R_[:, 0:SEQ], tmp[1][:, 0:SEQ], ALU.mult))
                cs = tmp[0][:, 0:SEQ].rearrange("p (n t) -> p n t", t=CH)
                tt(tmp[1][:, 0:SEQ].rearrange("p (n t) -> p n t", t=CH),
                   cs[:, :, CH - 1:CH].to_broadcast([P, NCH, CH]), cs, ALU.subtract).then_inc(s_cs, 1)
                dve.wait_ge(s_ep, 4 * c + 2)
                tt(Bt[:, c, 0:SEQ], b[:, 0:SEQ], tmp[2][:, 0:SEQ], ALU.mult)
                tt(Kt[:, c, 0:SEQ], K_[:, 0:SEQ], tmp[2][:, 0:SEQ], ALU.mult)
                dve.wait_ge(s_ep, 4 * c + 3)
                stt(kk[:, 0:SEQ], kk[:, 0:SEQ], -1.0, tmp[3][:, 0:SEQ], ALU.mult, ALU.mult)
                ts(kk[:, SEQ:NT], kk[:, SEQ:NT], -1.0, None, ALU.mult)
                dve.wait_ge(s_ep, 4 * c + 4)
                link(tt(b[:, 0:SEQ], b[:, 0:SEQ], tmp[1][:, 0:SEQ], ALU.mult))
                tt(K_[:, 0:SEQ], K_[:, 0:SEQ], tmp[1][:, 0:SEQ], ALU.mult).then_inc(s_prep, 1)
                dve.wait_ge(s_prep, c + 1)
            done(dve, ("tokV", 3))
            done(dve, ("svec", 5))
            for c in range(4):
                V_ = PR[:, 8 + c, 1:1 + NT]
                tt(V_, V_, yT[:, c, :], ALU.mult).then_inc(s_bv, 1)
            dve.memset(ST[:, 0, :, :], 0.0).then_inc(s_vz, 1)
            dve.wait_ge(s_vz, 1)

            def sample_step():
                dve.wait_ge(s_svl, 16 * 7)
                a_, b_, k_, w_, r_ = [sv[:, i, :].unsqueeze(1).to_broadcast([P, 32, HD]) for i in range(5)]
                link(tt(Stmp, SS, a_, ALU.mult))
                link(dve.tensor_reduce(ssa, Stmp, X, ALU.add))
                link(tt(SS, SS, w_, ALU.mult))
                link(tt(Stmp, b_, ssa.unsqueeze(2).to_broadcast([P, 32, HD]), ALU.mult))
                link(tt(SS, SS, Stmp, ALU.add))
                link(tt(Stmp, k_, svv.unsqueeze(2).to_broadcast([P, 32, HD]), ALU.mult))
                tt(SS, SS, Stmp, ALU.add).then_inc(s_ss, 1)
                dve.wait_ge(s_ss, 1)
                link(tt(Stmp, SS, r_, ALU.mult))
                dve.tensor_reduce(sy, Stmp, X, ALU.add).then_inc(s_ss, 1)

            for t in range(TILES):
                if t > 0:
                    filled(dve, ("Y", t - 1))
                for h in range(H):
                    o = filled(dve, ("AB", t, h))
                    tt(AB[:, h, :, :], o[:, :].rearrange("p (a t) -> p a t", a=4), maskAB, ALU.mult) \
                        .then_inc(evac["v"], 1)
                for q in range(2):
                    for h in range(4 * q, 4 * q + 4):
                        done(dve, ("AB", t, h))
                    if t > 0:
                        done(dve, ("G", t - 1))
                        done(dve, ("WT", t - 1))
                    idb = ident.unsqueeze(1).to_broadcast([P, 4, P])
                    tt(Xi[:, 4 * q:4 * q + 4, :], AB[:, 4 * q:4 * q + 4, 0, :], idb, ALU.add).then_inc(s_st, 1)
                dve.wait_ge(s_st, 2 * t + 2)
                for k in range(6):
                    for q in range(2):
                        qs = slice(4 * q, 4 * q + 4)
                        if k > 0:
                            o = filled(dve, ("XM", t, q, k))
                            tt(Xi[:, qs, :], Xi[:, qs, :], o[:, :].rearrange("p (h t) -> p h t", h=4), ALU.add) \
                                .then_inc(evac["v"], 1)
                        if k < 5 and rank[("NN", t, q, k)][0] == "v":
                            o = filled(dve, ("NN", t, q, k))
                            dve.tensor_copy(Ni[(k + 1) % 2][:, qs, :], o[:, :].rearrange("p (h t) -> p h t", h=4)) \
                                .then_inc(evac["v"], 1)
                for key, dst in (("akv", akv), ("G", Gt)):
                    o = filled(dve, (key, t))
                    dve.tensor_copy(dst, o[:, :]).then_inc(evac["v"], 1)
                done(dve, ("G", t))
                for u in range(2):
                    tk, n = 64 * u, 2 * t + u
                    if n > 0:
                        done(dve, ("S", n // 2 if n % 2 else n // 2 - 1, (n + 1) % 2))
                    link(tt(ST[:, n + 1, :, :], ST[:, n, :, :],
                            PC[:, :, n:n + 1].to_broadcast([P, 4, HD]), ALU.mult))
                    for e in range(2):
                        o = filled(dve, ("U", t, u, e))
                        of = [a[tk:tk + 64, :].rearrange("p (c e i) -> p c e i", e=2, i=HD)[:, :, e, :]
                              for a in (Ut, Gt)]
                        tt(of[0], o[tk:tk + 64, 0:256].rearrange("p (c i) -> p c i", c=4), of[1], ALU.add) \
                            .then_inc(evac["v"], 1)
                    o = filled(dve, ("S", t, u))
                    tt(ST[:, n + 1, :, :], ST[:, n + 1, :, :], o[:, 0:256].rearrange("p (c i) -> p c i", c=4),
                       ALU.add).then_inc(evac["v"], 1)
                if t == 0:
                    sample_step()
            o = filled(dve, ("ysT",))
            dve.tensor_copy(yT[:, 0:4, SEQ:NT], o[:, 0:4 * NS].rearrange("p (c n) -> p c n", c=4)) \
                .then_inc(evac["v"], 1)
            for c in range(4):
                for s in range(2):
                    o = filled(dve, ("mean", c, s))
                    hs = slice(s * HALF, (s + 1) * HALF)
                    stt(yT[:, c, hs], o[:, 0:HALF], -1.0 / HD, yT[:, c, hs], ALU.mult, ALU.add) \
                        .then_inc(evac["v"], 1)
                done(dve, ("mean", c, 1))
                tt(B0[:, c, :], yT[:, c, :], yT[:, c, :], ALU.mult).then_inc(s_yc, 1)
            for c in range(4):
                done(dve, ("var", c, 1))
                link(dve.reciprocal(B1[:, c, :], B1[:, c, :]))
                link(tt(yT[:, c, :], yT[:, c, :], B1[:, c, :], ALU.mult))
                link(ts(yT[:, c, :], yT[:, c, :], pcol("ln_x_w", c), pcol("ln_x_b", c), ALU.mult, ALU.add))
                link(tt(yT[:, c, :], yT[:, c, :], PR[:, 8 + c, 1:1 + NT], ALU.add))
            for c in range(4):
                for s in range(2):
                    o = filled(dve, ("gate", c, s))
                    hs = slice(s * HALF, (s + 1) * HALF)
                    tt(yT[:, c, hs], yT[:, c, hs], o[:, 0:HALF], ALU.mult).then_inc(evac["v"], 1)
            dve.memset(small[:, 42:43], 0.0).then_inc(s_fin, 1)
            dve.wait_ge(s_const, 64)
            for s in range(2):
                hs = slice(s * HALF, (s + 1) * HALF)
                for i in range(2):
                    o = filled(dve, ("rka", i, s))
                    tt(RK[i][:, hs], o[:, 0:HALF], cosT[:, hs], ALU.mult).then_inc(evac["v"], 1)
                    o = filled(dve, ("rkb", i, s))
                    tt(ropeT, o[:, 0:HALF], sinT[:, hs], ALU.mult).then_inc(evac["v"], 1)
                    done(dve, ("rkb", i, s))
                    link(tt(RK[i][:, hs], RK[i][:, hs], ropeT, ALU.add))
                for c in range(4):
                    o = filled(dve, ("rq", c, s))
                    tt(ropeT, o[:, 0:HALF], sinT[:, hs], ALU.mult).then_inc(evac["v"], 1)
                    link(tt(SQ[:, c, hs], SQ[:, c, hs], cosT[:, hs], ALU.mult))
                    done(dve, ("rq", c, s))
                    link(tt(SQ[:, c, hs], SQ[:, c, hs], ropeT, ALU.add))
            dve.memset(small[:, 43:44], 0.0).then_inc(s_rope, 1)
            dve.wait_ge(s_sink, 32)

            def softmax(n, rows, heads, W, sink):
                sm = Sm[n % 2][0:rows, 0:heads * 256].rearrange("p (h s) -> p h s", h=heads)[:, :, 0:W]
                stat = stats[n % 2]
                mx, neg, snk = stat[0:rows, 0:heads], stat[0:rows, 8:8 + heads], stat[0:rows, 24:24 + heads]
                link(dve.tensor_reduce(mx, sm, X, ALU.max))
                if sink is not None:
                    link(tt(mx, mx, sink, ALU.max))
                    link(tt(snk, sink, mx, ALU.subtract))
                ts(neg, mx, -1.0, None, ALU.mult).then_inc(s_max, 1)

            def normalise(n, rows, heads, W, sink):
                sm = Sm[n % 2][0:rows, 0:heads * 256].rearrange("p (h s) -> p h s", h=heads)[:, :, 0:W]
                stat = stats[n % 2]
                sums, snk = stat[0:rows, 16:16 + heads], stat[0:rows, 24:24 + heads]
                dve.wait_ge(s_exp, n + 1)
                if sink is not None:
                    link(tt(sums, sums, snk, ALU.add))
                link(dve.reciprocal(sums, sums))
                tt(sm, sm, sums.unsqueeze(2).to_broadcast([rows, heads, W]), ALU.mult).then_inc(s_prob, 1)

            def window_tile(t):
                W = P if t == 0 else 2 * P
                sm = Sm[t % 2].rearrange("p (h s) -> p h s", h=H)
                band = swamask[:, 2 * P - W:].unsqueeze(1).to_broadcast([P, 2, W])
                for e in range(2):
                    for i in range(2):
                        o = filled(dve, ("s", t, e, i))
                        stt(sm[:, 4 * i + e:4 * i + e + 3:2, 0:W], o[:, 0:2 * W].rearrange("p (n s) -> p n s", n=2),
                            HD ** -0.5, band, ALU.mult, ALU.add).then_inc(evac["v"], 1)
                done(dve, ("s", t, 1, 1))
                softmax(t, P, H, W, sinks[:, 0:H])

            window_tile(0)
            for t in range(TILES):
                if t < TILES - 1:
                    window_tile(t + 1)
                normalise(t, P, H, P if t == 0 else 2 * P, sinks)
            for e in range(2):
                o = filled(dve, ("qd", e))
                dve.tensor_copy(QD[:, :, :, e], o[:, 0:32].rearrange("p (c b) -> p b c", c=4)).then_inc(evac["v"], 1)
            for g in range(2):
                o = filled(dve, ("ss", g))
                dve.tensor_copy(sT.rearrange("p (b g m) -> p b g m", b=NS, g=2)[:, :, g, :],
                                o[:, 0:32].rearrange("p (b m) -> p b m", b=NS)).then_inc(evac["v"], 1)
            o = filled(dve, ("ssT",))
            ts(Sm[0][0:64, 0:P], o[0:64, 0:P], HD ** -0.5, None, ALU.mult).then_inc(evac["v"], 1)
            done(dve, ("ssT",))
            softmax(4, 64, 1, P, sinks[0:64, H:H + 1])
            normalise(4, 64, 1, P, sinks)
            o = filled(dve, ("spT",))
            dve.tensor_copy(pTs, o[:, 0:64]).then_inc(evac["v"], 1)
            o = filled(dve, ("so",))
            dve.tensor_copy(yT[:, 4:8, SEQ:NT], o[:, 0:32].rearrange("p (c b) -> p c b", c=4)) \
                .then_inc(evac["v"], 1)

            def residual(key, first, gi, hkey):
                for t in range(TILES + 1):
                    R = tile_rows(t)
                    if key == "wo":
                        dve.wait_ge(s_xr[t], 16)
                    for n in range(2):
                        o = filled(dve, (key, t, n))
                        ns = slice(n * 512, (n + 1) * 512)
                        tt(x[0:R, t, ns], x[0:R, t, ns], o[0:R, :], ALU.add).then_inc(evac["v"], 1)
                for t in range(TILES + 1):
                    R = tile_rows(t)
                    dve.wait_ge(s_sq2, first + t + 1)
                    ms = small[0:R, t:t + 1]
                    link(dve.reciprocal(ms, ms))
                    if t >= 2:
                        filled(dve, (hkey, t - 2, 1))
                        if key == "wc":
                            dve.wait_ge(s_hn[t % 2], 16 * (t // 2))
                    ts(xn[t % 2][0:R, :], x[0:R, t, :], ms, None, ALU.mult).then_inc(s_xn2, 1)
                    if t >= 1:
                        gained(hkey, t - 1, gi)
                gained(hkey, 4, gi)

            def gained(hkey, t, gi):
                R = tile_rows(t)
                for i in range(2):
                    o = filled(dve, (hkey, t, i))
                    g = gains[:, gi, 4 * i:4 * i + 4].unsqueeze(2).to_broadcast([P, 4, R])
                    tt(hA[:, 4 * i:4 * i + 4, t * P:t * P + R],
                       o[:, :].rearrange("p (k n) -> p k n", k=4)[:, :, 0:R], g, ALU.mult).then_inc(evac["v"], 1)

            dve.wait_ge(s_kvw, 32)
            residual("wo", 0, 2, "xT2")
            for what, n in CROSS_ORDER:
                if what == "xs":
                    sm = Sm[(5 + n) % 2][:, 0:1024].rearrange("p (h s) -> p h s", h=XH)
                    for i in range(2):
                        o = filled(dve, ("xs", n, i))
                        ts(sm[:, 2 * i:2 * i + 2, :], o[:, :].rearrange("p (n s) -> p n s", n=2), P ** -0.5, None,
                           ALU.mult).then_inc(evac["v"], 1)
                    done(dve, ("xs", n, 1))
                    softmax(5 + n, P, XH, MT, None)
                    if n > 0:
                        normalise(4 + n, P, XH, MT, None)
                    if n == TILES - 1:
                        normalise(5 + n, P, XH, MT, None)
                elif what == "cs":
                    o = filled(dve, ("cs", n))
                    dve.tensor_copy(csS[:, :, 4 * n:4 * n + 4], o[:, 0:8].rearrange("p (a h) -> p a h", a=2)) \
                        .then_inc(evac["v"], 1)
            o = filled(dve, ("csT",))
            ts(Sm[1][0:32, 0:MT], o[0:32, 0:MT], P ** -0.5, None, ALU.mult).then_inc(evac["v"], 1)
            done(dve, ("csT",))
            softmax(9, 32, 1, MT, None)
            normalise(9, 32, 1, MT, None)
            o = filled(dve, ("cpT",))
            dve.tensor_copy(cpS, o[:, 0:64].rearrange("p (a n) -> p a n", a=2)).then_inc(evac["v"], 1)
            o = filled(dve, ("co",))
            dve.tensor_copy(yT[:, 0:4, SEQ:NT], o[:, 0:4 * NS].rearrange("p (b h) -> p h b", h=XH)) \
                .then_inc(evac["v"], 1)
            residual("wc", 5, 3, "xT3")
            link(dve.memset(Lg, 0.0))
            dve.memset(onesm, 1.0)
            dve.memset(zer, 1.0)
            for i in range(NB3):
                dve.memset(xg[i], 0.0)
            dve.memset(slot_rows, 1e6).then_inc(s_init, 1)
            dve.wait_ge(s_init, 1)
            for t in range(T5):
                R = tile_rows(t)
                o = filled(dve, ("route", t))
                tt(Lg[0:R, t, :], o[0:R, 0:36], rbias[0:R, :], ALU.add).then_inc(evac["v"], 1)
            done(dve, ("route", 4))

            def wide(a, n):
                return a.unsqueeze(2).to_broadcast([P, T5, n])

            def first_max(src, n, top, out):
                io = iota[:, 0:n].unsqueeze(1).to_broadcast([P, T5, n])
                link(dve.tensor_reduce(top, src, X, ALU.max))
                link(tt(out, src, wide(top, n), ALU.is_lt))
                link(stt(out, out, 100.0, io, ALU.mult, ALU.add))
                link(dve.tensor_reduce(mi, out, X, ALU.min))
                link(tt(out, io, wide(mi, n), ALU.is_equal))

            lg, le = Lg[:, :, 0:4], Lg[:, :, 4:36]
            first_max(lg, 4, gmx, ohg)
            tt(Ta[:, :, 0:4], lg, wide(gmx, 4), ALU.subtract).then_inc(s_exp1, 1)
            dve.wait_ge(s_exp2, 1)
            link(dve.tensor_reduce(psel, Ta[:, :, 0:4], X, ALU.add))
            link(dve.reciprocal(psel, psel))
            link(ts(ohg, ohg, -NEG, NEG, ALU.mult, ALU.add))
            for t in range(T5):
                tt(Le[:, t, :].rearrange("p (g e) -> p g e", g=4), le[:, t, :].rearrange("p (g e) -> p g e", g=4),
                   ohg[:, t, :].unsqueeze(2).to_broadcast([P, 4, 8]), ALU.add)
            link(dve.memset(small[:, 44:45], 0.0))
            first_max(Le, NE, m1, oh[0])
            link(stt(Le, oh[0], NEG, Le, ALU.mult, ALU.add))
            first_max(Le, NE, m2, oh[1])
            tt(ee, m2, m1, ALU.subtract).then_inc(s_exp1, 1)
            for j in range(2):
                link(tt(oh[j], oh[j], wide(valid, NE), ALU.mult))
            tt(Mk, oh[0], oh[1], ALU.add).then_inc(s_mk, 1)
            dve.wait_ge(s_exp2, 2)
            link(ts(m1, ee, 1.0, None, ALU.add))
            link(dve.reciprocal(m1, m1))
            link(tt(cw[0], m1, psel, ALU.mult))
            link(tt(cw[1], cw[0], ee, ALU.mult))
            o = filled(dve, ("ranks",))
            dve.tensor_copy(RC, o[:, 0:6 * NE]).then_inc(evac["v"], 1)
            done(dve, ("ranks",))
            cnt_e = RC[:, T5 * NE:]
            link(ts(nb, cnt_e, 0.0, None, ALU.is_gt))
            for n in range(1, -(-NT // P)):
                link(ts(nb1, cnt_e, float(n * P), None, ALU.is_gt))
                link(tt(nb, nb, nb1, ALU.add))
            link(dve.tensor_tensor_scan(cum, zer, nb, 0.0, ALU.mult, ALU.add))
            link(tt(nb, cum, nb, ALU.subtract))
            link(stt(slot_all, nb.unsqueeze(1).to_broadcast([P, T5, NE]), float(P),
                     RC[:, 0:T5 * NE].rearrange("p (t e) -> p t e", t=T5), ALU.mult, ALU.add))
            link(ts(mi, valid, -1e6, 1e6, ALU.mult, ALU.add))
            for j in range(2):
                link(tt(Ta, oh[j], slot_all, ALU.mult))
                link(dve.tensor_reduce(sl[j], Ta, X, ALU.add))
                link(tt(sl[j], sl[j], mi, ALU.add))
            link(dve.tensor_copy(slI[0], sl[0]))
            dve.tensor_copy(slI[1], sl[1]).then_inc(s_slot, 1)
            link(tt(big, cum.unsqueeze(1).to_broadcast([P, NBLK, NE]),
                    iota.unsqueeze(2).to_broadcast([P, NBLK, NE]), ALU.is_le))
            link(dve.tensor_reduce(eid, big, X, ALU.add))
            link(ts(eid, eid, float(NE - 1), None, ALU.min))
            dve.tensor_copy(eidI, eid).then_inc(s_eid, 1)
            o = filled(dve, ("slots",))
            dve.tensor_copy(pidI, o[:, 0:NBLK]).then_inc(evac["v"], 1)
            done(dve, ("slots",))
            ts(tokI, pidI, 1, None, ALU.arith_shift_right).then_inc(s_idx, 1)
            bX, bG, bY = [banks[0], banks[1]], banks[2], banks[4]

            def rows_out(b):
                dve.wait_ge(s_pX, b + 1)
                for n in range(2):
                    g = gains[:, 3, 4 * n:4 * n + 4].unsqueeze(2).to_broadcast([P, 4, P])
                    ins = tt(xTe[:, 4 * n:4 * n + 4, :], bX[n][:, :].rearrange("p (k n) -> p k n", k=4), g, ALU.mult)
                ins.then_inc(s_vx, 1)

            def dve_block(i, b, r, first, nxt):
                dve.wait_ge(s_as, b + 1)
                tt(act_e, silu, bG[:, FH:2 * FH], ALU.mult).then_inc(s_vm, 1)
                if nxt:
                    rows_out(b + 1)
                dve.wait_ge(s_pY, b + 1)
                if not first:
                    dve.wait_ge(s_ys[i], r * 16)
                dve.tensor_copy(yb[i][:, 0:512], bY[:, :]).then_inc(s_vy, 1)

            rows_out(0)
            rounds = NBLK // NB3
            for i in range(NB3):
                dve_block(i, i, 0, True, True)
            with dve.Fori(1, rounds - 1) as it:
                for i in range(NB3):
                    dve_block(i, it * NB3 + i, it, False, True)
            for i in range(NB3):
                dve_block(i, (rounds - 1) * NB3 + i, rounds - 1, False, i < NB3 - 1)
            for t in range(T5):
                R = tile_rows(t)
                dve.wait_ge(s_yl[t % 2], 16 * (t // 2 + 1))
                link(stt(x[0:R, t, :], ydt[t % 2][0:R, 0, :], cw[0][0:R, t:t + 1], x[0:R, t, :], ALU.mult, ALU.add))
                stt(x[0:R, t, :], ydt[t % 2][0:R, 1, :], cw[1][0:R, t:t + 1], x[0:R, t, :], ALU.mult, ALU.add) \
                    .then_inc(s_comb, 1)
            for t in range(T5):
                R = tile_rows(t)
                dve.wait_ge(s_sq3, t + 1)
                ms = small[0:R, t:t + 1]
                link(dve.reciprocal(ms, ms))
                stt(x[0:R, t, :], x[0:R, t, :], ms, gfin[0:R, :], ALU.mult, ALU.mult).then_inc(s_res, 1)


_INS = ['x_prompt', 'x_sample', 'mem_prompt', 'state_rwkv_shift', 'state_rwkv_wkv', 'cache_swa_k', 'cache_swa_v',
        'cache_mem_k', 'cache_mem_v', 'norm_mix', 'w_in', 'mu_shift', 'w_decay0', 'w_decay_up', 'a0', 'w_a_up',
        'w_g_up', 'k_k', 'k_a', 'r_k', 'ln_x_w', 'ln_x_b', 'attn_sink', 'w_out', 'norm_cross', 'norm_mem', 'w_cq',
        'w_ck', 'w_cv', 'w_co', 'norm_ffn', 'w_group_router', 'b_group_router', 'w_expert_router',
        'b_expert_router', 'w_exp_gate', 'w_exp_up', 'w_exp_down', 'norm_final']
_OUTS = [('y_prompt', (1, 512, 1024)), ('y_sample', (8, 1, 1024)), ('prompt_shift', (1, 1, 1792)),
         ('prompt_wkv', (1, 1, 8, 64, 64)), ('prompt_swa_k', (1, 1, 128, 2, 64)),
         ('prompt_swa_v', (1, 1, 128, 2, 64)), ('prompt_mem_k', (1, 1, 256, 4, 128)),
         ('prompt_mem_v', (1, 1, 256, 4, 128)), ('sample_shift', (1, 8, 1792)), ('sample_wkv', (1, 8, 8, 64, 64)),
         ('sample_swa_k', (1, 8, 128, 2, 64)), ('sample_swa_v', (1, 8, 128, 2, 64))]


def tables():
    i = np.arange(P)
    ident = np.eye(P, dtype=np.float32)
    bones = (i[:, None] // HD == i[None, :] // HD).astype(np.float32)
    strict = bones * (i[:, None] < i[None, :])
    incl = bones * (i[:, None] <= i[None, :])
    diff = i[:, None] + P - np.arange(2 * P)[None, :]
    band = np.where((diff >= 0) & (diff < P), 0.0, NEG)
    tri = (i[:, None] < i[None, :]).astype(np.float32)
    swap = ((i[:, None] ^ 32) == i[None, :]).astype(np.float32)
    dup = [((i[:, None] // HD == g) & (i[:, None] % HD == i[None, :] % HD)).astype(np.float32) for g in range(2)]
    dsw = [((i[:, None] // HD == g) & ((i[:, None] % HD) ^ 32 == i[None, :] % HD)).astype(np.float32)
           for g in range(2)]
    pos = np.concatenate([np.arange(SEQ), np.full(NS, 1024)]).astype(np.float32)
    inv = (np.float32(10000.0) ** (-np.arange(32, dtype=np.float32) * np.float32(2.0) / np.float32(64)))
    ang = (pos[None, :] * inv.astype(np.float32)[:, None]).astype(np.float32)
    cos = np.tile(np.cos(ang), (4, 1))
    sin = np.tile(np.concatenate([-np.sin(ang), np.sin(ang)]), (2, 1))
    misc = np.zeros((P, 64), np.float32)
    misc[:, 0:NBLK] = np.arange(NBLK)
    tok = np.arange(TILES + 1)[None, :] * P + i[:, None]
    misc[:, NBLK:NBLK + 10] = (2 * tok[:, :, None] + np.arange(2)).reshape(P, 10)
    misc[:, NBLK + 10:NBLK + 15] = tok < NT
    parts = [ident, bones, strict, incl, strict, incl, band, tri, swap, dup[0], dup[1], dsw[0], dsw[1], cos, sin, misc]
    return np.concatenate(parts, axis=1).astype(np.float32)


def kernel(**inputs):
    import concourse.bacc as _bacc
    from concourse.bass_utils import run_bass_kernel_spmd as _run

    nc = _bacc.Bacc("TRN2", target_bir_lowering=False, num_devices=1)
    arrays, A, O = {}, {}, {}
    for name in _INS:
        a = np.ascontiguousarray(inputs[name])
        arrays[f"in_{name}"] = a
        A[name] = nc.dram_tensor(f"in_{name}", a.shape, mybir.dt.from_np(a.dtype), kind="ExternalInput").ap()
    c = tables()
    arrays["in_tables"] = c
    A["c_tables"] = nc.dram_tensor("in_tables", c.shape, F32, kind="ExternalInput").ap()
    for name, shape in _OUTS:
        O[name] = nc.dram_tensor(f"out_{name}", shape, F32, kind="ExternalOutput").ap()
    small_kernel(nc, A, O)
    r = _run(nc, [arrays], core_ids=[0])
    return tuple(r.results[0][f"out_{name}"] for name, _ in _OUTS)
```

```python
from contextlib import ExitStack

import numpy as np

import concourse.bass as bass
from concourse import mybir

F32 = mybir.dt.float32
I32 = mybir.dt.int32
U32 = mybir.dt.uint32
ALU = mybir.AluOpType
ACT = mybir.ActivationFunctionType
X = mybir.AxisListType.X

P = 128
D = 1024
KD = D // P
SEQ = 512
NS = 8
NT = SEQ + NS
HALF = NT // 2
TILES = SEQ // P
H = 8
HD = 64
PAIRS = H // 2
CH = 64
NCH = SEQ // CH
RW = 14
SW = 6
RCOLS = RW * P
MT = 256
XH = 4
EPS = 1e-5
GN_EPS = 64e-5
L2_EPS = 1e-12
KAPPA = float(np.exp(-0.5))
NEG = -1e30
NE = 32
FH = 128
PAIRS_E = 2 * NT
BS = 64
BSHIFT = BS.bit_length() - 1
OVER = (PAIRS_E - 1) // BS
NBLK = NE + OVER
MISC = NBLK + 16
BANKS = 8

PAR_ROWS = (("mu_shift", 14), ("w_decay0", 4), ("a0", 4), ("k_k", 4), ("k_a", 4), ("r_k", 4), ("ln_x_w", 4),
            ("ln_x_b", 4))


FRONT_ORDER = [("proj", 12), ("proj", 13), ("proj", 14), ("proj", 15), ("mT", 0), ("lora", 0), ("mem", 0),
               ("proj", 4), ("proj", 5), ("proj", 6), ("proj", 7), ("proj", 0), ("pre", 0), ("proj", 1), ("pre", 1),
               ("sums", 0), ("post", 0), ("proj", 2), ("sums", 1), ("pre", 2), ("post", 1), ("proj", 3), ("proj", 8),
               ("sums", 2), ("pre", 3), ("post", 2), ("proj", 9), ("proj", 10), ("sums", 3), ("post", 3),
               ("proj", 11), ("proj", 16), ("proj", 17), ("proj", 18), ("proj", 19)]

CROSS_ORDER = (("xs", 0), ("ckT", 0), ("xs", 1), ("ckT", 1), ("xp", 0), ("cs", 0), ("xs", 2), ("ckT", 2), ("cs", 1),
               ("ckT", 3), ("xp", 1), ("cs", 2), ("xs", 3), ("ckT", 4), ("cs", 3), ("ckT", 5), ("cs", 4),
               ("xp", 2), ("ckT", 6), ("cs", 5), ("ckT", 7), ("cs", 6), ("xp", 3), ("cs", 7))


def tile_rows(t):
    return P if t < TILES else NS


def bank_plan():
    g = [(("par",), "v"), (("shift_in",), "v")]
    for t in range(TILES + 1):
        g += [(("xT", t, i), "v") for i in range(2)]
    for what, n in FRONT_ORDER:
        if what == "proj":
            g += [(("proj", n, s), "a") for s in range(2)]
        elif what == "mT":
            g += [(("mT", t, i), "v") for t in range(2) for i in range(2)]
        elif what == "lora":
            g += [((key, c, s), "a") for key in ("lora_w", "lora_a") for c in range(4) for s in range(2)]
        elif what == "mem":
            g += [((key, t), "a") for key in ("mk", "mv", "mkT") for t in range(2)]
        elif what == "sums":
            g += [(("norm_k", n, s), "a") for s in range(2)] + [(("bonus", n, s), "v") for s in range(2)]
    g += [(("shift_out", i), "a") for i in range(4)]
    g += [(("svec", i), "a") for i in range(6)]
    g += [(("tokV", t), "a") for t in range(TILES)]
    for t in range(TILES):
        g += [(("tok", t, i), "a") for i in range(3)]
        g += [(("AB", t, h), "v") for h in range(H)]
        g += [(("N0", t, q), "a") for q in range(2)]
        for k in range(6):
            for q in range(2):
                if k > 0:
                    g += [(("XM", t, q, k), "v")]
                if k < 4:
                    g += [(("MM", t, q, k), "a")]
                if k < 5:
                    g += [(("NN", t, q, k), "v" if k % 2 else "a")]
        g += [(("akv", t), "v"), (("G", t), "v"), (("WT", t), "a")]
        for u in range(2):
            g += [(("U", t, u, 0), "v"), (("U", t, u, 1), "v"), (("S", t, u), "v")]
        g += [(("Y", t), "a")]
    g += [(("wkvT",), "a"), (("ysT",), "v")]
    g += [(("mean", c, s), "v") for c in range(4) for s in range(2)]
    g += [(("var", c, s), "a") for c in range(4) for s in range(2)]
    g += [(("gate", c, s), "v") for c in range(4) for s in range(2)]
    for s in range(2):
        for i in range(2):
            g += [(("rka", i, s), "v"), (("rkb", i, s), "v")]
        g += [(("rq", c, s), "v") for c in range(4)]
    g += [(("vtok",), "a"), (("kvout",), "a")]
    for t in range(-1, TILES):
        if t < TILES - 1:
            g += [(("s", t + 1, e, i), "v") for e in range(2) for i in range(2)]
        if t >= 0:
            g += [(("pT", t, i), "a") for i in range(4)]
            g += [(("o", t), "a")]
    g += [(("qd", e), "v") for e in range(2)]
    g += [(("kT", i), "a") for i in range(2)]
    g += [(("ss", e), "v") for e in range(2)]
    g += [(("ssT",), "v"), (("spT",), "v"), (("so",), "v")]
    g += [(("wo", t, n), "v") for t in range(TILES + 1) for n in range(2)]
    for t in range(TILES + 1):
        g += [(("xT2", t, i), "v") for i in range(2)]
    g += [(("q", h, s), "a") for h in range(XH) for s in range(2)]
    for step in CROSS_ORDER:
        what, n = step
        g += {"xs": [(("xs", n, i), "v") for i in range(2)],
              "xp": [(("xpT", n, i), "a") for i in range(2)] + [(("xo", n), "a")],
              "ckT": [(("ckT", n, i), "a") for i in range(2)],
              "cs": [(("cs", n), "v")]}[what]
    g += [(("csT",), "v"), (("cpT",), "v"), (("co",), "v")]
    g += [(("wc", t, n), "v") for t in range(TILES + 1) for n in range(2)]
    for t in range(TILES + 1):
        g += [(("xT3", t, i), "v") for i in range(2)]
    g += [(("route", t), "v") for t in range(TILES + 1)]
    g += [(("ranks",), "v"), (("slots",), "v")]
    return g


def small_kernel(nc, A, O):
    plan = bank_plan()
    place = {key: n for n, (key, _) in enumerate(plan)}
    rank, count = {}, {"v": 0, "a": 0}
    for key, e in plan:
        count[e] += 1
        rank[key] = (e, count[e])

    with ExitStack() as ctx:
        def sem(name):
            return ctx.enter_context(nc.semaphore(name))

        arena = ctx.enter_context(nc.sbuf_tensor("arena", [P, 53150], F32))
        at = {}

        def region(name, words, start=None):
            if start is None:
                start = at["_end"]
                at["_end"] = start + words
            at[name] = start
            return arena[:, start:start + words]

        at["_end"] = 0
        ident = region("ident", P)
        bones = region("bones", P)
        maskAB = region("maskAB", 4 * P).rearrange("p (a t) -> p a t", a=4)
        swamask = region("swamask", 2 * P)
        tri = region("tri", P)
        sel = region("sel", 5 * P).rearrange("p (a t) -> p a t", a=5)
        cosT = region("cosT", NT)
        sinT = region("sinT", NT)
        misc = region("misc", MISC)
        gains = region("gains", 4 * KD).rearrange("p (a k) -> p a k", a=4)
        par = region("par", 48)
        small = region("small", 64)
        lora = region("lora", 512)
        gup = region("gup", 512)
        mkT = region("mkT", XH * MT).rearrange("p (h s) -> p h s", h=XH)
        mv = region("mv", 2 * 512).rearrange("p (t n) -> p t n", t=2)
        stat = region("stat", 64)
        stats = [stat[:, 32 * i:32 * i + 32] for i in range(2)]
        sinks = region("sinks", 2 * H)
        saved = region("saved", RW * 9).rearrange("p (j n) -> p j n", j=RW)
        shiftS = region("shiftS", RW * NS).rearrange("p (j n) -> p j n", j=RW)
        PC = region("PC", 32).rearrange("p (c n) -> p c n", c=4)
        wS = region("wS", 32).rearrange("p (c n) -> p c n", c=4)
        hA = region("hA", KD * NT).rearrange("p (k n) -> p k n", k=KD)
        hB = region("hB", KD * NT).rearrange("p (k n) -> p k n", k=KD)
        ring = [region(f"ring{i}", 4096) for i in range(3)]
        PR = region("PR", RW * (NT + 1)).rearrange("p (j n) -> p j n", j=RW)
        SQ = region("SQ", SW * NT).rearrange("p (j n) -> p j n", j=SW)
        B0 = region("B0", 4 * NT).rearrange("p (c n) -> p c n", c=4)
        B1 = region("B1", 4 * NT).rearrange("p (c n) -> p c n", c=4)
        xreg = region("x", 5 * D)
        x = xreg.rearrange("p (t n) -> p t n", t=5)
        tokV = region("tokV", TILES * 512).rearrange("p (t n) -> p t n", t=TILES)
        STr = region("ST", 9 * 256)
        ST = STr.rearrange("p (s c i) -> p s c i", s=9, c=4)
        assert at["_end"] <= 53150, at["_end"]
        memT = arena[:, at["hB"]:at["hB"] + KD * MT].rearrange("p (k n) -> p k n", k=KD)
        memX = arena[:, at["hB"] + 2080:at["hB"] + 2080 + 2048].rearrange("p (t n) -> p t n", t=2)
        mkS = arena[:, at["hB"] + 2080:at["hB"] + 2080 + 1024].rearrange("p (t n) -> p t n", t=2)
        junk = arena[:, at["B0"]:at["B0"] + D]
        prow = arena[:, at["B0"] + 1100:at["B0"] + 1100 + P]
        srow = arena[:, at["B1"]:at["B1"] + RCOLS]
        sg = arena[:, at["x"]:at["x"] + 2080].rearrange("p (c n) -> p c n", c=4)
        aa = arena[:, at["x"] + 2080:at["x"] + 4160].rearrange("p (c n) -> p c n", c=4)
        reset = arena[:, at["x"] + 4160:at["x"] + 4160 + SEQ]
        tmp = [arena[:, at["x"] + 4672 + i * NT:at["x"] + 4672 + (i + 1) * NT] for i in range(9)]
        assert at["x"] + 4672 + 9 * NT <= at["_end"] and at["tokV"] == at["x"] + 5 * D
        sq, csum, tail, diffs = tmp[0:2], tmp[2:4], tmp[4:6], tmp[6:8]
        Bt = hA[:, 0:4, :]
        Kt = hA[:, 4:8, :]
        Xi = arena[:, at["x"]:at["x"] + 1024].rearrange("p (h t) -> p h t", h=H)
        Mi = [arena[:, at["x"] + 1024 * (1 + i):at["x"] + 1024 * (2 + i)].rearrange("p (h t) -> p h t", h=H)
              for i in range(2)]
        Ni = [arena[:, at["x"] + 1024 * (3 + i):at["x"] + 1024 * (4 + i)].rearrange("p (h t) -> p h t", h=H)
              for i in range(2)]
        AB = ring[1].rearrange("p (h a t) -> p h a t", h=H, a=4)
        tokX = ring[2][:, 0:1536].rearrange("p (i n) -> p i n", i=3)
        akv = ring[2][:, 1536:2048]
        Gt = ring[2][:, 2048:2560]
        WT = ring[2][:, 2560:3072].rearrange("p (c t) -> p c t", c=4)
        Ut = ring[2][:, 3072:3584]
        yT = hB
        SS = arena[:, at["hB"] + 2080:at["hB"] + 2080 + 2048].rearrange("p (i j) -> p i j", i=32)
        Stmp = ring[0][:, 0:2048].rearrange("p (i j) -> p i j", i=32)
        sv = ring[0][:, 3072:3072 + 5 * HD].rearrange("p (a j) -> p a j", a=5)
        svv = ring[0][:, 3400:3432]
        ssa = ring[0][:, 3432:3464]
        sy = ring[0][:, 3464:3496]
        svt6 = ring[0][0:NS, 0:3072].rearrange("p (a n) -> p a n", a=6)
        shiftO = arena[0:9, at["tokV"]:at["tokV"] + RCOLS]
        wkvO = ring[1][0:64, 0:512]
        RK = [hA.rearrange("p k n -> p (k n)")[:, i * NT:(i + 1) * NT] for i in range(2)]
        hAf = arena[:, at["hA"]:at["hA"] + KD * NT]
        vtok = hAf[:, 1040:1552].rearrange("p (t n) -> p t n", t=4)
        PTa = hAf[:, 1552:3600].rearrange("p (h a q) -> p h a q", h=H, a=2)
        PTc = arena[:, at["tokV"]:at["tokV"] + 1024].rearrange("p (h a q) -> p h a q", h=XH, a=2)
        kvO = hAf[:, 3600:3984]
        Sm = [ring[2][:, 2048 * i:2048 * (i + 1)] for i in range(2)]
        ropeT = arena[:, at["B0"]:at["B0"] + HALF]
        Kc = arena[:, at["tokV"]:at["tokV"] + 1024].rearrange("p (b n) -> p b n", b=NS)
        Vc = arena[:, at["tokV"] + 1024:at["tokV"] + 2048].rearrange("p (b n) -> p b n", b=NS)
        kTs = STr[:, 0:1024].rearrange("p (b s) -> p b s", b=NS)
        QD = STr[:, 1024:1088].rearrange("p (b c e) -> p b c e", b=NS, c=4)
        sT = STr[:, 2048:2048 + 64]
        pTs = STr[:, 2112:2112 + 64]
        xn = [arena[:, at["PR"] + i * D:at["PR"] + (i + 1) * D] for i in range(2)]
        kv_ring = [arena[:, at["PR"] + (2 + i) * 1024:at["PR"] + (3 + i) * 1024].rearrange("p (a n) -> p a n", a=2)
                   for i in range(4)]
        late = [hAf[:, i * 1024:(i + 1) * 1024].rearrange("p (a n) -> p a n", a=2) for i in range(4)]

        def values_of(b):
            return kv_ring[b] if b < 4 else late[b - 4]

        KT = [arena[:, at["B1"] + i * 1024:at["B1"] + (i + 1) * 1024].rearrange("p (h a s) -> p h a s", h=XH, a=2)
              for i in range(2)]
        csS = STr[:, 0:64].rearrange("p (a n) -> p a n", a=2)
        cpS = STr[:, 64:128].rearrange("p (a n) -> p a n", a=2)
        qT = SQ[:, 0:4, :]
        iota = misc[:, 0:NBLK]
        pair_no = misc[:, NBLK:NBLK + 10].rearrange("p (t j) -> p t j", j=2)
        valid = misc[:, NBLK + 10:NBLK + 15]
        NB3 = 4
        wslots = [at["ring0"] + i * 3072 for i in range(4)] + [at["SQ"], at["lora"], at["PR"], at["PR"] + 3072]
        assert at["stat"] - at["lora"] == 3072
        NW = len(wslots)
        we = [arena[:, w:w + 3072].rearrange("p (a n) -> p a n", a=3) for w in wslots]
        xg = [arena[:, at["hA"] + i * D:at["hA"] + (i + 1) * D] for i in range(NB3)]
        yb = [arena[0:BS, at["B0"] + i * D:at["B0"] + (i + 1) * D] for i in range(NB3)]
        xTe = [arena[:, at["PR"] + 6 * D + i * KD * BS:at["PR"] + 6 * D + (i + 1) * KD * BS]
               .rearrange("p (k n) -> p k n", k=KD) for i in range(2)]
        silu, act_f = [arena[:, at["maskAB"] + i * P:at["maskAB"] + (i + 1) * P] for i in range(2)]
        silu, act_e = silu[0:BS], act_f[0:BS]
        actT = arena[:, at["maskAB"] + 2 * P:at["maskAB"] + 2 * P + BS]
        gfin = arena[:, at["tokV"] + 1024:at["tokV"] + 2048]
        wrG = STr[:, 256:288].rearrange("p (k n) -> p k n", k=KD)
        wrE = STr[:, 288:544].rearrange("p (k n) -> p k n", k=KD)
        rbias = STr[:, 544:580]
        ydt = [arena[:, at["ring0"] + i * 2048:at["ring0"] + (i + 1) * 2048].rearrange("p (j n) -> p j n", j=2)
               for i in range(2)]
        hBf = arena[:, at["hB"]:at["hB"] + KD * NT]
        off = [0]

        def route_region(n, dt=None):
            v = hBf[:, off[0]:off[0] + n]
            off[0] += n
            return v if dt is None else v.bitcast(dt)

        T5 = TILES + 1
        Lg = route_region(T5 * 36).rearrange("p (t n) -> p t n", t=T5)
        Le = route_region(T5 * NE).rearrange("p (t n) -> p t n", t=T5)
        Ta = route_region(T5 * NE).rearrange("p (t n) -> p t n", t=T5)
        oh = [route_region(T5 * NE).rearrange("p (t n) -> p t n", t=T5) for _ in range(2)]
        ohg = route_region(T5 * 4).rearrange("p (t n) -> p t n", t=T5)
        Mk = route_region(T5 * NE).rearrange("p (t n) -> p t n", t=T5)
        RC = route_region(6 * NE)
        slot_all = route_region(T5 * NE).rearrange("p (t n) -> p t n", t=T5)
        gmx, psel, m1, m2, mi, ee = [route_region(T5) for _ in range(6)]
        cw = [route_region(T5) for _ in range(2)]
        sl = [route_region(T5) for _ in range(2)]
        slI = [route_region(T5, I32) for _ in range(2)]
        nb, cum, zer = [route_region(NE) for _ in range(3)]
        big = route_region(OVER * NE).rearrange("p (b e) -> p b e", b=OVER)
        far = route_region(T5 * NE).rearrange("p (t n) -> p t n", t=T5)
        eid = route_region(OVER + 1)
        eidI = route_region(OVER + 1, I32)
        nbI = route_region(NE, I32)
        slot_rows = route_region(BS)
        pidI = route_region(NBLK, I32)
        tokI = route_region(NBLK, I32)
        idg = [route_region(1, I32)[0:BS] for _ in range(NB3)]
        ids = [route_region(1, I32)[0:BS] for _ in range(NB3)]
        onesm = route_region(P)
        scrap = route_region(5)
        assert off[0] <= KD * NT
        banks = [ctx.enter_context(nc.psum_tensor(f"bank{i}", [P, 512], F32)) for i in range(BANKS)]

        vec_d = nc.dram_tensor("vec_d", (6, NS, 512), F32, kind="Internal").ap()
        hn_d = nc.dram_tensor("hn_d", (NT, D), F32, kind="Internal").ap()
        slot_d = nc.dram_tensor("slot_d", (NBLK * BS, 1), F32, kind="Internal").ap()
        pair_d = nc.dram_tensor("pair_d", (PAIRS_E, D), F32, kind="Internal").ap()
        ys_d = nc.dram_tensor("ys_d", (NS, 512), F32, kind="Internal").ap()

        full = sem("psum_full")
        evac = {"v": sem("emptied_by_vector"), "a": sem("emptied_by_scalar")}
        s_const = sem("constants_loaded")
        s_par = sem("params_loaded")
        s_x = [sem(f"x_loaded{t}") for t in range(5)]
        s_mem = sem("mem_loaded")
        s_w = [sem(f"weights_loaded{i}") for i in range(3)]
        s_sq = sem("row_norms_ready")
        s_eps = sem("eps_set")
        s_xn = sem("rows_normed")
        s_vz = sem("vector_zeroed")
        v_ch = sem("vector_chain")
        a_ch = sem("scalar_chain")
        s_mix = sem("chunks_mixed")
        s_act = sem("lora_inputs_ready")
        s_kk = sem("key_squares_ready")
        s_rk = sem("bonus_products_ready")
        s_cs = sem("decay_sums_ready")
        s_ep = sem("decay_factors_ready")
        s_inv = sem("chunk_decays_inverted")
        s_tilde = sem("start_referred_operands_ready")
        s_prep = sem("rwkv_operands_ready")
        s_bv = sem("bonus_applied")
        s_st = sem("state_ready")
        s_svd = sem("sample_vectors_out")
        s_svl = sem("sample_vectors_in")
        s_ss = sem("sample_states_done")
        s_ysl = sem("sample_outputs_in")
        s_yc = sem("y_centred")
        s_fin = sem("y_final")
        s_mout = sem("mem_rows_written")
        s_shout = sem("shift_rows_written")
        s_out = sem("outputs_written")
        s_wkvo = sem("prompt_states_written")
        s_sink = sem("sinks_loaded")
        s_sso = sem("sample_states_written")
        s_cache = sem("window_rows_loaded")
        s_newkv = sem("new_window_rows_written")
        s_xr = [sem(f"x_reloaded{t}") for t in range(5)]
        s_kvr = [sem(f"memory_cache_loaded{i}") for i in range(4)]
        s_late = sem("late_memory_values_loaded")
        s_max = sem("row_maxima_ready")
        s_exp = sem("exponentials_ready")
        s_prob = sem("probabilities_ready")
        s_sq2 = sem("row_norms2_ready")
        s_xn2 = sem("rows_normed2")
        s_rope = sem("keys_rotated")
        s_rw = sem("router_weights_loaded")
        s_hn = [sem(f"normed_rows_written{i}") for i in range(2)]
        s_mk = sem("choices_ready")
        s_exp1 = sem("router_exponents_ready")
        s_exp2 = sem("router_exponentials_done")
        s_init = sem("slot_table_cleared")
        s_sinit = sem("slot_table_written")
        s_slot = sem("slots_ready")
        s_scat = sem("slots_scattered")
        s_srow = sem("slot_rows_loaded")
        s_eid = sem("expert_ids_ready")
        s_idx = sem("row_indices_ready")
        s_wgu = [sem(f"gate_up_loaded{i}") for i in range(NW)]
        s_wd = [sem(f"down_loaded{i}") for i in range(NW)]
        s_osc = sem("beyond_rows_scattered")
        s_free = sem("beyond_block_may_start")
        s_ow = sem("beyond_weights_loaded")
        s_ogx = sem("beyond_rows_gathered")
        s_oP = sem("beyond_tensor_steps")
        s_oV = sem("beyond_vector_steps")
        s_oA = sem("beyond_scalar_steps")
        s_gx = [sem(f"rows_gathered{i}") for i in range(NB3)]
        s_ys = [sem(f"rows_scattered{i}") for i in range(NB3)]
        s_idc = sem("pool_index_copied")
        s_pX = sem("rows_transposed")
        s_pG = sem("gate_up_products")
        s_pA = sem("activation_transposed")
        s_pY = sem("down_products")
        s_vx = sem("rows_in_sbuf")
        s_as = sem("silu_done")
        s_vm = sem("activation_done")
        s_aa = sem("activation_in_sbuf")
        s_vy = sem("left_half_out")
        s_ay = sem("right_half_out")
        s_yl = [sem(f"pair_rows_loaded{i}") for i in range(2)]
        s_comb = sem("experts_added")
        s_sq3 = sem("row_norms3_ready")
        s_res = sem("results_ready")
        s_kvw = sem("prompt_window_rows_written")
        outs = [0]

        def bank(key):
            return banks[place[key] % BANKS]

        def reuse(pe, key):
            n = place[key]
            if n >= BANKS:
                e, k = rank[plan[n - BANKS][0]]
                pe.wait_ge(evac[e], k)
            return bank(key)

        def filled(eng, key):
            eng.wait_ge(full, place[key] + 1)
            return bank(key)

        def done(eng, key):
            e, k = rank[key]
            eng.wait_ge(evac[e], k)

        PARC = {}
        r = 0
        for name, n in PAR_ROWS:
            PARC[name] = r
            r += n

        def pcol(name, c):
            return par[:, PARC[name] + c:PARC[name] + c + 1]

        block = ctx.enter_context(nc.Block())

        w_in = A["w_in"][0].rearrange("(p k) n -> p k n", k=KD)
        loads = []
        for i, grp in enumerate((3, "w_ck", "w_cv", 1, 0, 2, 4)):
            if isinstance(grp, str):
                loads.append(((grp,), i % 3, A[grp][0].rearrange("(p k) n -> p k n", k=KD), KD))
            else:
                loads.append((("w_in", grp), i % 3, w_in[:, :, grp * 512:(grp + 1) * 512], KD))
        n_early = len(loads)
        w_o = A["w_out"][0].rearrange("(c p) n -> p c n", p=P)
        loads.append((("wo", 0), 0, w_o[:, 0:4, :], 4))
        loads.append((("wo", 1), 1, w_o[:, 4:8, :], 4))
        loads.append((("w_cq",), 1, A["w_cq"][0].rearrange("(p k) n -> p k n", k=KD), KD))
        loads.append((("w_co",), 0, A["w_co"][0].rearrange("(c p) n -> p c n", p=P), 4))
        slot_of, loaded_at, cnt = {}, {}, [0, 0, 0]
        for key, s, _, _ in loads:
            cnt[s] += 16
            slot_of[key], loaded_at[key] = s, cnt[s]

        def weights(key, k=KD):
            return ring[slot_of[key]].rearrange("p (k n) -> p k n", k=k)

        def weights_in(pe, key):
            pe.wait_ge(s_w[slot_of[key]], loaded_at[key])

        last_use = {("w_in", 3): ("proj", 15, 1), ("w_in", 1): ("proj", 7, 1), ("w_in", 0): ("proj", 3, 1),
                    ("w_in", 2): ("proj", 11, 1), ("w_in", 4): ("proj", 19, 1), ("w_ck",): ("mk", 1),
                    ("w_cv",): ("mv", 1), ("wo", 0): ("wo", 4, 1), ("wo", 1): ("wo", 4, 1), ("w_cq",): ("q", 3, 1)}

        @block.sync
        def _(sp):
            c = A["c_tables"]
            sp.dma_start(ident, c[:, 0:P]).then_inc(s_par, 16)
            r = 0
            for name, n in PAR_ROWS:
                src = A[name][0]
                if name == "r_k":
                    src = src.rearrange("h d -> (h d)")
                sp.dma_start(prow[r:r + n, :], src.rearrange("(r c) -> r c", c=P)).then_inc(s_par, 16)
                r += n
            sp.dma_start(srow[0:NS, :], A["state_rwkv_shift"][0]).then_inc(s_par, 16)
            for i, name in enumerate(("norm_mix", "norm_mem", "norm_cross", "norm_ffn")):
                sp.dma_start(gains[:, i, :], A[name][0].rearrange("(p k) -> p k", k=KD)).then_inc(s_par, 16)
            for t in range(TILES):
                sp.dma_start(x[:, t, :], A["x_prompt"][0, t * P:(t + 1) * P, :]).then_inc(s_x[t], 16)
            sp.dma_start(x[0:NS, 4, :], A["x_sample"][:, 0, :]).then_inc(s_x[4], 16)
            for i in range(3):
                key, s, src, k = loads[i]
                sp.dma_start(weights(key, k), src).then_inc(s_w[s], 16)
                if i == 0:
                    sp.dma_start(arena[:, P:at["gains"]], c[:, P:at["gains"]]).then_inc(s_const, 16)
                    sp.dma_start(memX, A["mem_prompt"][0].rearrange("(t p) n -> p t n", p=P)).then_inc(s_mem, 16)
                    sp.dma_start(lora[0:64, :], A["w_decay_up"][0]).then_inc(s_const, 16)
                    sp.dma_start(lora[64:128, :], A["w_a_up"][0]).then_inc(s_const, 16)
                    sp.dma_start(gup, A["w_g_up"][0]).then_inc(s_const, 16)
            row = A["attn_sink"]
            sp.dma_start(sinks[:, 0:H], bass.AP(row.tensor, row.offset, [[0, P], [1, H]])).then_inc(s_sink, 16)
            sp.dma_start(sinks[0:64, H:H + 1], bass.AP(row.tensor, row.offset, [[0, NS], [1, H], [1, 1]])) \
                .then_inc(s_sink, 16)
            for i in range(3, n_early):
                key, s, src, k = loads[i]
                prev = [l[0] for l in loads[:i] if l[1] == s][-1]
                sp.wait_ge(full, place[last_use[prev]] + 1)
                sp.dma_start(weights(key, k), src).then_inc(s_w[s], 16)
            done(sp, ("mk", 1))
            sp.dma_start(O["prompt_mem_k"][0, 0].rearrange("(t p) h d -> p t (h d)", p=P), mkS).then_inc(s_mout, 16)
            done(sp, ("mv", 1))
            sp.dma_start(O["prompt_mem_v"][0, 0].rearrange("(t p) h d -> p t (h d)", p=P), mv).then_inc(s_mout, 16)
            done(sp, ("shift_out", 3))
            sp.dma_start(O["prompt_shift"][0], shiftO[0:1, :]).then_inc(s_shout, 16)
            sp.dma_start(O["sample_shift"][0], shiftO[1:9, :]).then_inc(s_shout, 16)
            for kv in "kv":
                sp.dma_start(O[f"sample_swa_{kv}"][0, :, 0:P - 1], A[f"cache_swa_{kv}"][0, :, 1:P]) \
                    .then_inc(s_out, 16)
            sp.wait_ge(s_mout, 32)
            done(sp, ("mkT", 1))
            sp.dma_start(SS.rearrange("p i j -> p (i j)"),
                         A["state_rwkv_wkv"][0].rearrange("b h (u i) j -> (b h u) (i j)", u=2)).then_inc(s_svl, 16)
            done(sp, ("svec", 5))
            sp.dma_start(vec_d.rearrange("a b n -> b a n"), svt6).then_inc(s_svd, 16)
            sp.wait_ge(s_svd, 16)
            for a in range(5):
                src = vec_d[a].rearrange("b (h j) -> (b h) j", j=HD)
                src = bass.AP(src.tensor, src.offset, [[HD, NS * H], [0, 2], [1, HD]])
                sp.dma_start(sv[:, a, :], src).then_inc(s_svl, 16)
            sp.dma_start(svv, vec_d[5].rearrange("b (q i) -> (b q) i", i=32)).then_inc(s_svl, 16)
            sp.wait_ge(s_ss, 1)
            sp.dma_start(O["sample_wkv"][0].rearrange("b h (u i) j -> (b h u) (i j)", u=2),
                         SS.rearrange("p i j -> p (i j)")).then_inc(s_sso, 16)
            sp.wait_ge(s_ss, 2)
            sp.dma_start(ys_d.rearrange("b (q i) -> (b q) i", i=32), sy).then_inc(s_svd, 16)
            sp.wait_ge(s_svd, 32)
            sp.dma_start(svt6[:, 0, :], ys_d).then_inc(s_ysl, 16)
            sp.wait_ge(full, place[("WT", 3)] + 1)
            for t in range(TILES):
                sp.dma_start(x[:, t, :], A["x_prompt"][0, t * P:(t + 1) * P, :]).then_inc(s_xr[t], 16)
            sp.dma_start(x[0:NS, 4, :], A["x_sample"][:, 0, :]).then_inc(s_xr[4], 16)
            done(sp, ("wkvT",))
            for kv, dst in (("k", Kc), ("v", Vc)):
                sp.dma_start(dst[0:P - 1, :, :], A[f"cache_swa_{kv}"][0, :, 1:P].rearrange("b p h d -> p b (h d)")) \
                    .then_inc(s_cache, 16)
            sp.dma_start(O["prompt_wkv"][0, 0].rearrange("h i j -> i h j"),
                         wkvO.rearrange("i (h j) -> i h j", h=H)).then_inc(s_wkvo, 16)
            done(sp, ("ysT",))
            for i in range(n_early, n_early + 2):
                key, s, src, k = loads[i]
                if i == n_early + 1:
                    sp.wait_ge(s_wkvo, 16)
                sp.dma_start(weights(key, k), src).then_inc(s_w[s], 16)
            done(sp, ("kvout",))
            sp.dma_start(O["prompt_swa_k"][0, 0].rearrange("p h d -> p (h d)"), kvO[:, 0:P]).then_inc(s_kvw, 16)
            sp.dma_start(O["prompt_swa_v"][0, 0].rearrange("p h d -> p (h d)"), vtok[:, 3, :]).then_inc(s_kvw, 16)
            for i, kv in enumerate("kv"):
                sp.dma_start(O[f"sample_swa_{kv}"][0, :, P - 1].rearrange("b h d -> b (h d)"),
                             kvO[0:NS, (1 + i) * P:(2 + i) * P]).then_inc(s_newkv, 16)
            sp.wait_ge(s_newkv, 32)
            for kv, dst in (("k", Kc), ("v", Vc)):
                sp.dma_start(dst[P - 1:P, :, :],
                             O[f"sample_swa_{kv}"][0:1, :, P - 1].rearrange("a b h d -> a b (h d)")) \
                    .then_inc(s_cache, 16)
            def memory_load(kv, b, dst, signal):
                src = A[f"cache_mem_{kv}"][0, b]
                sp.dma_start(dst, src.rearrange("(a p) h d -> p a (h d)", p=P)).then_inc(signal, 16)

            sp.wait_ge(s_fin, 1)
            for b in range(4):
                memory_load("k", b, kv_ring[b], s_kvr[b])
            for i in range(n_early + 2, n_early + 4):
                key, s, src, k = loads[i]
                sp.wait_ge(full, place[("wo", 4, 1)] + 1)
                sp.dma_start(weights(key, k), src).then_inc(s_w[s], 16)
            sp.wait_ge(full, place[("q", 3, 1)] + 1)
            for b in range(4, NS):
                if b == 6:
                    for m in range(4, NS):
                        memory_load("v", m, late[m - 4], s_late)
                sp.wait_ge(full, place[("ckT", b - 4, 1)] + 1)
                memory_load("k", b, kv_ring[b % 4], s_kvr[b % 4])
            for b in range(4):
                sp.wait_ge(full, place[("ckT", b + 4, 1)] + 1)
                memory_load("v", b, kv_ring[b], s_kvr[b])
            sp.dma_start(wrG, A["w_group_router"][0].rearrange("(p k) n -> p k n", k=KD)).then_inc(s_rw, 16)
            sp.dma_start(wrE, A["w_expert_router"][0].rearrange("(p k) n -> p k n", k=KD)).then_inc(s_rw, 16)
            b1, b2, b3 = A["b_group_router"], A["b_expert_router"], A["norm_final"]
            sp.dma_start(rbias[:, 0:4], bass.AP(b1.tensor, b1.offset, [[0, P], [1, 4]])).then_inc(s_rw, 16)
            sp.dma_start(rbias[:, 4:36], bass.AP(b2.tensor, b2.offset, [[0, P], [1, NE]])).then_inc(s_rw, 16)
            sp.dma_start(gfin, bass.AP(b3.tensor, b3.offset, [[0, P], [1, D]])).then_inc(s_rw, 16)
            wge = A["w_exp_gate"][0].rearrange("g e (p k) f -> (g e) p (k f)", k=KD)
            wue = A["w_exp_up"][0].rearrange("g e (p k) f -> (g e) p (k f)", k=KD)
            wde = A["w_exp_down"][0].rearrange("g e f d -> (g e) f d")

            def load_expert(i, e, gu, dn):
                sp.dma_start(we[i][:, 0, :], wge[bass.ds(e, 1)].rearrange("a p n -> (a p) n")).then_inc(gu, 16)
                sp.dma_start(we[i][:, 1, :], wue[bass.ds(e, 1)].rearrange("a p n -> (a p) n")).then_inc(gu, 16)
                sp.dma_start(we[i][:, 2, :], wde[bass.ds(e, 1)].rearrange("a p n -> (a p) n")).then_inc(dn, 16)

            for t in range(T5):
                R = tile_rows(t)
                sp.wait_ge(s_xn2, 6 + t)
                sp.dma_start(hn_d[t * P:t * P + R, :], xn[t % 2][0:R, :]).then_inc(s_hn[t % 2], 16)
            sp.wait_ge(s_init, 1)
            sp.dma_start(slot_d.rearrange("(b p) a -> b (p a)", p=BS), slot_rows[0:NBLK, :]).then_inc(s_sinit, 16)
            sp.wait_ge(full, place[("wc", 4, 1)] + 1)
            for i in range(6):
                load_expert(i, i, s_wgu[i], s_wd[i])
            sp.wait_ge(s_hn[0], 48)
            sp.wait_ge(s_hn[1], 32)
            sp.wait_ge(full, place[("xT3", 4, 1)] + 1)
            for i in range(6, 8):
                load_expert(i, i, s_wgu[i], s_wd[i])
            sp.wait_ge(s_scat, 16 * 2 * T5)
            sp.dma_start(slot_rows[0:NBLK, :], slot_d.rearrange("(b p) a -> b (p a)", p=BS)).then_inc(s_srow, 16)
            with sp.Fori(1, NE // NW) as it:
                for i in range(NW):
                    sp.wait_ge(s_pY, it * NW + (i + 1 - NW))
                    sp.wait_ge(s_eid, 1)
                    load_expert(i, it * NW + i, s_wgu[i], s_wd[i])
            for i in range(NB3):
                sp.wait_ge(s_ys[i], 16 * (NE // NB3))
            sp.wait_ge(s_pY, NE)
            beyond = sp.value_load(eidI[0:1, OVER:OVER + 1], min_val=0, max_val=OVER)
            with sp.If(beyond > 0):
                with sp.Fori(0, OVER) as n:
                    sp.wait_ge(s_free, n + 1)
                    sp.wait_ge(s_eid, 1)
                    e = sp.value_load(eidI[0:1, bass.ds(n, 1)], min_val=0, max_val=NE - 1)
                    load_expert(0, e, s_ow, s_ow)
                sp.wait_ge(s_free, OVER + 1)
            with sp.Else():
                sp.wait_ge(s_pY, NE)
            prow_d = pair_d.rearrange("(t j) d -> t j d", j=2)
            for t in range(T5):
                R = tile_rows(t)
                if t >= 2:
                    sp.wait_ge(s_comb, t - 1)
                sp.dma_start(ydt[t % 2][0:R, :, :], prow_d[t * P:t * P + R]).then_inc(s_yl[t % 2], 16)
            for t in range(T5):
                R = tile_rows(t)
                sp.wait_ge(s_res, t + 1)
                dst = O["y_prompt"][0, t * P:(t + 1) * P, :] if t < TILES else O["y_sample"][:, 0, :]
                sp.dma_start(dst, x[0:R, t, :]).then_inc(s_out, 16)
            sp.wait_ge(s_out, 16 * (2 + T5))

        @block.gpsimd
        def _(pool):
            pool.wait_ge(s_inv, 1)
            pool.wait_ge(s_prep, 4)
            pool.wait_ge(full, place[("proj", 19, 1)] + 1)
            for n in range(NCH):
                cols = slice(n * CH, (n + 1) * CH)
                inv = small[:, 8:40].rearrange("p (c n) -> p c n", c=4)[:, :, n:n + 1].to_broadcast([P, 4, CH])
                pool.tensor_tensor(Bt[:, :, cols], B1[:, :, cols], inv, ALU.mult).then_inc(s_tilde, 1)
                pool.tensor_tensor(Kt[:, :, cols], PR[:, 4:8, 1 + n * CH:1 + (n + 1) * CH], inv, ALU.mult) \
                    .then_inc(s_tilde, 1)
            pool.wait_ge(s_sinit, 16)
            pool.wait_ge(s_slot, 1)
            pool.wait_ge(s_const, 64)
            for t in range(T5):
                for j in range(2):
                    pool.indirect_dma_start(slot_d, bass.IndirectOffsetOnAxis(slI[j][:, t:t + 1].bitcast(U32), 0),
                                            pair_no[:, t, j:j + 1], None, bounds_check=NBLK * BS - 1,
                                            oob_is_err=False).then_inc(s_scat, 16)
            pool.wait_ge(s_idx, 1)
            for i in range(2):
                pool.wait_ge(s_hn[i], 16 * (3 - i))

            def wait(sem, value):
                pool.wait_ge(sem, value)
                pool.wait_ge(s_idx, 1)

            def carried(sem, value, cell=0):
                pool.wait_ge(sem, value)
                return pool.tensor_tensor(scrap[:, cell:cell + 1], scrap[:, 1:2], scrap[:, 1:2], ALU.add)

            def index_in(value):
                carried(s_idc, value)

            pool.memset(scrap, 0.0)

            def gather(i, b):
                pool.tensor_copy(idg[i], tokI[0:BS, bass.ds(b, 1)]).then_inc(s_idc, 1)

            def scatter_index(i, b):
                pool.tensor_copy(ids[i], pidI[0:BS, bass.ds(b, 1)]).then_inc(s_idc, 1)

            def start_gather(i, signal=None):
                pool.indirect_dma_start(xg[i][0:BS], None, hn_d, bass.IndirectOffsetOnAxis(idg[i].bitcast(U32), 0),
                                        bounds_check=NT - 1, oob_is_err=False).then_inc(signal or s_gx[i], 16)

            def start_scatter(i):
                pool.indirect_dma_start(pair_d, bass.IndirectOffsetOnAxis(ids[i].bitcast(U32), 0), yb[i], None,
                                        bounds_check=PAIRS_E - 1, oob_is_err=False).then_inc(s_ys[i], 16)

            for i in range(NB3):
                gather(i, i)
                pool.wait_ge(s_idc, i + 1)
                start_gather(i)
            with pool.Fori(1, NE // NB3) as it:
                for i in range(NB3):
                    wait(s_pX, it * NB3 + (i + 1 - NB3))
                    wait(s_gx[i], it * 16)
                    gather(i, it * NB3 + i)
                    index_in(it * (2 * NB3) + (2 * i + 1 - NB3))
                    start_gather(i)
                    wait(s_vy, it * NB3 + (i + 1 - NB3))
                    wait(s_ay, it * NB3 + (i + 1 - NB3))
                    scatter_index(i, it * NB3 + (i - NB3))
                    index_in(it * (2 * NB3) + (2 * i + 2 - NB3))
                    start_scatter(i)
            last = NE // NB3 - 1
            for i in range(NB3):
                pool.wait_ge(s_vy, NB3 * last + i + 1)
                pool.wait_ge(s_ay, NB3 * last + i + 1)
                pool.wait_ge(s_ys[i], 16 * last)
                scatter_index(i, NB3 * last + i)
                pool.wait_ge(s_idc, 2 * NB3 * last + NB3 + i + 1)
                start_scatter(i)
            pool.wait_ge(s_ys[0], 16 * (NE // NB3))
            pool.wait_ge(s_pX, NE)
            beyond = pool.value_load(eidI[0:1, OVER:OVER + 1], min_val=0, max_val=OVER)
            with pool.If(beyond > 0):
                pool.memset(scrap, 0.0).then_inc(s_free, 1)
                with pool.Fori(0, OVER) as n:
                    wait(s_free, n + 1)
                    pool.tensor_copy(idg[0], tokI[0:BS, bass.ds(n + NE, 1)]).then_inc(s_idc, 1)
                    pool.tensor_copy(ids[0], pidI[0:BS, bass.ds(n + NE, 1)]).then_inc(s_idc, 1)
                    index_in(n * 2 + (2 * NE + 2))
                    start_gather(0, s_ogx)
                    carried(s_oV, n * 3 + 3, 2)
                    carried(s_oA, n * 3 + 3, 3)
                    pool.indirect_dma_start(pair_d, bass.IndirectOffsetOnAxis(ids[0].bitcast(U32), 0), yb[0], None,
                                            bounds_check=PAIRS_E - 1, oob_is_err=False).then_inc(s_osc, 16)
                    carried(s_osc, n * 16 + 16, 4).then_inc(s_free, 1)
            with pool.Else():
                pool.memset(scrap, 0.0)

        @block.tensor
        def _(pe):
            last = [None]

            def mm(out, lhsT, rhs, start=True, stop=True):
                last[0] = pe.matmul(out, lhsT, rhs, start=start, stop=stop, skip_group_check=True)

            def tr(out, in_):
                n = in_.shape[0]
                last[0] = pe.transpose(out, in_, ident[0:n, 0:n])

            def close():
                last[0].then_inc(full, 1)

            pe.wait_ge(s_par, 16 * 14)
            o = reuse(pe, ("par",))
            tr(o[:, 0:42], prow[0:42, :])
            close()
            o = reuse(pe, ("shift_in",))
            for j in range(RW):
                tr(o[:, NS * j:NS * j + NS], srow[0:NS, j * P:(j + 1) * P])
            close()
            for t in range(TILES + 1):
                R = tile_rows(t)
                pe.wait_ge(s_xn, t + 1)
                for i in range(2):
                    o = reuse(pe, ("xT", t, i))
                    xk = x[0:R, t, :].rearrange("p (q k) -> p k q", k=KD)
                    for k in range(4):
                        tr(o[:, k * P:k * P + R], xk[:, 4 * i + k, :])
                    close()

            def project(j):
                grp = j // 4
                key = ("w_in", grp)
                weights_in(pe, key)
                w = weights(key)
                for s in range(2):
                    o = reuse(pe, ("proj", j, s))
                    for k in range(KD):
                        mm(o[:, 0:HALF], w[:, k, (j % 4) * P:(j % 4 + 1) * P], hA[:, k, s * HALF:(s + 1) * HALF],
                           k == 0, k == KD - 1)
                    close()

            def memory_rows_T():
                for t in range(2):
                    pe.wait_ge(s_xn, 6 + t)
                    for i in range(2):
                        o = reuse(pe, ("mT", t, i))
                        xk = memX[:, t, :].rearrange("p (q k) -> p k q", k=KD)
                        for k in range(4):
                            tr(o[:, k * P:(k + 1) * P], xk[:, 4 * i + k, :])
                        close()

            def lora_products():
                pe.wait_ge(s_const, 64)
                pe.wait_ge(s_act, 1)
                for key, b in (("lora_w", 0), ("lora_a", 64)):
                    for c in range(4):
                        for s in range(2):
                            o = reuse(pe, (key, c, s))
                            mm(o[:, 0:HALF], lora[b:b + 64, c * P:(c + 1) * P],
                               PR[b:b + 64, 12, 1 + s * HALF:1 + (s + 1) * HALF])
                            close()

            def memory_products():
                done(pe, ("mT", 1, 1))
                for key, wk in (("mk", ("w_ck",)), ("mv", ("w_cv",))):
                    weights_in(pe, wk)
                    for t in range(2):
                        o = reuse(pe, (key, t))
                        for k in range(KD):
                            mm(o[:, :], memT[:, k, t * P:(t + 1) * P], weights(wk)[:, k, :], k == 0, k == KD - 1)
                        close()
                for t in range(2):
                    done(pe, ("mk", t))
                    o = reuse(pe, ("mkT", t))
                    for h in range(XH):
                        tr(o[:, h * P:(h + 1) * P], mkS[:, t, h * P:(h + 1) * P])
                    close()

            def head_sums(c):
                pe.wait_ge(s_kk, c + 1)
                for s in range(2):
                    o = reuse(pe, ("norm_k", c, s))
                    mm(o[:, 0:HALF], bones, sq[c % 2][:, s * HALF:(s + 1) * HALF])
                    close()
                pe.wait_ge(s_rk, c + 1)
                for s in range(2):
                    o = reuse(pe, ("bonus", c, s))
                    mm(o[:, 0:HALF], bones, B1[:, c, s * HALF:(s + 1) * HALF])
                    close()

            done(pe, ("xT", 4, 1))
            for what, n in FRONT_ORDER:
                if what == "proj":
                    project(n)
                elif what == "mT":
                    memory_rows_T()
                elif what == "lora":
                    lora_products()
                elif what == "mem":
                    memory_products()
                elif what == "sums":
                    head_sums(n)
            pe.wait_ge(s_mix, 14)
            for i in range(4):
                o = reuse(pe, ("shift_out", i))
                for j in range(4 * i, min(4 * i + 4, RW)):
                    tr(o[0:9, (j % 4) * P:(j % 4 + 1) * P], saved[:, j, :])
                close()
            pe.wait_ge(s_prep, 4)
            pe.wait_ge(s_prep, 4)
            for i in range(6):
                o = reuse(pe, ("svec", i))
                for c in range(4):
                    src = (B0[:, c, SEQ:NT], B1[:, c, SEQ:NT], PR[:, 4 + c, 1 + SEQ:1 + NT], wS[:, c, :],
                           PR[:, c, 1 + SEQ:1 + NT], PR[:, 8 + c, 1 + SEQ:1 + NT])[i]
                    tr(o[0:NS, c * P:(c + 1) * P], src)
                close()
            for t in range(TILES):
                o = reuse(pe, ("tokV", t))
                for c in range(4):
                    tr(o[:, c * P:(c + 1) * P], PR[:, 8 + c, 1 + t * P:1 + (t + 1) * P])
                close()
            for t in range(TILES):
                lo, hi = t * P, (t + 1) * P
                for i, src in enumerate((B0, B1, PR[:, 4:8, :])):
                    o = reuse(pe, ("tok", t, i))
                    off = 1 if i == 2 else 0
                    for c in range(4):
                        tr(o[:, c * P:(c + 1) * P], src[:, c, off + lo:off + hi])
                    close()
                pe.wait_ge(s_tilde, 4 * (t + 1))
                for h in range(H):
                    c, b = h // 2, 64 * (h % 2)
                    o = reuse(pe, ("AB", t, h))
                    for i, src in enumerate((Bt, Kt)):
                        mm(o[:, i * 256:i * 256 + P], src[b:b + 64, c, lo:hi], B0[b:b + 64, c, lo:hi])
                        mm(o[:, i * 256 + P:i * 256 + 256], src[b:b + 64, c, lo:hi], PR[b:b + 64, c, 1 + lo:1 + hi])
                    close()
                for q in range(2):
                    o = reuse(pe, ("N0", t, q))
                    for h in range(4 * q, 4 * q + 4):
                        done(pe, ("AB", t, h))
                        tr(o[:, (h % 4) * P:(h % 4 + 1) * P], AB[:, h, 0, :])
                    close()

                def M(h, k):
                    return AB[:, h, 0, :] if k == 0 else Mi[k % 2][:, h, :]

                for k in range(6):
                    for q in range(2):
                        hs = range(4 * q, 4 * q + 4)
                        if k == 0:
                            done(pe, ("N0", t, q))
                        else:
                            done(pe, ("NN", t, q, k - 1))
                            if k < 5:
                                done(pe, ("MM", t, q, k - 1))
                            if k == 1:
                                pe.wait_ge(s_st, 2 * t + q + 1)
                            else:
                                done(pe, ("XM", t, q, k - 1))
                            o = reuse(pe, ("XM", t, q, k))
                            for h in hs:
                                mm(o[:, (h % 4) * P:(h % 4 + 1) * P], Ni[k % 2][:, h, :], Xi[:, h, :])
                            close()
                        if k < 4:
                            o = reuse(pe, ("MM", t, q, k))
                            for h in hs:
                                mm(o[:, (h % 4) * P:(h % 4 + 1) * P], Ni[k % 2][:, h, :], M(h, k))
                            close()
                        if k < 5:
                            o = reuse(pe, ("NN", t, q, k))
                            for h in hs:
                                mm(o[:, (h % 4) * P:(h % 4 + 1) * P], M(h, k), Ni[k % 2][:, h, :])
                            close()
                o = reuse(pe, ("akv", t))
                done(pe, ("tokV", t))
                for h in range(H):
                    mm(o[:, h * HD:(h + 1) * HD], AB[:, h, 2, :], tokV[:, t, h * HD:(h + 1) * HD])
                close()
                done(pe, ("akv", t))
                done(pe, ("XM", t, 1, 5))
                o = reuse(pe, ("G", t))
                for h in range(H):
                    mm(o[:, h * HD:(h + 1) * HD], Xi[:, h, :], akv[:, h * HD:(h + 1) * HD])
                close()
                o = reuse(pe, ("WT", t))
                done(pe, ("tok", t, 0))
                for h in range(H):
                    c, b = h // 2, 64 * (h % 2)
                    mm(o[b:b + 64, c * P:(c + 1) * P], tokX[:, 0, h * HD:(h + 1) * HD], Xi[:, h, :])
                close()
                done(pe, ("WT", t))
                done(pe, ("tok", t, 2))
                for u in range(2):
                    tk = 64 * u
                    n = 2 * t + u
                    if n == 0:
                        pe.wait_ge(s_vz, 1)
                    elif u == 0:
                        done(pe, ("S", t - 1, 1))
                    else:
                        done(pe, ("S", t, 0))
                    for e in range(2):
                        o = reuse(pe, ("U", t, u, e))
                        b = 64 * e
                        for c in range(4):
                            mm(o[tk:tk + 64, c * HD:(c + 1) * HD], WT[b:b + 64, c, tk:tk + 64],
                               ST[b:b + 64, n, c, :])
                        close()
                    done(pe, ("U", t, u, 1))
                    o = reuse(pe, ("S", t, u))
                    for h in range(H):
                        c, b = h // 2, 64 * (h % 2)
                        hc = slice(h * HD, (h + 1) * HD)
                        mm(o[b:b + 64, c * HD:(c + 1) * HD], tokX[tk:tk + 64, 2, hc], tokV[tk:tk + 64, t, hc],
                           True, False)
                        mm(o[b:b + 64, c * HD:(c + 1) * HD], tokX[tk:tk + 64, 1, hc], Ut[tk:tk + 64, hc], False, True)
                    close()
                o = reuse(pe, ("Y", t))
                for h in range(H):
                    c, b = h // 2, 64 * (h % 2)
                    hc = slice(h * HD, (h + 1) * HD)
                    yo = o[b:b + 64, c * P:(c + 1) * P]
                    mm(yo, tokV[:, t, hc], AB[:, h, 3, :], c == 0, False)
                    mm(yo, Ut[:, hc], AB[:, h, 1, :], False, False)
                    for u in range(2):
                        mm(o[b:b + 64, c * P + 64 * u:c * P + 64 * u + 64], ST[b:b + 64, 2 * t + u, c, :],
                           PR[b:b + 64, c, 1 + lo + 64 * u:1 + lo + 64 * u + 64], False, True)
                close()
            o = reuse(pe, ("wkvT",))
            done(pe, ("S", 3, 1))
            for c in range(4):
                tr(o[0:64, c * P:(c + 1) * P], ST[:, 8, c, :])
            close()
            pe.wait_ge(s_ysl, 16)
            o = reuse(pe, ("ysT",))
            for c in range(4):
                tr(o[:, c * NS:(c + 1) * NS], svt6[:, 0, c * P:(c + 1) * P])
            close()
            done(pe, ("ysT",))
            done(pe, ("Y", 3))
            for c in range(4):
                for s in range(2):
                    o = reuse(pe, ("mean", c, s))
                    mm(o[:, 0:HALF], bones, yT[:, c, s * HALF:(s + 1) * HALF])
                    close()
            for c in range(4):
                pe.wait_ge(s_yc, c + 1)
                for s in range(2):
                    o = reuse(pe, ("var", c, s))
                    mm(o[:, 0:HALF], bones, B0[:, c, s * HALF:(s + 1) * HALF])
                    close()
            for c in range(4):
                for s in range(2):
                    o = reuse(pe, ("gate", c, s))
                    mm(o[:, 0:HALF], gup[:, c * P:(c + 1) * P], PR[:, 13, 1 + s * HALF:1 + (s + 1) * HALF])
                    close()
            for s in range(2):
                cols = slice(s * HALF, (s + 1) * HALF)
                for i in range(2):
                    o = reuse(pe, ("rka", i, s))
                    mm(o[:, 0:HALF], sel[:, 1 + i, :], SQ[:, 4, cols])
                    close()
                    o = reuse(pe, ("rkb", i, s))
                    mm(o[:, 0:HALF], sel[:, 3 + i, :], SQ[:, 4, cols])
                    close()
                for c in range(4):
                    o = reuse(pe, ("rq", c, s))
                    mm(o[:, 0:HALF], sel[:, 0, :], SQ[:, c, cols])
                    close()
            o = reuse(pe, ("vtok",))
            for t in range(TILES):
                tr(o[:, t * P:(t + 1) * P], SQ[:, 5, t * P:(t + 1) * P])
            close()
            pe.wait_ge(s_rope, 1)
            o = reuse(pe, ("kvout",))
            for i in range(2):
                tr(o[:, i * HD:(i + 1) * HD], RK[i][0:HD, 3 * P:4 * P])
                tr(o[0:NS, P + i * HD:P + (i + 1) * HD], RK[i][0:HD, SEQ:NT])
            tr(o[0:NS, 2 * P:3 * P], SQ[:, 5, SEQ:NT])
            close()
            done(pe, ("vtok",))

            def window_scores(t):
                k0 = max(t - 1, 0) * P
                W = (t + 1) * P - k0
                for e in range(2):
                    b = 64 * e
                    for i in range(2):
                        o = reuse(pe, ("s", t, e, i))
                        for n in range(2):
                            mm(o[:, n * W:(n + 1) * W], SQ[b:b + 64, 2 * i + n, t * P:(t + 1) * P],
                               RK[i][b:b + 64, k0:k0 + W])
                        close()

            window_scores(0)
            for t in range(TILES):
                if t < TILES - 1:
                    window_scores(t + 1)
                pe.wait_ge(s_prob, t + 1)
                na = 1 if t == 0 else 2
                sm = Sm[t % 2].rearrange("p (h s) -> p h s", h=H)
                for i in range(4):
                    o = reuse(pe, ("pT", t, i))
                    for n in range(2):
                        for a in range(na):
                            tr(o[:, (2 * n + a) * P:(2 * n + a + 1) * P], sm[:, 2 * i + n, a * P:(a + 1) * P])
                    close()
                done(pe, ("pT", t, 3))
                o = reuse(pe, ("o", t))
                for h in range(H):
                    c, b, g = h // 2, 64 * (h % 2), h // 4
                    for a in range(na):
                        mm(o[b:b + 64, c * P:(c + 1) * P], vtok[:, t + 1 - na + a, g * HD:(g + 1) * HD],
                           PTa[:, h, a, :], a == 0, a == na - 1)
                close()
            pe.wait_ge(s_cache, 64)
            for e in range(2):
                o = reuse(pe, ("qd", e))
                mm(o[:, 0:32].rearrange("p (c b) -> p c b", c=4), sel[:, 1 + e, :], SQ[:, 0:4, SEQ:NT])
                close()
            for i in range(2):
                o = reuse(pe, ("kT", i))
                for m in range(4):
                    tr(o[:, m * P:(m + 1) * P], Kc[:, 4 * i + m, :])
                close()
            done(pe, ("kT", 1))
            done(pe, ("qd", 1))
            for g in range(2):
                o = reuse(pe, ("ss", g))
                for b in range(NS):
                    mm(o[:, 4 * b:4 * b + 4], kTs[64 * g:64 * g + 64, b, :],
                       QD[64 * g:64 * g + 64, b, 2 * g:2 * g + 2, :].rearrange("p c e -> p (c e)"))
                close()
            done(pe, ("ss", 1))
            o = reuse(pe, ("ssT",))
            tr(o[0:64, 0:P], sT)
            close()
            pe.wait_ge(s_prob, 5)
            o = reuse(pe, ("spT",))
            tr(o[:, 0:64], Sm[0][0:64, 0:P])
            close()
            done(pe, ("spT",))
            o = reuse(pe, ("so",))
            for e in range(2):
                for b in range(NS):
                    for g in range(2):
                        mm(o[64 * e:64 * e + 64, 0:32].rearrange("p (c b) -> p c b", c=4)[:, 2 * g:2 * g + 2, b],
                           Vc[:, b, g * HD:(g + 1) * HD],
                           pTs.rearrange("p (b g n e) -> p b g n e", b=NS, g=2, n=2)[:, b, g, :, e])
                close() if e else None
            done(pe, ("so",))
            pe.wait_ge(s_fin, 1)
            for i in range(2):
                weights_in(pe, ("wo", i))
            for t in range(TILES + 1):
                R = tile_rows(t)
                for n in range(2):
                    o = reuse(pe, ("wo", t, n))
                    for c in range(8):
                        mm(o[0:R, :], yT[:, c, t * P:t * P + R],
                           weights(("wo", c // 4), 4)[:, c % 4, n * 512:(n + 1) * 512], c == 0, c == 7)
                    close()

            def transpose_rows(key, first):
                for t in range(TILES + 1):
                    R = tile_rows(t)
                    pe.wait_ge(s_xn2, first + t + 1)
                    for i in range(2):
                        o = reuse(pe, (key, t, i))
                        xk = xn[t % 2][0:R, :].rearrange("p (q k) -> p k q", k=KD)
                        for k in range(4):
                            tr(o[:, k * P:k * P + R], xk[:, 4 * i + k, :])
                        close()

            transpose_rows("xT2", 0)
            weights_in(pe, ("w_cq",))
            done(pe, ("xT2", 4, 1))
            for h in range(XH):
                for s in range(2):
                    o = reuse(pe, ("q", h, s))
                    for k in range(KD):
                        mm(o[:, 0:HALF], weights(("w_cq",))[:, k, h * P:(h + 1) * P],
                           hA[:, k, s * HALF:(s + 1) * HALF], k == 0, k == KD - 1)
                    close()
            done(pe, ("q", 3, 1))

            def prompt_scores(t):
                for i in range(2):
                    o = reuse(pe, ("xs", t, i))
                    for n in range(2):
                        mm(o[:, n * MT:(n + 1) * MT], qT[:, 2 * i + n, t * P:(t + 1) * P], mkT[:, 2 * i + n, :])
                    close()

            def prompt_values(t):
                pe.wait_ge(s_prob, 6 + t)
                sm = Sm[(5 + t) % 2][:, 0:1024].rearrange("p (h s) -> p h s", h=XH)
                for i in range(2):
                    o = reuse(pe, ("xpT", t, i))
                    for n in range(2):
                        for a in range(2):
                            tr(o[:, (2 * n + a) * P:(2 * n + a + 1) * P], sm[:, 2 * i + n, a * P:(a + 1) * P])
                    close()
                done(pe, ("xpT", t, 1))
                o = reuse(pe, ("xo", t))
                for h in range(XH):
                    for a in range(2):
                        mm(o[:, h * P:(h + 1) * P], mv[:, a, h * P:(h + 1) * P], PTc[:, h, a, :], a == 0, a == 1)
                close()

            def keys_T(b):
                pe.wait_ge(s_kvr[b % 4], 16 * (b // 4 + 1))
                for st in range(2):
                    o = reuse(pe, ("ckT", b, st))
                    for h in range(XH):
                        tr(o[:, h * P:(h + 1) * P], kv_ring[b % 4][:, st, h * P:(h + 1) * P])
                    close()

            def sample_scores(b):
                done(pe, ("ckT", b, 1))
                o = reuse(pe, ("cs", b))
                for st in range(2):
                    for h in range(XH):
                        mm(o[:, 4 * st + h:4 * st + h + 1], KT[b % 2][:, h, st, :], qT[:, h, SEQ + b:SEQ + b + 1])
                close()

            for what, n in CROSS_ORDER:
                {"xs": prompt_scores, "xp": prompt_values, "ckT": keys_T, "cs": sample_scores}[what](n)
            done(pe, ("cs", 7))
            o = reuse(pe, ("csT",))
            for st in range(2):
                tr(o[0:32, st * P:(st + 1) * P], csS[:, st, :])
            close()
            pe.wait_ge(s_prob, 10)
            o = reuse(pe, ("cpT",))
            for st in range(2):
                tr(o[:, st * 32:(st + 1) * 32], Sm[1][0:32, st * P:(st + 1) * P])
            close()
            done(pe, ("cpT",))
            o = reuse(pe, ("co",))
            for b in range(NS):
                if b < 4:
                    pe.wait_ge(s_kvr[b], 48)
                elif b == 4:
                    pe.wait_ge(s_late, 64)
                for h in range(XH):
                    for st in range(2):
                        mm(o[:, 4 * b + h:4 * b + h + 1], values_of(b)[:, st, h * P:(h + 1) * P],
                           cpS[:, st, 4 * b + h:4 * b + h + 1], st == 0, st == 1)
            close()
            done(pe, ("co",))
            done(pe, ("xo", 3))
            weights_in(pe, ("w_co",))
            for t in range(TILES + 1):
                R = tile_rows(t)
                for n in range(2):
                    o = reuse(pe, ("wc", t, n))
                    for h in range(XH):
                        mm(o[0:R, :], yT[:, h, t * P:t * P + R], weights(("w_co",), 4)[:, h, n * 512:(n + 1) * 512],
                           h == 0, h == XH - 1)
                    close()
            transpose_rows("xT3", 5)
            done(pe, ("xT3", 4, 1))
            pe.wait_ge(s_rw, 16 * 5)
            for t in range(T5):
                R = tile_rows(t)
                o = reuse(pe, ("route", t))
                for w, lo, n in ((wrG, 0, 4), (wrE, 4, NE)):
                    for k in range(KD):
                        mm(o[0:R, lo:lo + n], hA[:, k, t * P:t * P + R], w[:, k, :], k == 0, k == KD - 1)
                close()
            pe.wait_ge(s_mk, 1)
            o = reuse(pe, ("ranks",))
            for t in range(T5 + 1):
                lhs = [(onesm, u) for u in range(min(t, T5))] + ([(tri, t)] if t < T5 else [])
                for n, (m, u) in enumerate(lhs):
                    mm(o[:, t * NE:(t + 1) * NE], m, Mk[:, u, :], n == 0, n == len(lhs) - 1)
            close()
            pe.wait_ge(s_srow, 16)
            o = reuse(pe, ("slots",))
            tr(o[0:BS, 0:NBLK], slot_rows[0:NBLK, :])
            close()
            done(pe, ("slots",))
            bX, bG, bA = banks[0], [banks[2], banks[6]], banks[3]
            bY = [banks[4], banks[5]]

            def rows_T(i, b, r):
                pe.wait_ge(s_gx[i % NB3], r * 32 + (i // NB3 * 16 + 16))
                if b is not None:
                    pe.wait_ge(s_vx, b)
                transposes(i % NB3).then_inc(s_pX, 1)

            def transposes(i):
                xk = xg[i].rearrange("p (q k) -> p k q", k=KD)
                for k in range(KD):
                    n = P if k == 0 else BS
                    ins = pe.transpose(bX[:, k * BS:k * BS + n], xk[0:n, k, :], ident[0:n, 0:n])
                return ins

            def gate_up_products(i):
                for k in range(KD):
                    ins = pe.matmul(bG[i % 2][0:BS, 0:2 * FH].rearrange("p (a f) -> p a f", a=2), xTe[i % 2][:, k, :],
                                    we[i][:, 0:2, k * FH:(k + 1) * FH], start=k == 0, stop=k == KD - 1)
                return ins

            def down_products(i):
                for n in range(2):
                    ins = pe.matmul(bY[n][0:BS, :], actT, we[i][:, 2, n * 512:(n + 1) * 512], start=True, stop=True)
                return ins

            def gate_up(i, b, r):
                pe.wait_ge(s_wgu[i], r * 32 + 32)
                pe.wait_ge(s_vx, b + 1)
                gate_up_products(i).then_inc(s_pG, 1)

            def act_T(b):
                pe.wait_ge(s_vm, b + 1)
                pe.transpose(bA[:, 0:P], act_f, ident).then_inc(s_pA, 1)

            def down(i, b, r, first=False):
                pe.wait_ge(s_aa, b + 1)
                pe.wait_ge(s_wd[i], r * 16 + 16)
                if not first:
                    pe.wait_ge(s_vy, b)
                    pe.wait_ge(s_ay, b)
                down_products(i).then_inc(s_pY, 1)

            rows_T(0, None, 0)
            rows_T(1, 1, 0)
            gate_up(0, 0, 0)
            rounds = NE // NW

            def pe_round(it, first, final):
                for i in range(NW):
                    b = it * NW + i
                    if not (final and i == NW - 1):
                        gate_up((i + 1) % NW, b + 1, it if i < NW - 1 else it + 1)
                    act_T(b)
                    if not (final and i >= NW - 2):
                        rows_T((i + 2) % NW, b + 2, it if i < NW - 2 else it + 1)
                    down(i, b, it, first and i == 0)

            pe_round(0, True, False)
            with pe.Fori(1, rounds - 1) as it:
                pe_round(it, False, False)
            pe_round(rounds - 1, False, True)
            pe.wait_ge(s_vx, NE)
            pe.wait_ge(s_vy, NE)
            pe.wait_ge(s_ay, NE)
            beyond = pe.value_load(eidI[0:1, OVER:OVER + 1], min_val=0, max_val=OVER)
            with pe.If(beyond > 0):
                with pe.Fori(0, OVER) as n:
                    pe.wait_ge(s_ogx, n * 16 + 16)
                    transposes(0).then_inc(s_oP, 1)
                    pe.wait_ge(s_oV, n * 3 + 1)
                    pe.wait_ge(s_ow, n * 48 + 48)
                    gate_up_products(0).then_inc(s_oP, 1)
                    pe.wait_ge(s_oV, n * 3 + 2)
                    pe.transpose(bA[:, 0:P], act_f, ident).then_inc(s_oP, 1)
                    pe.wait_ge(s_oA, n * 3 + 2)
                    down_products(0).then_inc(s_oP, 1)
            with pe.Else():
                pe.wait_ge(s_vx, NE)

        @block.scalar
        def _(act):
            chain = [0]

            def link(ins):
                chain[0] += 1
                ins.then_inc(a_ch, 1)
                act.wait_ge(a_ch, chain[0])

            act.wait_ge(s_eps, 1)
            for t in range(TILES + 1):
                R = tile_rows(t)
                act.wait_ge(s_x[t], 16)
                ms = small[0:R, t:t + 1]
                link(act.activation(junk[0:R, :], x[0:R, t, :], ACT.Square, accum_out=ms))
                act.activation(ms, ms, ACT.Sqrt, scale=1.0 / D, bias=small[0:R, 41:42]).then_inc(s_sq, 1)
            act.wait_ge(s_mem, 16)
            for t in range(2):
                ms = small[:, 5 + t:6 + t]
                link(act.activation(junk, memX[:, t, :], ACT.Square, accum_out=ms))
                act.activation(ms, ms, ACT.Sqrt, scale=1.0 / D, bias=small[:, 41:42]).then_inc(s_sq, 1)
            def from_psum(keys, write):
                for key in keys:
                    o = filled(act, key)
                    write(key, o).then_inc(evac["a"], 1)

            def projected(key, o):
                _, j, s = key
                dst = PR[:, j, 1 + s * HALF:1 + (s + 1) * HALF] if j < RW else SQ[:, j - RW, s * HALF:(s + 1) * HALF]
                return act.copy(dst, o[:, 0:HALF])

            def lora_sigmoid(key, o):
                name, c, s = key
                dst, bias = (sg, "w_decay0") if name == "lora_w" else (aa, "a0")
                return act.activation(dst[:, c, s * HALF:(s + 1) * HALF], o[:, 0:HALF], ACT.Sigmoid,
                                      bias=pcol(bias, c))

            def memory(key, o):
                name, t = key
                if name == "mkT":
                    return act.copy(mkT[:, :, t * P:(t + 1) * P], o[:, :].rearrange("p (h s) -> p h s", h=XH))
                return act.copy((mkS if name == "mk" else mv)[:, t, :], o[:, :])

            for what, n in FRONT_ORDER:
                if what == "proj":
                    from_psum([("proj", n, s) for s in range(2)], projected)
                elif what == "lora":
                    act.wait_ge(s_mix, 2)
                    link(act.activation(PR[0:64, 12, 1:1 + NT], PR[0:64, 12, 1:1 + NT], ACT.Tanh))
                    act.activation(PR[:, 13, 1:1 + NT], PR[:, 13, 1:1 + NT], ACT.Sigmoid).then_inc(s_act, 1)
                    from_psum([(key, c, s) for key in ("lora_w", "lora_a") for c in range(4) for s in range(2)],
                              lora_sigmoid)
                elif what == "mem":
                    from_psum([(key, t) for key in ("mk", "mv", "mkT") for t in range(2)], memory)
                elif what == "sums":
                    from_psum([("norm_k", n, s) for s in range(2)],
                              lambda key, o: act.activation(sq[n % 2][:, key[2] * HALF:(key[2] + 1) * HALF],
                                                            o[:, 0:HALF], ACT.Sqrt))
                    act.wait_ge(s_cs, n + 1)
                    act.activation(wS[:, n, :], sg[:, n, SEQ:NT], ACT.Exp, scale=-KAPPA)
                    act.activation(csum[n % 2][:, 0:SEQ], csum[n % 2][:, 0:SEQ], ACT.Exp, scale=-KAPPA) \
                        .then_inc(s_ep, 1)
                    act.activation(tail[n % 2][:, 0:SEQ], tail[n % 2][:, 0:SEQ], ACT.Exp, scale=-KAPPA) \
                        .then_inc(s_ep, 1)
            act.wait_ge(s_prep, 4)
            for i in range(4):
                o = filled(act, ("shift_out", i))
                n = min(4, RW - 4 * i) * P
                act.copy(shiftO[:, i * 512:i * 512 + n], o[0:9, 0:n]).then_inc(evac["a"], 1)
            for i in range(6):
                o = filled(act, ("svec", i))
                act.copy(svt6[:, i, :], o[0:NS, :]).then_inc(evac["a"], 1)
            act.wait_ge(s_shout, 32)
            for t in range(TILES):
                o = filled(act, ("tokV", t))
                act.copy(tokV[:, t, :], o[:, :]).then_inc(evac["a"], 1)
            for t in range(TILES):
                for i in range(3):
                    o = filled(act, ("tok", t, i))
                    act.copy(tokX[:, i, :], o[:, :]).then_inc(evac["a"], 1)
                for q in range(2):
                    o = filled(act, ("N0", t, q))
                    act.copy(Ni[0][:, 4 * q:4 * q + 4, :], o[:, :].rearrange("p (h t) -> p h t", h=4)) \
                        .then_inc(evac["a"], 1)
                for k in range(6):
                    for q in range(2):
                        for key, dst in (("MM", Mi), ("NN", Ni)):
                            if (key, t, q, k) in rank and rank[(key, t, q, k)][0] == "a":
                                o = filled(act, (key, t, q, k))
                                act.copy(dst[(k + 1) % 2][:, 4 * q:4 * q + 4, :],
                                         o[:, :].rearrange("p (h t) -> p h t", h=4)).then_inc(evac["a"], 1)
                o = filled(act, ("WT", t))
                act.copy(WT, o[:, :].rearrange("p (c t) -> p c t", c=4)).then_inc(evac["a"], 1)
                o = filled(act, ("Y", t))
                if t == 0:
                    act.wait_ge(s_bv, 4)
                act.copy(yT[:, 0:4, t * P:(t + 1) * P], o[:, :].rearrange("p (c t) -> p c t", c=4)) \
                    .then_inc(evac["a"], 1)
            o = filled(act, ("wkvT",))
            act.copy(wkvO, o[0:64, :]).then_inc(evac["a"], 1)
            for c in range(4):
                for s in range(2):
                    o = filled(act, ("var", c, s))
                    act.activation(B1[:, c, s * HALF:(s + 1) * HALF], o[:, 0:HALF], ACT.Sqrt, scale=1.0 / HD,
                                   bias=small[:, 40:41]).then_inc(evac["a"], 1)
            o = filled(act, ("vtok",))
            act.copy(vtok, o[:, :].rearrange("p (t n) -> p t n", t=4)).then_inc(evac["a"], 1)
            o = filled(act, ("kvout",))
            link(act.copy(kvO[:, 0:P], o[:, 0:P]))
            act.copy(kvO[0:NS, P:3 * P], o[0:NS, P:3 * P]).then_inc(evac["a"], 1)

            def exps(n, rows, heads, W, sink):
                act.wait_ge(s_max, n + 1)
                stat = stats[n % 2]
                sm = Sm[n % 2][0:rows, 0:heads * (2048 // H if heads == H else 256)] \
                    .rearrange("p (h s) -> p h s", h=heads)
                if sink:
                    link(act.activation(stat[0:rows, 24:24 + heads], stat[0:rows, 24:24 + heads], ACT.Exp))
                for h in range(heads):
                    ins = act.activation(sm[:, h, 0:W], sm[:, h, 0:W], ACT.Exp, bias=stat[0:rows, 8 + h:9 + h],
                                         accum_out=stat[0:rows, 16 + h:17 + h])
                ins.then_inc(s_exp, 1)

            act.wait_ge(s_sso, 16)
            exps(0, P, H, P, True)
            for t in range(TILES):
                if t < TILES - 1:
                    exps(t + 1, P, H, 2 * P, True)
                na = 1 if t == 0 else 2
                for i in range(4):
                    o = filled(act, ("pT", t, i))
                    act.copy(PTa[:, 2 * i:2 * i + 2, 0:na, :],
                             o[:, :].rearrange("p (n a q) -> p n a q", n=2, a=2)[:, :, 0:na, :]) \
                        .then_inc(evac["a"], 1)
                o = filled(act, ("o", t))
                act.copy(yT[:, 4:8, t * P:(t + 1) * P], o[:, :].rearrange("p (c q) -> p c q", c=4)) \
                    .then_inc(evac["a"], 1)
            for i in range(2):
                o = filled(act, ("kT", i))
                act.copy(kTs[:, 4 * i:4 * i + 4, :], o[:, :].rearrange("p (b s) -> p b s", b=4)) \
                    .then_inc(evac["a"], 1)
            exps(4, 64, 1, P, True)

            def row_norms(first, sem):
                for t in range(TILES + 1):
                    R = tile_rows(t)
                    act.wait_ge(evac["v"], sem[t])
                    ms = small[0:R, t:t + 1]
                    link(act.activation(junk[0:R, :], x[0:R, t, :], ACT.Square, accum_out=ms))
                    act.activation(ms, ms, ACT.Sqrt, scale=1.0 / D, bias=small[0:R, 41:42]).then_inc(s_sq2, 1)

            row_norms(0, [rank[("wo", t, 1)][1] for t in range(5)])
            for h in range(XH):
                for s in range(2):
                    o = filled(act, ("q", h, s))
                    act.copy(qT[:, h, s * HALF:(s + 1) * HALF], o[:, 0:HALF]).then_inc(evac["a"], 1)
            for what, n in CROSS_ORDER:
                if what == "xs":
                    exps(5 + n, P, XH, MT, False)
                elif what == "xp":
                    for i in range(2):
                        o = filled(act, ("xpT", n, i))
                        act.copy(PTc[:, 2 * i:2 * i + 2, :, :], o[:, :].rearrange("p (n a q) -> p n a q", n=2, a=2)) \
                            .then_inc(evac["a"], 1)
                    o = filled(act, ("xo", n))
                    act.copy(yT[:, 0:4, n * P:(n + 1) * P], o[:, :].rearrange("p (c q) -> p c q", c=4)) \
                        .then_inc(evac["a"], 1)
                elif what == "ckT":
                    for st in range(2):
                        o = filled(act, ("ckT", n, st))
                        act.copy(KT[n % 2][:, :, st, :], o[:, :].rearrange("p (h s) -> p h s", h=XH)) \
                            .then_inc(evac["a"], 1)
            exps(9, 32, 1, MT, False)
            row_norms(5, [rank[("wc", t, 1)][1] for t in range(5)])
            act.wait_ge(s_exp1, 1)
            act.activation(Ta[:, :, 0:4], Ta[:, :, 0:4], ACT.Exp).then_inc(s_exp2, 1)
            act.wait_ge(s_exp1, 2)
            act.activation(ee, ee, ACT.Exp).then_inc(s_exp2, 1)
            bG, bA, bY = [banks[2], banks[6]], banks[3], banks[5]

            def act_block(i, b, r, first=False):
                act.wait_ge(s_pG, b + 1)
                act.activation(silu, bG[i % 2][0:BS, 0:FH], ACT.Silu).then_inc(s_as, 1)
                act.wait_ge(s_pA, b + 1)
                act.copy(actT, bA[:, 0:BS]).then_inc(s_aa, 1)
                act.wait_ge(s_pY, b + 1)
                if not first:
                    act.wait_ge(s_ys[i], r * 16)
                act.copy(yb[i][:, 512:1024], bY[0:BS, :]).then_inc(s_ay, 1)

            for i in range(NB3):
                act_block(i, i, 0, True)
            with act.Fori(1, NE // NB3) as it:
                for i in range(NB3):
                    act_block(i, it * NB3 + i, it)
            beyond = act.value_load(eidI[0:1, OVER:OVER + 1], min_val=0, max_val=OVER)
            with act.If(beyond > 0):
                act.wait_ge(s_ys[0], 16 * (NE // NB3))
                with act.Fori(0, OVER) as n:
                    act.wait_ge(s_oP, n * 4 + 2)
                    act.activation(silu, bG[0][0:BS, 0:FH], ACT.Silu).then_inc(s_oA, 1)
                    act.wait_ge(s_oP, n * 4 + 3)
                    act.copy(actT, bA[:, 0:BS]).then_inc(s_oA, 1)
                    act.wait_ge(s_oP, n * 4 + 4)
                    act.copy(yb[0][:, 512:1024], bY[0:BS, :]).then_inc(s_oA, 1)
            with act.Else():
                act.wait_ge(s_pY, NE)
            for t in range(T5):
                R = tile_rows(t)
                act.wait_ge(s_comb, t + 1)
                ms = small[0:R, t:t + 1]
                link(act.activation(junk[0:R, :], x[0:R, t, :], ACT.Square, accum_out=ms))
                act.activation(ms, ms, ACT.Sqrt, scale=1.0 / D, bias=small[0:R, 41:42]).then_inc(s_sq3, 1)

        @block.vector
        def _(dve):
            chain = [0]

            def link(ins):
                chain[0] += 1
                ins.then_inc(v_ch, 1)
                dve.wait_ge(v_ch, chain[0])

            tt, ts, stt = dve.tensor_tensor, dve.tensor_scalar, dve.scalar_tensor_tensor
            link(dve.memset(PR[:, :, 0:1], 0.0))
            link(dve.memset(small[:, 40:41], GN_EPS))
            dve.memset(small[:, 41:42], EPS).then_inc(s_eps, 1)
            o = filled(dve, ("par",))
            dve.tensor_copy(par[:, 0:42], o[:, 0:42]).then_inc(evac["v"], 1)
            o = filled(dve, ("shift_in",))
            dve.tensor_copy(shiftS, o[:, 0:RW * NS].rearrange("p (j n) -> p j n", j=RW)).then_inc(evac["v"], 1)

            for t in range(7):
                R = tile_rows(t) if t < 5 else P
                rows = x[0:R, t, :] if t < 5 else memX[:, t - 5, :]
                dve.wait_ge(s_sq, t + 1)
                ms = small[0:R, t:t + 1]
                link(dve.reciprocal(ms, ms))
                ts(rows, rows, ms, None, ALU.mult).then_inc(s_xn, 1)
                if t < 5:
                    for i in range(2):
                        o = filled(dve, ("xT", t, i))
                        g = gains[:, 0, 4 * i:4 * i + 4].unsqueeze(2).to_broadcast([P, 4, R])
                        tt(hA[:, 4 * i:4 * i + 4, t * P:t * P + R],
                           o[:, :].rearrange("p (k n) -> p k n", k=4)[:, :, 0:R], g, ALU.mult) \
                            .then_inc(evac["v"], 1)

            def mix(n, j):
                done(dve, ("proj", j, 1))
                link(dve.tensor_copy(saved[:, j, :], PR[:, j, SEQ:SEQ + 9]))
                d = diffs[n % 2]
                tt(d[:, 0:SEQ], PR[:, j, 0:SEQ], PR[:, j, 1:1 + SEQ], ALU.subtract)
                link(tt(d[:, SEQ:NT], shiftS[:, j, :], PR[:, j, 1 + SEQ:1 + NT], ALU.subtract))
                ins = stt(PR[:, j, 1:1 + NT], d, pcol("mu_shift", j), PR[:, j, 1:1 + NT], ALU.mult, ALU.add)
                ins.then_inc(s_mix, 1)

            def memory_gained():
                for t in range(2):
                    for i in range(2):
                        o = filled(dve, ("mT", t, i))
                        g = gains[:, 1, 4 * i:4 * i + 4].unsqueeze(2).to_broadcast([P, 4, P])
                        tt(memT[:, 4 * i:4 * i + 4, t * P:(t + 1) * P],
                           o[:, :].rearrange("p (k n) -> p k n", k=4), g, ALU.mult).then_inc(evac["v"], 1)
                link(dve.memset(reset, 1.0))
                link(dve.memset(reset.rearrange("p (n t) -> p n t", t=CH)[:, :, 0:1], 0.0))
                link(ts(small[:, 48:52], par[:, PARC["k_a"]:PARC["k_a"] + 4], -1.0, 1.0, ALU.mult, ALU.add))

            def chunked(a):
                return a[:, 0:SEQ].rearrange("p (n t) -> p n t", t=CH)

            def before_sums(c, mixed):
                dve.wait_ge(s_mix, mixed)
                R_, K_ = PR[:, c, 1:1 + NT], PR[:, 4 + c, 1:1 + NT]
                kk, cs = B0[:, c, :], csum[c % 2]
                done(dve, ("lora_a", c, 1))
                link(ts(kk, K_, pcol("k_k", c), None, ALU.mult))
                tt(sq[c % 2], kk, kk, ALU.mult).then_inc(s_kk, 1)
                link(ts(tmp[8], aa[:, c, :], pcol("k_a", c), small[:, 48 + c:49 + c], ALU.mult, ALU.add))
                link(tt(K_, K_, tmp[8], ALU.mult))
                stt(B1[:, c, :], R_, pcol("r_k", c), K_, ALU.mult, ALU.mult).then_inc(s_rk, 1)
                link(dve.tensor_tensor_scan(cs[:, 0:SEQ], reset, sg[:, c, 0:SEQ], 0.0, ALU.mult, ALU.add))
                tt(chunked(tail[c % 2]), chunked(cs)[:, :, CH - 1:CH].to_broadcast([P, NCH, CH]), chunked(cs),
                   ALU.subtract).then_inc(s_cs, 1)

            def after_sums(c):
                R_, K_ = PR[:, c, 1:1 + NT], PR[:, 4 + c, 1:1 + NT]
                kk, b, norm = B0[:, c, :], B1[:, c, :], sq[c % 2]
                decay, left = csum[c % 2], tail[c % 2]
                done(dve, ("norm_k", c, 1))
                link(ts(norm, norm, L2_EPS, None, ALU.max))
                link(dve.reciprocal(norm, norm))
                link(tt(kk, kk, norm, ALU.mult))
                for s in range(2):
                    o = filled(dve, ("bonus", c, s))
                    dve.tensor_copy(yT[:, c, s * HALF:(s + 1) * HALF], o[:, 0:HALF]).then_inc(evac["v"], 1)
                link(tt(b, kk, aa[:, c, :], ALU.mult))
                dve.wait_ge(s_ep, 2 * c + 1)
                dve.tensor_copy(PC[:, c, :], chunked(decay)[:, :, CH - 1])
                tt(R_[:, 0:SEQ], R_[:, 0:SEQ], decay[:, 0:SEQ], ALU.mult)
                stt(chunked(kk)[:, :, 1:CH], chunked(kk)[:, :, 1:CH], -1.0, chunked(decay)[:, :, 0:CH - 1],
                    ALU.mult, ALU.mult)
                ts(chunked(kk)[:, :, 0:1], chunked(kk)[:, :, 0:1], -1.0, None, ALU.mult)
                ts(kk[:, SEQ:NT], kk[:, SEQ:NT], -1.0, None, ALU.mult)
                dve.wait_ge(s_ep, 2 * c + 2)
                tt(b[:, 0:SEQ], b[:, 0:SEQ], left[:, 0:SEQ], ALU.mult)
                tt(K_[:, 0:SEQ], K_[:, 0:SEQ], left[:, 0:SEQ], ALU.mult).then_inc(s_prep, 1)
                dve.wait_ge(s_prep, c + 1)

            dve.wait_ge(evac["v"], 2)
            mixed = 0
            for what, n in FRONT_ORDER:
                if what == "proj" and n < RW:
                    mix(mixed, n)
                    mixed += 1
                elif what == "mT":
                    memory_gained()
                elif what == "pre":
                    before_sums(n, mixed)
                elif what == "post":
                    after_sums(n)
            dve.reciprocal(small[:, 8:40].rearrange("p (c n) -> p c n", c=4), PC).then_inc(s_inv, 1)
            done(dve, ("tokV", 3))
            done(dve, ("svec", 5))
            for c in range(4):
                V_ = PR[:, 8 + c, 1:1 + NT]
                tt(V_, V_, yT[:, c, :], ALU.mult).then_inc(s_bv, 1)
            dve.memset(ST[:, 0, :, :], 0.0).then_inc(s_vz, 1)
            dve.wait_ge(s_vz, 1)

            def sample_step():
                dve.wait_ge(s_svl, 16 * 7)
                a_, b_, k_, w_, r_ = [sv[:, i, :].unsqueeze(1).to_broadcast([P, 32, HD]) for i in range(5)]
                link(tt(Stmp, SS, a_, ALU.mult))
                link(dve.tensor_reduce(ssa, Stmp, X, ALU.add))
                link(tt(SS, SS, w_, ALU.mult))
                link(tt(Stmp, b_, ssa.unsqueeze(2).to_broadcast([P, 32, HD]), ALU.mult))
                link(tt(SS, SS, Stmp, ALU.add))
                link(tt(Stmp, k_, svv.unsqueeze(2).to_broadcast([P, 32, HD]), ALU.mult))
                tt(SS, SS, Stmp, ALU.add).then_inc(s_ss, 1)
                dve.wait_ge(s_ss, 1)
                link(tt(Stmp, SS, r_, ALU.mult))
                dve.tensor_reduce(sy, Stmp, X, ALU.add).then_inc(s_ss, 1)

            for t in range(TILES):
                if t > 0:
                    filled(dve, ("Y", t - 1))
                for h in range(H):
                    o = filled(dve, ("AB", t, h))
                    tt(AB[:, h, :, :], o[:, :].rearrange("p (a t) -> p a t", a=4), maskAB, ALU.mult) \
                        .then_inc(evac["v"], 1)
                for q in range(2):
                    for h in range(4 * q, 4 * q + 4):
                        done(dve, ("AB", t, h))
                    if t > 0:
                        done(dve, ("G", t - 1))
                        done(dve, ("WT", t - 1))
                    idb = ident.unsqueeze(1).to_broadcast([P, 4, P])
                    tt(Xi[:, 4 * q:4 * q + 4, :], AB[:, 4 * q:4 * q + 4, 0, :], idb, ALU.add).then_inc(s_st, 1)
                dve.wait_ge(s_st, 2 * t + 2)
                for k in range(6):
                    for q in range(2):
                        qs = slice(4 * q, 4 * q + 4)
                        if k > 0:
                            o = filled(dve, ("XM", t, q, k))
                            tt(Xi[:, qs, :], Xi[:, qs, :], o[:, :].rearrange("p (h t) -> p h t", h=4), ALU.add) \
                                .then_inc(evac["v"], 1)
                        if k < 5 and rank[("NN", t, q, k)][0] == "v":
                            o = filled(dve, ("NN", t, q, k))
                            dve.tensor_copy(Ni[(k + 1) % 2][:, qs, :], o[:, :].rearrange("p (h t) -> p h t", h=4)) \
                                .then_inc(evac["v"], 1)
                for key, dst in (("akv", akv), ("G", Gt)):
                    o = filled(dve, (key, t))
                    dve.tensor_copy(dst, o[:, :]).then_inc(evac["v"], 1)
                done(dve, ("G", t))
                for u in range(2):
                    tk, n = 64 * u, 2 * t + u
                    if n > 0:
                        done(dve, ("S", n // 2 if n % 2 else n // 2 - 1, (n + 1) % 2))
                    link(tt(ST[:, n + 1, :, :], ST[:, n, :, :],
                            PC[:, :, n:n + 1].to_broadcast([P, 4, HD]), ALU.mult))
                    for e in range(2):
                        o = filled(dve, ("U", t, u, e))
                        of = [a[tk:tk + 64, :].rearrange("p (c e i) -> p c e i", e=2, i=HD)[:, :, e, :]
                              for a in (Ut, Gt)]
                        tt(of[0], o[tk:tk + 64, 0:256].rearrange("p (c i) -> p c i", c=4), of[1], ALU.add) \
                            .then_inc(evac["v"], 1)
                    o = filled(dve, ("S", t, u))
                    tt(ST[:, n + 1, :, :], ST[:, n + 1, :, :], o[:, 0:256].rearrange("p (c i) -> p c i", c=4),
                       ALU.add).then_inc(evac["v"], 1)
                if t == 0:
                    sample_step()
            o = filled(dve, ("ysT",))
            dve.tensor_copy(yT[:, 0:4, SEQ:NT], o[:, 0:4 * NS].rearrange("p (c n) -> p c n", c=4)) \
                .then_inc(evac["v"], 1)
            for c in range(4):
                for s in range(2):
                    o = filled(dve, ("mean", c, s))
                    hs = slice(s * HALF, (s + 1) * HALF)
                    stt(yT[:, c, hs], o[:, 0:HALF], -1.0 / HD, yT[:, c, hs], ALU.mult, ALU.add) \
                        .then_inc(evac["v"], 1)
                done(dve, ("mean", c, 1))
                tt(B0[:, c, :], yT[:, c, :], yT[:, c, :], ALU.mult).then_inc(s_yc, 1)
            for c in range(4):
                done(dve, ("var", c, 1))
                link(dve.reciprocal(B1[:, c, :], B1[:, c, :]))
                link(tt(yT[:, c, :], yT[:, c, :], B1[:, c, :], ALU.mult))
                link(ts(yT[:, c, :], yT[:, c, :], pcol("ln_x_w", c), pcol("ln_x_b", c), ALU.mult, ALU.add))
                link(tt(yT[:, c, :], yT[:, c, :], PR[:, 8 + c, 1:1 + NT], ALU.add))
            for c in range(4):
                for s in range(2):
                    o = filled(dve, ("gate", c, s))
                    hs = slice(s * HALF, (s + 1) * HALF)
                    tt(yT[:, c, hs], yT[:, c, hs], o[:, 0:HALF], ALU.mult).then_inc(evac["v"], 1)
            dve.memset(small[:, 42:43], 0.0).then_inc(s_fin, 1)
            dve.wait_ge(s_const, 64)
            for s in range(2):
                hs = slice(s * HALF, (s + 1) * HALF)
                for i in range(2):
                    o = filled(dve, ("rka", i, s))
                    tt(RK[i][:, hs], o[:, 0:HALF], cosT[:, hs], ALU.mult).then_inc(evac["v"], 1)
                    o = filled(dve, ("rkb", i, s))
                    tt(ropeT, o[:, 0:HALF], sinT[:, hs], ALU.mult).then_inc(evac["v"], 1)
                    done(dve, ("rkb", i, s))
                    link(tt(RK[i][:, hs], RK[i][:, hs], ropeT, ALU.add))
                for c in range(4):
                    o = filled(dve, ("rq", c, s))
                    tt(ropeT, o[:, 0:HALF], sinT[:, hs], ALU.mult).then_inc(evac["v"], 1)
                    link(tt(SQ[:, c, hs], SQ[:, c, hs], cosT[:, hs], ALU.mult))
                    done(dve, ("rq", c, s))
                    link(tt(SQ[:, c, hs], SQ[:, c, hs], ropeT, ALU.add))
            dve.memset(small[:, 43:44], 0.0).then_inc(s_rope, 1)
            dve.wait_ge(s_sink, 32)

            def softmax(n, rows, heads, W, sink):
                sm = Sm[n % 2][0:rows, 0:heads * 256].rearrange("p (h s) -> p h s", h=heads)[:, :, 0:W]
                stat = stats[n % 2]
                mx, neg, snk = stat[0:rows, 0:heads], stat[0:rows, 8:8 + heads], stat[0:rows, 24:24 + heads]
                link(dve.tensor_reduce(mx, sm, X, ALU.max))
                if sink is not None:
                    link(tt(mx, mx, sink, ALU.max))
                    link(tt(snk, sink, mx, ALU.subtract))
                ts(neg, mx, -1.0, None, ALU.mult).then_inc(s_max, 1)

            def normalise(n, rows, heads, W, sink):
                sm = Sm[n % 2][0:rows, 0:heads * 256].rearrange("p (h s) -> p h s", h=heads)[:, :, 0:W]
                stat = stats[n % 2]
                sums, snk = stat[0:rows, 16:16 + heads], stat[0:rows, 24:24 + heads]
                dve.wait_ge(s_exp, n + 1)
                if sink is not None:
                    link(tt(sums, sums, snk, ALU.add))
                link(dve.reciprocal(sums, sums))
                tt(sm, sm, sums.unsqueeze(2).to_broadcast([rows, heads, W]), ALU.mult).then_inc(s_prob, 1)

            def window_tile(t):
                W = P if t == 0 else 2 * P
                sm = Sm[t % 2].rearrange("p (h s) -> p h s", h=H)
                band = swamask[:, 2 * P - W:].unsqueeze(1).to_broadcast([P, 2, W])
                for e in range(2):
                    for i in range(2):
                        o = filled(dve, ("s", t, e, i))
                        stt(sm[:, 4 * i + e:4 * i + e + 3:2, 0:W], o[:, 0:2 * W].rearrange("p (n s) -> p n s", n=2),
                            HD ** -0.5, band, ALU.mult, ALU.add).then_inc(evac["v"], 1)
                done(dve, ("s", t, 1, 1))
                softmax(t, P, H, W, sinks[:, 0:H])

            window_tile(0)
            for t in range(TILES):
                if t < TILES - 1:
                    window_tile(t + 1)
                normalise(t, P, H, P if t == 0 else 2 * P, sinks)
            for e in range(2):
                o = filled(dve, ("qd", e))
                dve.tensor_copy(QD[:, :, :, e], o[:, 0:32].rearrange("p (c b) -> p b c", c=4)).then_inc(evac["v"], 1)
            for g in range(2):
                o = filled(dve, ("ss", g))
                dve.tensor_copy(sT.rearrange("p (b g m) -> p b g m", b=NS, g=2)[:, :, g, :],
                                o[:, 0:32].rearrange("p (b m) -> p b m", b=NS)).then_inc(evac["v"], 1)
            o = filled(dve, ("ssT",))
            ts(Sm[0][0:64, 0:P], o[0:64, 0:P], HD ** -0.5, None, ALU.mult).then_inc(evac["v"], 1)
            done(dve, ("ssT",))
            softmax(4, 64, 1, P, sinks[0:64, H:H + 1])
            normalise(4, 64, 1, P, sinks)
            o = filled(dve, ("spT",))
            dve.tensor_copy(pTs, o[:, 0:64]).then_inc(evac["v"], 1)
            o = filled(dve, ("so",))
            dve.tensor_copy(yT[:, 4:8, SEQ:NT], o[:, 0:32].rearrange("p (c b) -> p c b", c=4)) \
                .then_inc(evac["v"], 1)

            def residual(key, first, gi, hkey):
                for t in range(TILES + 1):
                    R = tile_rows(t)
                    if key == "wo":
                        dve.wait_ge(s_xr[t], 16)
                    for n in range(2):
                        o = filled(dve, (key, t, n))
                        ns = slice(n * 512, (n + 1) * 512)
                        tt(x[0:R, t, ns], x[0:R, t, ns], o[0:R, :], ALU.add).then_inc(evac["v"], 1)
                for t in range(TILES + 1):
                    R = tile_rows(t)
                    dve.wait_ge(s_sq2, first + t + 1)
                    ms = small[0:R, t:t + 1]
                    link(dve.reciprocal(ms, ms))
                    if t >= 2:
                        filled(dve, (hkey, t - 2, 1))
                        if key == "wc":
                            dve.wait_ge(s_hn[t % 2], 16 * (t // 2))
                    ts(xn[t % 2][0:R, :], x[0:R, t, :], ms, None, ALU.mult).then_inc(s_xn2, 1)
                    if t >= 1:
                        gained(hkey, t - 1, gi)
                gained(hkey, 4, gi)

            def gained(hkey, t, gi):
                R = tile_rows(t)
                for i in range(2):
                    o = filled(dve, (hkey, t, i))
                    g = gains[:, gi, 4 * i:4 * i + 4].unsqueeze(2).to_broadcast([P, 4, R])
                    tt(hA[:, 4 * i:4 * i + 4, t * P:t * P + R],
                       o[:, :].rearrange("p (k n) -> p k n", k=4)[:, :, 0:R], g, ALU.mult).then_inc(evac["v"], 1)

            dve.wait_ge(s_kvw, 32)
            residual("wo", 0, 2, "xT2")
            for what, n in CROSS_ORDER:
                if what == "xs":
                    sm = Sm[(5 + n) % 2][:, 0:1024].rearrange("p (h s) -> p h s", h=XH)
                    for i in range(2):
                        o = filled(dve, ("xs", n, i))
                        ts(sm[:, 2 * i:2 * i + 2, :], o[:, :].rearrange("p (n s) -> p n s", n=2), P ** -0.5, None,
                           ALU.mult).then_inc(evac["v"], 1)
                    done(dve, ("xs", n, 1))
                    softmax(5 + n, P, XH, MT, None)
                    if n > 0:
                        normalise(4 + n, P, XH, MT, None)
                    if n == TILES - 1:
                        normalise(5 + n, P, XH, MT, None)
                elif what == "cs":
                    o = filled(dve, ("cs", n))
                    dve.tensor_copy(csS[:, :, 4 * n:4 * n + 4], o[:, 0:8].rearrange("p (a h) -> p a h", a=2)) \
                        .then_inc(evac["v"], 1)
            o = filled(dve, ("csT",))
            ts(Sm[1][0:32, 0:MT], o[0:32, 0:MT], P ** -0.5, None, ALU.mult).then_inc(evac["v"], 1)
            done(dve, ("csT",))
            softmax(9, 32, 1, MT, None)
            normalise(9, 32, 1, MT, None)
            o = filled(dve, ("cpT",))
            dve.tensor_copy(cpS, o[:, 0:64].rearrange("p (a n) -> p a n", a=2)).then_inc(evac["v"], 1)
            o = filled(dve, ("co",))
            dve.tensor_copy(yT[:, 0:4, SEQ:NT], o[:, 0:4 * NS].rearrange("p (b h) -> p h b", h=XH)) \
                .then_inc(evac["v"], 1)
            residual("wc", 5, 3, "xT3")
            link(dve.memset(Lg, 0.0))
            dve.memset(onesm, 1.0)
            dve.memset(zer, 1.0)
            dve.memset(slot_rows, 1e6).then_inc(s_init, 1)
            dve.wait_ge(s_init, 1)
            for t in range(T5):
                R = tile_rows(t)
                o = filled(dve, ("route", t))
                tt(Lg[0:R, t, :], o[0:R, 0:36], rbias[0:R, :], ALU.add).then_inc(evac["v"], 1)
            done(dve, ("route", 4))

            def wide(a, n):
                return a.unsqueeze(2).to_broadcast([P, T5, n])

            def first_max(src, n, top, out):
                io = iota[:, 0:n].unsqueeze(1).to_broadcast([P, T5, n])
                link(dve.tensor_reduce(top, src, X, ALU.max))
                link(tt(out, src, wide(top, n), ALU.is_lt))
                link(stt(out, out, 100.0, io, ALU.mult, ALU.add))
                link(dve.tensor_reduce(mi, out, X, ALU.min))
                link(tt(out, io, wide(mi, n), ALU.is_equal))

            lg, le = Lg[:, :, 0:4], Lg[:, :, 4:36]
            first_max(lg, 4, gmx, ohg)
            tt(Ta[:, :, 0:4], lg, wide(gmx, 4), ALU.subtract).then_inc(s_exp1, 1)
            dve.wait_ge(s_exp2, 1)
            link(dve.tensor_reduce(psel, Ta[:, :, 0:4], X, ALU.add))
            link(dve.reciprocal(psel, psel))
            link(ts(ohg, ohg, -NEG, NEG, ALU.mult, ALU.add))
            for t in range(T5):
                tt(Le[:, t, :].rearrange("p (g e) -> p g e", g=4), le[:, t, :].rearrange("p (g e) -> p g e", g=4),
                   ohg[:, t, :].unsqueeze(2).to_broadcast([P, 4, 8]), ALU.add)
            link(dve.memset(small[:, 44:45], 0.0))
            first_max(Le, NE, m1, oh[0])
            link(stt(Le, oh[0], NEG, Le, ALU.mult, ALU.add))
            first_max(Le, NE, m2, oh[1])
            tt(ee, m2, m1, ALU.subtract).then_inc(s_exp1, 1)
            for j in range(2):
                link(tt(oh[j], oh[j], wide(valid, NE), ALU.mult))
            tt(Mk, oh[0], oh[1], ALU.add).then_inc(s_mk, 1)
            dve.wait_ge(s_exp2, 2)
            link(ts(m1, ee, 1.0, None, ALU.add))
            link(dve.reciprocal(m1, m1))
            link(tt(cw[0], m1, psel, ALU.mult))
            link(tt(cw[1], cw[0], ee, ALU.mult))
            o = filled(dve, ("ranks",))
            dve.tensor_copy(RC, o[:, 0:6 * NE]).then_inc(evac["v"], 1)
            done(dve, ("ranks",))
            cnt_e = RC[:, T5 * NE:]
            link(ts(nb, cnt_e, float(BS - 1), None, ALU.add))
            link(dve.tensor_copy(nbI, nb))
            link(ts(nbI, nbI, BSHIFT, None, ALU.arith_shift_right))
            link(dve.tensor_copy(nb, nbI))
            link(ts(nb, nb, -1.0, 0.0, ALU.add, ALU.max))
            link(dve.tensor_tensor_scan(cum, zer, nb, 0.0, ALU.mult, ALU.add))
            link(tt(nb, cum, nb, ALU.subtract))
            link(stt(nb, nb, float(NE - 1), iota[:, 0:NE], ALU.add, ALU.subtract))
            rk = RC[:, 0:T5 * NE].rearrange("p (t e) -> p t e", t=T5)
            link(ts(far, rk, float(BS), None, ALU.is_ge))
            link(tt(far, far, nb.unsqueeze(1).to_broadcast([P, T5, NE]), ALU.mult))
            link(tt(far, far, iota[:, 0:NE].unsqueeze(1).to_broadcast([P, T5, NE]), ALU.add))
            link(stt(slot_all, far, float(BS), rk, ALU.mult, ALU.add))
            link(ts(mi, valid, -1e6, 1e6, ALU.mult, ALU.add))
            for j in range(2):
                link(tt(Ta, oh[j], slot_all, ALU.mult))
                link(dve.tensor_reduce(sl[j], Ta, X, ALU.add))
                link(tt(sl[j], sl[j], mi, ALU.add))
            link(dve.tensor_copy(slI[0], sl[0]))
            dve.tensor_copy(slI[1], sl[1]).then_inc(s_slot, 1)
            link(tt(big, cum.unsqueeze(1).to_broadcast([P, OVER, NE]),
                    iota[:, 0:OVER].unsqueeze(2).to_broadcast([P, OVER, NE]), ALU.is_le))
            link(dve.tensor_reduce(eid[:, 0:OVER], big, X, ALU.add))
            link(ts(eid[:, 0:OVER], eid[:, 0:OVER], float(NE - 1), None, ALU.min))
            link(dve.tensor_copy(eid[:, OVER:OVER + 1], cum[:, NE - 1:NE]))
            dve.tensor_copy(eidI, eid).then_inc(s_eid, 1)
            o = filled(dve, ("slots",))
            dve.tensor_copy(pidI[0:BS], o[0:BS, 0:NBLK]).then_inc(evac["v"], 1)
            done(dve, ("slots",))
            ts(tokI[0:BS], pidI[0:BS], 1, None, ALU.arith_shift_right).then_inc(s_idx, 1)
            bX, bG, bY = banks[0], [banks[2], banks[6]], banks[4]

            def rows_gained(i):
                g = gains[:, 3, :].unsqueeze(2).to_broadcast([P, KD, BS])
                return tt(xTe[i % 2], bX[:, 0:KD * BS].rearrange("p (k n) -> p k n", k=KD), g, ALU.mult)

            def rows_out(i, b):
                dve.wait_ge(s_pX, b + 1)
                rows_gained(i).then_inc(s_vx, 1)

            def dve_block(i, b, r, first, nxt):
                dve.wait_ge(s_as, b + 1)
                tt(act_e, silu, bG[i % 2][0:BS, FH:2 * FH], ALU.mult).then_inc(s_vm, 1)
                if nxt:
                    rows_out(i, b + 2)
                dve.wait_ge(s_pY, b + 1)
                if not first:
                    dve.wait_ge(s_ys[i], r * 16)
                dve.tensor_copy(yb[i][:, 0:512], bY[0:BS, :]).then_inc(s_vy, 1)

            rows_out(0, 0)
            rows_out(1, 1)
            rounds = NE // NB3
            for i in range(NB3):
                dve_block(i, i, 0, True, True)
            with dve.Fori(1, rounds - 1) as it:
                for i in range(NB3):
                    dve_block(i, it * NB3 + i, it, False, True)
            for i in range(NB3):
                dve_block(i, (rounds - 1) * NB3 + i, rounds - 1, False, i < NB3 - 2)
            beyond = dve.value_load(eidI[0:1, OVER:OVER + 1], min_val=0, max_val=OVER)
            with dve.If(beyond > 0):
                dve.wait_ge(s_ys[0], 16 * (NE // NB3))
                with dve.Fori(0, OVER) as n:
                    dve.wait_ge(s_oP, n * 4 + 1)
                    rows_gained(0).then_inc(s_oV, 1)
                    dve.wait_ge(s_oA, n * 3 + 1)
                    tt(act_e, silu, bG[0][0:BS, FH:2 * FH], ALU.mult).then_inc(s_oV, 1)
                    dve.wait_ge(s_oP, n * 4 + 4)
                    dve.tensor_copy(yb[0][:, 0:512], bY[0:BS, :]).then_inc(s_oV, 1)
            with dve.Else():
                dve.wait_ge(s_pY, NE)
            for t in range(T5):
                R = tile_rows(t)
                dve.wait_ge(s_yl[t % 2], 16 * (t // 2 + 1))
                link(stt(x[0:R, t, :], ydt[t % 2][0:R, 0, :], cw[0][0:R, t:t + 1], x[0:R, t, :], ALU.mult, ALU.add))
                stt(x[0:R, t, :], ydt[t % 2][0:R, 1, :], cw[1][0:R, t:t + 1], x[0:R, t, :], ALU.mult, ALU.add) \
                    .then_inc(s_comb, 1)
            for t in range(T5):
                R = tile_rows(t)
                dve.wait_ge(s_sq3, t + 1)
                ms = small[0:R, t:t + 1]
                link(dve.reciprocal(ms, ms))
                stt(x[0:R, t, :], x[0:R, t, :], ms, gfin[0:R, :], ALU.mult, ALU.mult).then_inc(s_res, 1)


_INS = ['x_prompt', 'x_sample', 'mem_prompt', 'state_rwkv_shift', 'state_rwkv_wkv', 'cache_swa_k', 'cache_swa_v',
        'cache_mem_k', 'cache_mem_v', 'norm_mix', 'w_in', 'mu_shift', 'w_decay0', 'w_decay_up', 'a0', 'w_a_up',
        'w_g_up', 'k_k', 'k_a', 'r_k', 'ln_x_w', 'ln_x_b', 'attn_sink', 'w_out', 'norm_cross', 'norm_mem', 'w_cq',
        'w_ck', 'w_cv', 'w_co', 'norm_ffn', 'w_group_router', 'b_group_router', 'w_expert_router',
        'b_expert_router', 'w_exp_gate', 'w_exp_up', 'w_exp_down', 'norm_final']
_OUTS = [('y_prompt', (1, 512, 1024)), ('y_sample', (8, 1, 1024)), ('prompt_shift', (1, 1, 1792)),
         ('prompt_wkv', (1, 1, 8, 64, 64)), ('prompt_swa_k', (1, 1, 128, 2, 64)),
         ('prompt_swa_v', (1, 1, 128, 2, 64)), ('prompt_mem_k', (1, 1, 256, 4, 128)),
         ('prompt_mem_v', (1, 1, 256, 4, 128)), ('sample_shift', (1, 8, 1792)), ('sample_wkv', (1, 8, 8, 64, 64)),
         ('sample_swa_k', (1, 8, 128, 2, 64)), ('sample_swa_v', (1, 8, 128, 2, 64))]


def tables():
    i = np.arange(P)
    ident = np.eye(P, dtype=np.float32)
    bones = (i[:, None] // HD == i[None, :] // HD).astype(np.float32)
    strict = bones * (i[:, None] < i[None, :])
    incl = bones * (i[:, None] <= i[None, :])
    diff = i[:, None] + P - np.arange(2 * P)[None, :]
    band = np.where((diff >= 0) & (diff < P), 0.0, NEG)
    tri = (i[:, None] < i[None, :]).astype(np.float32)
    swap = ((i[:, None] ^ 32) == i[None, :]).astype(np.float32)
    dup = [((i[:, None] // HD == g) & (i[:, None] % HD == i[None, :] % HD)).astype(np.float32) for g in range(2)]
    dsw = [((i[:, None] // HD == g) & ((i[:, None] % HD) ^ 32 == i[None, :] % HD)).astype(np.float32)
           for g in range(2)]
    pos = np.concatenate([np.arange(SEQ), np.full(NS, 1024)]).astype(np.float32)
    inv = (np.float32(10000.0) ** (-np.arange(32, dtype=np.float32) * np.float32(2.0) / np.float32(64)))
    ang = (pos[None, :] * inv.astype(np.float32)[:, None]).astype(np.float32)
    cos = np.tile(np.cos(ang), (4, 1))
    sin = np.tile(np.concatenate([-np.sin(ang), np.sin(ang)]), (2, 1))
    misc = np.zeros((P, MISC), np.float32)
    misc[:, 0:NBLK] = np.arange(NBLK)
    tok = np.arange(TILES + 1)[None, :] * P + i[:, None]
    misc[:, NBLK:NBLK + 10] = (2 * tok[:, :, None] + np.arange(2)).reshape(P, 10)
    misc[:, NBLK + 10:NBLK + 15] = tok < NT
    parts = [ident, bones, strict, incl, strict, incl, band, tri, swap, dup[0], dup[1], dsw[0], dsw[1], cos, sin, misc]
    return np.concatenate(parts, axis=1).astype(np.float32)


def kernel(**inputs):
    import concourse.bacc as _bacc
    from concourse.bass_utils import run_bass_kernel_spmd as _run

    nc = _bacc.Bacc("TRN2", target_bir_lowering=False, num_devices=1)
    arrays, A, O = {}, {}, {}
    for name in _INS:
        a = np.ascontiguousarray(inputs[name])
        arrays[f"in_{name}"] = a
        A[name] = nc.dram_tensor(f"in_{name}", a.shape, mybir.dt.from_np(a.dtype), kind="ExternalInput").ap()
    c = tables()
    arrays["in_tables"] = c
    A["c_tables"] = nc.dram_tensor("in_tables", c.shape, F32, kind="ExternalInput").ap()
    for name, shape in _OUTS:
        O[name] = nc.dram_tensor(f"out_{name}", shape, F32, kind="ExternalOutput").ap()
    small_kernel(nc, A, O)
    r = _run(nc, [arrays], core_ids=[0])
    return tuple(r.results[0][f"out_{name}"] for name, _ in _OUTS)
```

```python
from contextlib import ExitStack

import numpy as np

import concourse.bass as bass
from concourse import mybir

F32 = mybir.dt.float32
I32 = mybir.dt.int32
U32 = mybir.dt.uint32
ALU = mybir.AluOpType
ACT = mybir.ActivationFunctionType
X = mybir.AxisListType.X

P = 128
D = 1024
KD = D // P
SEQ = 512
NS = 8
NT = SEQ + NS
HALF = NT // 2
TILES = SEQ // P
H = 8
HD = 64
PAIRS = H // 2
CH = 64
NCH = SEQ // CH
RW = 14
SW = 6
RCOLS = RW * P
MT = 256
XH = 4
EPS = 1e-5
GN_EPS = 64e-5
L2_EPS = 1e-12
KAPPA = float(np.exp(-0.5))
NEG = -1e30
NE = 32
FH = 128
PAIRS_E = 2 * NT
BS = 64
BSHIFT = BS.bit_length() - 1
OVER = (PAIRS_E - 1) // BS
NBLK = NE + OVER
COUNT = max(NBLK, BS)
MISC = COUNT + 16
BANKS = 8

PAR_ROWS = (("mu_shift", 14), ("w_decay0", 4), ("a0", 4), ("k_k", 4), ("k_a", 4), ("r_k", 4), ("ln_x_w", 4),
            ("ln_x_b", 4))


FRONT_ORDER = [("proj", 12), ("proj", 13), ("proj", 14), ("lora_in", 0), ("proj", 15), ("mT", 0), ("lora", 0), ("mem", 0),
               ("proj", 4), ("proj", 5), ("proj", 6), ("proj", 7), ("proj", 0), ("pre", 0), ("proj", 1), ("pre", 1),
               ("sums", 0), ("post", 0), ("proj", 2), ("sums", 1), ("pre", 2), ("post", 1), ("proj", 3), ("proj", 8),
               ("sums", 2), ("pre", 3), ("post", 2), ("proj", 9), ("proj", 10), ("sums", 3), ("post", 3),
               ("proj", 11), ("proj", 16), ("proj", 17), ("proj", 18), ("proj", 19)]

RECUR_ORDER = [("tok", 0, 0), ("AB", 0, 0), ("AB", 0, 1), ("N0", 0, 0), ("level", 0, 0), ("level", 0, 1),
               ("sample", 0, 0)] + [("level", 0, k) for k in range(2, 6)] + [("fin", 0, 0)]
for _t in range(1, TILES):
    RECUR_ORDER += [("tok", _t, 0), ("U", _t - 1, 0)] + [("sample", 0, 1)] * (_t == 1) + \
        [("AB", _t, 0), ("S", _t - 1, 0), ("AB", _t, 1), ("U", _t - 1, 1), ("N0", _t, 0), ("level", _t, 0),
         ("S", _t - 1, 1), ("level", _t, 1), ("Y", _t - 1, 0)]
    if _t < TILES - 1:
        RECUR_ORDER += [("level", _t, 2), ("rq", 2 * _t - 2, 0), ("level", _t, 3), ("rq", 2 * _t - 2, 1),
                        ("level", _t, 4), ("rq", 2 * _t - 1, 0), ("level", _t, 5), ("rq", 2 * _t - 1, 1)]
    else:
        RECUR_ORDER += [("rk", 0, 0), ("level", _t, 2), ("rk", 0, 1), ("rk", 1, 0), ("level", _t, 3), ("rk", 1, 1),
                        ("vk", 0, 0), ("level", _t, 4), ("ws", 0, 0), ("level", _t, 5)]
    RECUR_ORDER += [("fin", _t, 0)]
RECUR_ORDER += [("ws", 1, 0), ("U", 3, 0), ("wp", 0, 0), ("S", 3, 0), ("ws", 2, 0), ("U", 3, 1), ("wp", 1, 0),
                ("S", 3, 1), ("ws", 3, 0), ("Y", 3, 0), ("wp", 2, 0), ("wp", 3, 0)]

CROSS_ORDER = (("xs", 0), ("ckT", 0), ("xs", 1), ("ckT", 1), ("xp", 0), ("cs", 0), ("xs", 2), ("ckT", 2), ("cs", 1),
               ("ckT", 3), ("xp", 1), ("cs", 2), ("xs", 3), ("ckT", 4), ("cs", 3), ("ckT", 5), ("cs", 4),
               ("xp", 2), ("ckT", 6), ("cs", 5), ("ckT", 7), ("cs", 6), ("xp", 3), ("cs", 7))


def tile_rows(t):
    return P if t < TILES else NS


def projected_rows(key, hkey):
    g = []
    for t in range(TILES + 2):
        if t <= TILES:
            g += [((key, t, n), "v") for n in range(2)]
        if t >= 1:
            g += [((hkey, t - 1, i), "v") for i in range(2)]
    return g


def bank_plan():
    g = [(("par",), "v"), (("shift_in",), "v")]
    for t in range(TILES + 1):
        g += [(("xT", t, i), "v") for i in range(2)]
    for what, n in FRONT_ORDER:
        if what == "proj":
            g += [(("proj", n, s), "a") for s in range(2)]
        elif what == "mT":
            g += [(("mT", t, i), "v") for t in range(2) for i in range(2)]
        elif what == "lora":
            g += [((key, c, s), "a") for key in ("lora_w", "lora_a") for c in range(4) for s in range(2)]
        elif what == "mem":
            g += [((key, t), "a") for key in ("mk", "mv", "mkT") for t in range(2)]
        elif what == "sums":
            g += [(("norm_k", n, s), "a") for s in range(2)] + [(("bonus", n, s), "v") for s in range(2)]
    g += [(("shift_out", i), "a") for i in range(4)]
    g += [(("svec", i), "a") for i in range(6)]
    g += [(("tokV", t), "a") for t in range(TILES)]
    for what, t, n in RECUR_ORDER:
        if what == "level":
            for q in range(2):
                if n > 0:
                    g += [(("XM", t, q, n), "v")]
                if n < 4:
                    g += [(("MM", t, q, n), "a")]
                if n < 5:
                    g += [(("NN", t, q, n), "v" if n % 2 else "a")]
        else:
            g += {"tok": [(("tok", t, i), "a") for i in range(3)],
                  "AB": [(("AB", t, h), "v") for h in range(4 * n, 4 * n + 4)],
                  "N0": [(("N0", t, q), "a") for q in range(2)],
                  "fin": [(("akv", t), "v"), (("G", t), "v"), (("WT", t), "a")],
                  "U": [(("U", t, n, 0), "v"), (("U", t, n, 1), "v")],
                  "S": [(("S", t, n), "v")],
                  "Y": [(("Y", t), "a")],
                  "sample": [],
                  "rq": [(("rq", t, n), "v")],
                  "rk": [(("rka", t, n), "v"), (("rkb", t, n), "v")],
                  "vk": [(("vtok",), "a"), (("kvout",), "a")],
                  "ws": [(("s", t, e, i), "v") for e in range(2) for i in range(2)],
                  "wp": [(("pT", t, i), "a") for i in range(4)] + [(("o", t), "a")]}[what]
    g += [(("wkvT",), "a"), (("ysT",), "v")]
    g += [(("mean", c, s), "v") for c in range(4) for s in range(2)]
    g += [(("gate", c, s), "a") for c in range(4) for s in range(2)]
    g += [(("qd", e), "v") for e in range(2)]
    g += [(("var", c, s), "a") for c in range(4) for s in range(2)]
    g += [(("kT", i), "a") for i in range(2)]
    g += [(("ss", e), "v") for e in range(2)]
    g += [(("ssT",), "v")]
    g += [(("spT",), "v"), (("so",), "v")]
    g += projected_rows("wo", "xT2")
    g += [(("q", h, s), "a") for h in range(XH) for s in range(2)]
    for step in CROSS_ORDER:
        what, n = step
        g += {"xs": [(("xs", n, i), "v") for i in range(2)],
              "xp": [(("xpT", n, i), "a") for i in range(2)] + [(("xo", n), "a")],
              "ckT": [(("ckT", n, i), "a") for i in range(2)],
              "cs": [(("cs", n), "v")]}[what]
    g += [(("csT",), "v"), (("cpT",), "v"), (("co",), "v")]
    g += projected_rows("wc", "xT3")
    g += [(("route", t), "v") for t in range(TILES + 1)]
    g += [(("ranks",), "v"), (("slots",), "v")]
    return g


def small_kernel(nc, A, O):
    plan = bank_plan()
    place = {key: n for n, (key, _) in enumerate(plan)}
    rank, count = {}, {"v": 0, "a": 0}
    for key, e in plan:
        count[e] += 1
        rank[key] = (e, count[e])

    with ExitStack() as ctx:
        def sem(name):
            return ctx.enter_context(nc.semaphore(name))

        arena = ctx.enter_context(nc.sbuf_tensor("arena", [P, 53166], F32))
        at = {}

        def region(name, words, start=None):
            if start is None:
                start = at["_end"]
                at["_end"] = start + words
            at[name] = start
            return arena[:, start:start + words]

        at["_end"] = 0
        ident = region("ident", P)
        bones = region("bones", P)
        maskAB = region("maskAB", 4 * P).rearrange("p (a t) -> p a t", a=4)
        swamask = region("swamask", 2 * P)
        tri = region("tri", P)
        sel = region("sel", 5 * P).rearrange("p (a t) -> p a t", a=5)
        cosT = region("cosT", NT)
        sinT = region("sinT", NT)
        misc = region("misc", MISC)
        gains = region("gains", 4 * KD).rearrange("p (a k) -> p a k", a=4)
        par = region("par", 48)
        small = region("small", 64)
        lora = region("lora", 512)
        gup = region("gup", 512)
        mkT = region("mkT", XH * MT).rearrange("p (h s) -> p h s", h=XH)
        mv = region("mv", 2 * 512).rearrange("p (t n) -> p t n", t=2)
        stat = region("stat", 64)
        stats = [stat[:, 32 * i:32 * i + 32] for i in range(2)]
        sinks = region("sinks", 2 * H)
        saved = region("saved", RW * 9).rearrange("p (j n) -> p j n", j=RW)
        shiftS = region("shiftS", RW * NS).rearrange("p (j n) -> p j n", j=RW)
        PC = region("PC", 32).rearrange("p (c n) -> p c n", c=4)
        wS = region("wS", 32).rearrange("p (c n) -> p c n", c=4)
        hA = region("hA", KD * NT).rearrange("p (k n) -> p k n", k=KD)
        hB = region("hB", KD * NT).rearrange("p (k n) -> p k n", k=KD)
        ring = [region(f"ring{i}", 4096) for i in range(3)]
        PR = region("PR", RW * (NT + 1)).rearrange("p (j n) -> p j n", j=RW)
        SQ = region("SQ", SW * NT).rearrange("p (j n) -> p j n", j=SW)
        B0 = region("B0", 4 * NT).rearrange("p (c n) -> p c n", c=4)
        B1 = region("B1", 4 * NT).rearrange("p (c n) -> p c n", c=4)
        xreg = region("x", 5 * D)
        x = xreg.rearrange("p (t n) -> p t n", t=5)
        tokV = region("tokV", TILES * 512).rearrange("p (t n) -> p t n", t=TILES)
        STr = region("ST", 9 * 256)
        ST = STr.rearrange("p (s c i) -> p s c i", s=9, c=4)
        assert at["_end"] <= 53166, at["_end"]
        memT = arena[:, at["hB"]:at["hB"] + KD * MT].rearrange("p (k n) -> p k n", k=KD)
        memX = arena[:, at["hB"] + 2080:at["hB"] + 2080 + 2048].rearrange("p (t n) -> p t n", t=2)
        mkS = arena[:, at["hB"] + 2080:at["hB"] + 2080 + 1024].rearrange("p (t n) -> p t n", t=2)
        junk = arena[:, at["B0"]:at["B0"] + D]
        prow = arena[:, at["B0"] + 1100:at["B0"] + 1100 + P]
        srow = arena[:, at["B1"]:at["B1"] + RCOLS]
        sg = arena[:, at["x"]:at["x"] + 2080].rearrange("p (c n) -> p c n", c=4)
        aa = arena[:, at["x"] + 2080:at["x"] + 4160].rearrange("p (c n) -> p c n", c=4)
        reset = arena[:, at["x"] + 4160:at["x"] + 4160 + SEQ]
        tmp = [arena[:, at["x"] + 4672 + i * NT:at["x"] + 4672 + (i + 1) * NT] for i in range(9)]
        assert at["x"] + 4672 + 9 * NT <= at["_end"] and at["tokV"] == at["x"] + 5 * D
        sq, csum, tail, diffs = tmp[0:2], tmp[2:4], tmp[4:6], tmp[6:8]
        Bt = hA[:, 0:4, :]
        Kt = hA[:, 4:8, :]
        Xi = arena[:, at["x"]:at["x"] + 1024].rearrange("p (h t) -> p h t", h=H)
        Mi = [arena[:, at["x"] + 1024 * (1 + i):at["x"] + 1024 * (2 + i)].rearrange("p (h t) -> p h t", h=H)
              for i in range(2)]
        Ni = [arena[:, at["x"] + 1024 * (3 + i):at["x"] + 1024 * (4 + i)].rearrange("p (h t) -> p h t", h=H)
              for i in range(2)]
        ABs = [ring[1 - i].rearrange("p (h a t) -> p h a t", h=H, a=4) for i in range(2)]
        tokXs = [[ring[2][:, 0:512], ring[2][:, 512:1024], ring[2][:, 1024:1536]],
                 [ring[2][:, 0:512], ring[2][:, 3584:4096], PR[:, 12, 0:512]]]
        akv = ring[2][:, 1536:2048]
        Gt = ring[2][:, 2048:2560]
        WT = ring[2][:, 2560:3072].rearrange("p (c t) -> p c t", c=4)
        Ut = ring[2][:, 3072:3584]
        yT = hB
        SS = arena[:, at["hB"] + 2080:at["hB"] + 2080 + 2048].rearrange("p (i j) -> p i j", i=32)
        Stmp = ring[0][:, 0:2048].rearrange("p (i j) -> p i j", i=32)
        sv = ring[0][:, 3072:3072 + 5 * HD].rearrange("p (a j) -> p a j", a=5)
        svv = ring[0][:, 3400:3432]
        ssa = ring[0][:, 3432:3464]
        sy = ring[0][:, 3464:3496]
        svt6 = ring[0][0:NS, 0:3072].rearrange("p (a n) -> p a n", a=6)
        ysr = ring[1][0:NS, 512:1024]
        shiftO = arena[0:9, at["tokV"]:at["tokV"] + RCOLS]
        wkvO = ring[1][0:64, 0:512]
        RK = [hA.rearrange("p k n -> p (k n)")[:, i * NT:(i + 1) * NT] for i in range(2)]
        hAf = arena[:, at["hA"]:at["hA"] + KD * NT]
        vtok = hAf[:, 1040:1552].rearrange("p (t n) -> p t n", t=4)
        PTa = hAf[:, 1552:3600].rearrange("p (h a q) -> p h a q", h=H, a=2)
        PTc = arena[:, at["tokV"]:at["tokV"] + 1024].rearrange("p (h a q) -> p h a q", h=XH, a=2)
        kvO = hAf[:, 3600:3984]
        Sm = [ring[2][:, 2048 * i:2048 * (i + 1)] for i in range(2)]
        ropeT = lora[:, 0:HALF]
        SmW = [arena[:, at[f"B{1 - i}"]:at[f"B{1 - i}"] + 2048] for i in range(2)]
        ysq = ring[2][:, 0:4 * NT].rearrange("p (c n) -> p c n", c=4)
        ydev = B0
        gateS = hAf[:, 1552:1552 + 4 * NT].rearrange("p (c n) -> p c n", c=4)
        Kc = arena[:, at["tokV"]:at["tokV"] + 1024].rearrange("p (b n) -> p b n", b=NS)
        Vc = arena[:, at["tokV"] + 1024:at["tokV"] + 2048].rearrange("p (b n) -> p b n", b=NS)
        kTs = STr[:, 0:1024].rearrange("p (b s) -> p b s", b=NS)
        QD = STr[:, 1024:1088].rearrange("p (b c e) -> p b c e", b=NS, c=4)
        sT = STr[:, 2048:2048 + 64]
        pTs = STr[:, 2112:2112 + 64]
        xn = [arena[:, at["PR"] + i * D:at["PR"] + (i + 1) * D] for i in range(2)]
        kv_ring = [arena[:, at["PR"] + (2 + i) * 1024:at["PR"] + (3 + i) * 1024].rearrange("p (a n) -> p a n", a=2)
                   for i in range(4)]
        late = [hAf[:, i * 1024:(i + 1) * 1024].rearrange("p (a n) -> p a n", a=2) for i in range(4)]

        def values_of(b):
            return kv_ring[b] if b < 4 else late[b - 4]

        KT = [arena[:, at["B1"] + i * 1024:at["B1"] + (i + 1) * 1024].rearrange("p (h a s) -> p h a s", h=XH, a=2)
              for i in range(2)]
        csS = STr[:, 0:64].rearrange("p (a n) -> p a n", a=2)
        cpS = STr[:, 64:128].rearrange("p (a n) -> p a n", a=2)
        qT = SQ[:, 0:4, :]
        iota = misc[:, 0:COUNT]
        pair_no1 = misc[:, COUNT:COUNT + 10]
        valid = misc[:, COUNT + 10:COUNT + 15]
        NB3 = 4
        wslots = [at["ring0"] + i * 3072 for i in range(4)] + [at["SQ"], at["lora"], at["PR"], at["PR"] + 3072]
        assert at["stat"] - at["lora"] == 3072
        NW = len(wslots)
        we = [arena[:, w:w + 3072].rearrange("p (a n) -> p a n", a=3) for w in wslots]
        xg = [arena[:, at["hA"] + i * D:at["hA"] + (i + 1) * D] for i in range(NB3)]
        yb = [arena[0:BS, at["B0"] + i * D:at["B0"] + (i + 1) * D] for i in range(NB3)]
        xTe = [arena[:, at["PR"] + 6 * D + i * KD * BS:at["PR"] + 6 * D + (i + 1) * KD * BS]
               .rearrange("p (k n) -> p k n", k=KD) for i in range(2)]
        silu, act_f = [arena[:, at["maskAB"] + i * P:at["maskAB"] + (i + 1) * P] for i in range(2)]
        silu, act_e = silu[0:BS], act_f[0:BS]
        actT = arena[:, at["maskAB"] + 2 * P:at["maskAB"] + 2 * P + BS]
        gfin = arena[:, at["tokV"] + 1024:at["tokV"] + 2048]
        wr = STr[:, 256:256 + KD * 36].rearrange("p (k n) -> p k n", k=KD)
        rbias = STr[:, 544:580]
        ydt = [arena[:, at["ring0"] + i * 2048:at["ring0"] + (i + 1) * 2048].rearrange("p (j n) -> p j n", j=2)
               for i in range(5)]
        hBf = arena[:, at["hB"]:at["hB"] + KD * NT]
        off = [0]

        def route_region(n, dt=None):
            v = hBf[:, off[0]:off[0] + n]
            off[0] += n
            return v if dt is None else v.bitcast(dt)

        T5 = TILES + 1
        Lg = route_region(T5 * 36).rearrange("p (t n) -> p t n", t=T5)
        Le = route_region(T5 * NE).rearrange("p (t n) -> p t n", t=T5)
        Ta = route_region(T5 * NE).rearrange("p (t n) -> p t n", t=T5)
        oh = [route_region(T5 * NE).rearrange("p (t n) -> p t n", t=T5) for _ in range(2)]
        ohg = route_region(T5 * 4).rearrange("p (t n) -> p t n", t=T5)
        Mk = route_region(T5 * NE).rearrange("p (t n) -> p t n", t=T5)
        RC = route_region(6 * NE)
        slot_all = route_region(T5 * NE).rearrange("p (t n) -> p t n", t=T5)
        gmx, psel, m1, m2, mi, ee = [route_region(T5) for _ in range(6)]
        cw = [route_region(T5) for _ in range(2)]
        J = 2 * T5
        slot = route_region(J)
        slot_block = route_region(J)
        slot_blockI = route_region(J, I32)
        in_block = route_region(J * NBLK).rearrange("p (j b) -> p j b", j=J)
        in_row = route_region(J * BS).rearrange("p (j r) -> p j r", j=J)
        nb, cum, zer = [route_region(NE) for _ in range(3)]
        big = route_region(OVER * NE).rearrange("p (b e) -> p b e", b=OVER)
        far = route_region(T5 * NE).rearrange("p (t n) -> p t n", t=T5)
        eid = route_region(OVER + 1)
        eidI = route_region(OVER + 1, I32)
        nbI = route_region(NE, I32)
        pid = route_region(NBLK)
        none = route_region(NBLK)
        pidI = route_region(NBLK, I32)
        tokI = route_region(NBLK, I32)
        idg = [route_region(1, I32)[0:BS] for _ in range(NB3)]
        ids = [route_region(1, I32)[0:BS] for _ in range(NB3)]
        onesm = route_region(P)
        scrap = route_region(5)
        assert off[0] <= KD * NT
        banks = [ctx.enter_context(nc.psum_tensor(f"bank{i}", [P, 512], F32)) for i in range(BANKS)]

        vec_d = nc.dram_tensor("vec_d", (6, NS, 512), F32, kind="Internal").ap()
        hn_d = nc.dram_tensor("hn_d", (NT, D), F32, kind="Internal").ap()
        pair_d = nc.dram_tensor("pair_d", (PAIRS_E, D), F32, kind="Internal").ap()
        ys_d = nc.dram_tensor("ys_d", (NS, 512), F32, kind="Internal").ap()

        full = sem("psum_full")
        evac = {"v": sem("emptied_by_vector"), "a": sem("emptied_by_scalar")}
        s_const = sem("constants_loaded")
        s_par = sem("params_loaded")
        s_x = [sem(f"x_loaded{t}") for t in range(5)]
        s_mem = sem("mem_loaded")
        s_w = [sem(f"weights_loaded{i}") for i in range(3)]
        s_sq = sem("row_norms_ready")
        s_eps = sem("eps_set")
        s_xn = sem("rows_normed")
        s_vz = sem("vector_zeroed")
        v_ch = sem("vector_chain")
        a_ch = sem("scalar_chain")
        s_pch = sem("pool_chain")
        s_sa = sem("sample_products_ready")
        s_ssa = sem("sample_sums_ready")
        s_mix = sem("chunks_mixed")
        s_act = sem("lora_inputs_ready")
        s_kk = sem("key_squares_ready")
        s_rk = sem("bonus_products_ready")
        s_cs = sem("decay_sums_ready")
        s_ep = sem("decay_factors_ready")
        s_inv = sem("chunk_decays_inverted")
        s_tilde = sem("start_referred_operands_ready")
        s_prep = sem("rwkv_operands_ready")
        s_bv = sem("bonus_applied")
        s_st = sem("state_ready")
        s_svd = sem("sample_vectors_out")
        s_svl = sem("sample_vectors_in")
        s_ss = sem("sample_states_done")
        s_ysl = sem("sample_outputs_in")
        s_yc = sem("y_centred")
        s_fin = sem("y_final")
        s_mout = sem("mem_rows_written")
        s_shout = sem("shift_rows_written")
        s_out = sem("outputs_written")
        s_wkvo = sem("prompt_states_written")
        s_sink = sem("sinks_loaded")
        s_sso = sem("sample_states_written")
        s_cache = sem("window_rows_loaded")
        s_newkv = sem("new_window_rows_written")
        s_xr = [sem(f"x_reloaded{t}") for t in range(5)]
        s_kvr = [sem(f"memory_cache_loaded{i}") for i in range(4)]
        s_late = sem("late_memory_values_loaded")
        s_max = sem("row_maxima_ready")
        s_exp = sem("exponentials_ready")
        s_prob = sem("probabilities_ready")
        s_sq2 = sem("row_norms2_ready")
        s_xn2 = sem("rows_normed2")
        s_rope = sem("keys_rotated")
        s_rw = sem("router_weights_loaded")
        s_hn = [sem(f"normed_rows_written{i}") for i in range(2)]
        s_mk = sem("choices_ready")
        s_exp1 = sem("router_exponents_ready")
        s_exp2 = sem("router_exponentials_done")
        s_slot = sem("slots_ready")
        s_eid = sem("expert_ids_ready")
        s_idx = sem("row_indices_ready")
        s_wgu = [sem(f"gate_up_loaded{i}") for i in range(NW)]
        s_wd = [sem(f"down_loaded{i}") for i in range(NW)]
        s_osc = sem("beyond_rows_scattered")
        s_free = sem("beyond_block_may_start")
        s_ow = sem("beyond_weights_loaded")
        s_ogx = sem("beyond_rows_gathered")
        s_oP = sem("beyond_tensor_steps")
        s_oV = sem("beyond_vector_steps")
        s_oA = sem("beyond_scalar_steps")
        s_gx = [sem(f"rows_gathered{i}") for i in range(NB3)]
        s_ys = [sem(f"rows_scattered{i}") for i in range(NB3)]
        s_idc = sem("pool_index_copied")
        s_pX = sem("rows_transposed")
        s_pG = sem("gate_up_products")
        s_pA = sem("activation_transposed")
        s_pY = sem("down_products")
        s_vx = sem("rows_in_sbuf")
        s_as = sem("silu_done")
        s_vm = sem("activation_done")
        s_aa = sem("activation_in_sbuf")
        s_vy = sem("left_half_out")
        s_ay = sem("right_half_out")
        s_yl = [sem(f"pair_rows_loaded{i}") for i in range(5)]
        s_comb = sem("experts_added")
        s_sq3 = sem("row_norms3_ready")
        s_res = sem("results_ready")
        s_kvw = sem("prompt_window_rows_written")

        def bank(key):
            return banks[place[key] % BANKS]

        def reuse(pe, key):
            n = place[key]
            if n >= BANKS:
                e, k = rank[plan[n - BANKS][0]]
                pe.wait_ge(evac[e], k)
            return bank(key)

        def filled(eng, key):
            eng.wait_ge(full, place[key] + 1)
            return bank(key)

        def done(eng, key):
            e, k = rank[key]
            eng.wait_ge(evac[e], k)

        PARC = {}
        r = 0
        for name, n in PAR_ROWS:
            PARC[name] = r
            r += n

        def pcol(name, c):
            return par[:, PARC[name] + c:PARC[name] + c + 1]

        block = ctx.enter_context(nc.Block())

        w_in = A["w_in"][0].rearrange("(p k) n -> p k n", k=KD)
        loads = []
        for i, grp in enumerate((3, "w_ck", "w_cv", 1, 0, 2, 4)):
            if isinstance(grp, str):
                loads.append(((grp,), i % 3, A[grp][0].rearrange("(p k) n -> p k n", k=KD), KD))
            else:
                loads.append((("w_in", grp), i % 3, w_in[:, :, grp * 512:(grp + 1) * 512], KD))
        n_early = len(loads)
        w_o = A["w_out"][0].rearrange("(c p) n -> p c n", p=P)
        loads.append((("wo", 0), 0, w_o[:, 0:4, :], 4))
        loads.append((("wo", 1), 1, w_o[:, 4:8, :], 4))
        loads.append((("w_cq",), 2, A["w_cq"][0].rearrange("(p k) n -> p k n", k=KD), KD))
        loads.append((("w_co",), 0, A["w_co"][0].rearrange("(c p) n -> p c n", p=P), 4))
        slot_of, loaded_at, cnt = {}, {}, [0, 0, 0]
        for key, s, _, _ in loads:
            cnt[s] += 16
            slot_of[key], loaded_at[key] = s, cnt[s]

        def weights(key, k=KD):
            return ring[slot_of[key]].rearrange("p (k n) -> p k n", k=k)

        def weights_in(pe, key):
            pe.wait_ge(s_w[slot_of[key]], loaded_at[key])

        last_use = {("w_in", 3): ("proj", 15, 1), ("w_in", 1): ("proj", 7, 1), ("w_in", 0): ("proj", 3, 1),
                    ("w_in", 2): ("proj", 11, 1), ("w_in", 4): ("proj", 19, 1), ("w_ck",): ("mk", 1),
                    ("w_cv",): ("mv", 1), ("wo", 0): ("wo", 4, 1), ("wo", 1): ("wo", 4, 1), ("w_cq",): ("q", 3, 1)}

        @block.sync
        def _(sp):
            c = A["c_tables"]
            sp.dma_start(ident, c[:, 0:P]).then_inc(s_par, 16)
            r = 0
            for name, n in PAR_ROWS:
                src = A[name][0]
                if name == "r_k":
                    src = src.rearrange("h d -> (h d)")
                sp.dma_start(prow[r:r + n, :], src.rearrange("(r c) -> r c", c=P)).then_inc(s_par, 16)
                r += n
            sp.dma_start(srow[0:NS, :], A["state_rwkv_shift"][0]).then_inc(s_par, 16)
            for i, name in enumerate(("norm_mix", "norm_mem", "norm_cross", "norm_ffn")):
                sp.dma_start(gains[:, i, :], A[name][0].rearrange("(p k) -> p k", k=KD)).then_inc(s_par, 16)
            for t in range(TILES):
                sp.dma_start(x[:, t, :], A["x_prompt"][0, t * P:(t + 1) * P, :]).then_inc(s_x[t], 16)
            sp.dma_start(x[0:NS, 4, :], A["x_sample"][:, 0, :]).then_inc(s_x[4], 16)
            for i in range(3):
                key, s, src, k = loads[i]
                sp.dma_start(weights(key, k), src).then_inc(s_w[s], 16)
                if i == 0:
                    sp.dma_start(arena[:, P:at["gains"]], c[:, P:at["gains"]]).then_inc(s_const, 16)
                    sp.dma_start(memX, A["mem_prompt"][0].rearrange("(t p) n -> p t n", p=P)).then_inc(s_mem, 16)
                    sp.dma_start(lora[0:64, :], A["w_decay_up"][0]).then_inc(s_const, 16)
                    sp.dma_start(lora[64:128, :], A["w_a_up"][0]).then_inc(s_const, 16)
                    sp.dma_start(gup, A["w_g_up"][0]).then_inc(s_const, 16)
            row = A["attn_sink"]
            sp.dma_start(sinks[:, 0:H], bass.AP(row.tensor, row.offset, [[0, P], [1, H]])).then_inc(s_sink, 16)
            sp.dma_start(sinks[0:64, H:H + 1], bass.AP(row.tensor, row.offset, [[0, NS], [1, H], [1, 1]])) \
                .then_inc(s_sink, 16)
            for i in range(3, n_early):
                key, s, src, k = loads[i]
                prev = [l[0] for l in loads[:i] if l[1] == s][-1]
                sp.wait_ge(full, place[last_use[prev]] + 1)
                sp.dma_start(weights(key, k), src).then_inc(s_w[s], 16)
            done(sp, ("mk", 1))
            sp.dma_start(O["prompt_mem_k"][0, 0].rearrange("(t p) h d -> p t (h d)", p=P), mkS).then_inc(s_mout, 16)
            done(sp, ("mv", 1))
            sp.dma_start(O["prompt_mem_v"][0, 0].rearrange("(t p) h d -> p t (h d)", p=P), mv).then_inc(s_mout, 16)
            done(sp, ("shift_out", 3))
            sp.dma_start(O["prompt_shift"][0], shiftO[0:1, :]).then_inc(s_shout, 16)
            sp.dma_start(O["sample_shift"][0], shiftO[1:9, :]).then_inc(s_shout, 16)
            for kv in "kv":
                sp.dma_start(O[f"sample_swa_{kv}"][0, :, 0:P - 1], A[f"cache_swa_{kv}"][0, :, 1:P]) \
                    .then_inc(s_out, 16)
            sp.wait_ge(s_mout, 32)
            done(sp, ("mkT", 1))
            sp.dma_start(SS.rearrange("p i j -> p (i j)"),
                         A["state_rwkv_wkv"][0].rearrange("b h (u i) j -> (b h u) (i j)", u=2)).then_inc(s_svl, 16)
            done(sp, ("svec", 5))
            sp.dma_start(vec_d.rearrange("a b n -> b a n"), svt6).then_inc(s_svd, 16)
            sp.wait_ge(s_svd, 16)
            for a in range(5):
                src = vec_d[a].rearrange("b (h j) -> (b h) j", j=HD)
                src = bass.AP(src.tensor, src.offset, [[HD, NS * H], [0, 2], [1, HD]])
                sp.dma_start(sv[:, a, :], src).then_inc(s_svl, 16)
            sp.dma_start(svv, vec_d[5].rearrange("b (q i) -> (b q) i", i=32)).then_inc(s_svl, 16)
            sp.wait_ge(s_ss, 1)
            sp.dma_start(O["sample_wkv"][0].rearrange("b h (u i) j -> (b h u) (i j)", u=2),
                         SS.rearrange("p i j -> p (i j)")).then_inc(s_sso, 16)
            sp.wait_ge(s_ss, 2)
            sp.dma_start(ys_d.rearrange("b (q i) -> (b q) i", i=32), sy).then_inc(s_svd, 16)
            sp.wait_ge(s_svd, 32)
            sp.wait_ge(full, place[("Y", 2)] + 1)
            sp.dma_start(ysr, ys_d).then_inc(s_ysl, 16)
            sp.wait_ge(full, place[("WT", 3)] + 1)
            for t in range(TILES):
                sp.dma_start(x[:, t, :], A["x_prompt"][0, t * P:(t + 1) * P, :]).then_inc(s_xr[t], 16)
            sp.dma_start(x[0:NS, 4, :], A["x_sample"][:, 0, :]).then_inc(s_xr[4], 16)
            done(sp, ("kvout",))
            sp.dma_start(O["prompt_swa_k"][0, 0].rearrange("p h d -> p (h d)"), kvO[:, 0:P]).then_inc(s_kvw, 16)
            sp.dma_start(O["prompt_swa_v"][0, 0].rearrange("p h d -> p (h d)"), vtok[:, 3, :]).then_inc(s_kvw, 16)
            for i, kv in enumerate("kv"):
                sp.dma_start(O[f"sample_swa_{kv}"][0, :, P - 1].rearrange("b h d -> b (h d)"),
                             kvO[0:NS, (1 + i) * P:(2 + i) * P]).then_inc(s_newkv, 16)
            sp.wait_ge(s_newkv, 32)
            done(sp, ("wkvT",))
            for kv, dst in (("k", Kc), ("v", Vc)):
                sp.dma_start(dst[0:P - 1, :, :], A[f"cache_swa_{kv}"][0, :, 1:P].rearrange("b p h d -> p b (h d)")) \
                    .then_inc(s_cache, 16)
            for kv, dst in (("k", Kc), ("v", Vc)):
                sp.dma_start(dst[P - 1:P, :, :],
                             O[f"sample_swa_{kv}"][0:1, :, P - 1].rearrange("a b h d -> a b (h d)")) \
                    .then_inc(s_cache, 16)
            sp.dma_start(O["prompt_wkv"][0, 0].rearrange("h i j -> i h j"),
                         wkvO.rearrange("i (h j) -> i h j", h=H)).then_inc(s_wkvo, 16)
            done(sp, ("ysT",))
            for i in (n_early + 1, n_early):
                key, s, src, k = loads[i]
                if i == n_early + 1:
                    sp.wait_ge(s_wkvo, 16)
                sp.dma_start(weights(key, k), src).then_inc(s_w[s], 16)
            def memory_load(kv, b, dst, signal):
                src = A[f"cache_mem_{kv}"][0, b]
                sp.dma_start(dst, src.rearrange("(a p) h d -> p a (h d)", p=P)).then_inc(signal, 16)

            sp.wait_ge(s_fin, 1)
            for b in range(4):
                memory_load("k", b, kv_ring[b], s_kvr[b])
            for i in range(n_early + 2, n_early + 4):
                key, s, src, k = loads[i]
                if key == ("w_co",):
                    sp.wait_ge(full, place[("wo", 4, 1)] + 1)
                sp.dma_start(weights(key, k), src).then_inc(s_w[s], 16)
            sp.wait_ge(full, place[("q", 3, 1)] + 1)
            for b in range(4, NS):
                if b == 6:
                    for m in range(4, NS):
                        memory_load("v", m, late[m - 4], s_late)
                sp.wait_ge(full, place[("ckT", b - 4, 1)] + 1)
                memory_load("k", b, kv_ring[b % 4], s_kvr[b % 4])
            for b in range(4):
                sp.wait_ge(full, place[("ckT", b + 4, 1)] + 1)
                memory_load("v", b, kv_ring[b], s_kvr[b])
            sp.dma_start(wr[:, :, 0:4], A["w_group_router"][0].rearrange("(p k) n -> p k n", k=KD)).then_inc(s_rw, 16)
            sp.dma_start(wr[:, :, 4:36], A["w_expert_router"][0].rearrange("(p k) n -> p k n", k=KD)).then_inc(s_rw, 16)
            b1, b2, b3 = A["b_group_router"], A["b_expert_router"], A["norm_final"]
            sp.dma_start(rbias[:, 0:4], bass.AP(b1.tensor, b1.offset, [[0, P], [1, 4]])).then_inc(s_rw, 16)
            sp.dma_start(rbias[:, 4:36], bass.AP(b2.tensor, b2.offset, [[0, P], [1, NE]])).then_inc(s_rw, 16)
            sp.dma_start(gfin, bass.AP(b3.tensor, b3.offset, [[0, P], [1, D]])).then_inc(s_rw, 16)
            wge = A["w_exp_gate"][0].rearrange("g e (p k) f -> (g e) p (k f)", k=KD)
            wue = A["w_exp_up"][0].rearrange("g e (p k) f -> (g e) p (k f)", k=KD)
            wde = A["w_exp_down"][0].rearrange("g e f d -> (g e) f d")

            def load_expert(i, e, gu, dn):
                sp.dma_start(we[i][:, 0, :], wge[bass.ds(e, 1)].rearrange("a p n -> (a p) n")).then_inc(gu, 16)
                sp.dma_start(we[i][:, 1, :], wue[bass.ds(e, 1)].rearrange("a p n -> (a p) n")).then_inc(gu, 16)
                sp.dma_start(we[i][:, 2, :], wde[bass.ds(e, 1)].rearrange("a p n -> (a p) n")).then_inc(dn, 16)

            for t in range(T5):
                R = tile_rows(t)
                sp.wait_ge(s_xn2, 6 + t)
                sp.dma_start(hn_d[t * P:t * P + R, :], xn[t % 2][0:R, :]).then_inc(s_hn[t % 2], 16)
            sp.wait_ge(full, place[("wc", 4, 1)] + 1)
            for i in range(6):
                load_expert(i, i, s_wgu[i], s_wd[i])
            sp.wait_ge(s_hn[0], 48)
            sp.wait_ge(s_hn[1], 32)
            sp.wait_ge(full, place[("xT3", 4, 1)] + 1)
            for i in range(6, 8):
                load_expert(i, i, s_wgu[i], s_wd[i])
            with sp.Fori(1, NE // NW) as it:
                for i in range(NW):
                    sp.wait_ge(s_pY, it * NW + (i + 1 - NW))
                    sp.wait_ge(s_eid, 1)
                    load_expert(i, it * NW + i, s_wgu[i], s_wd[i])
            for i in range(NB3):
                sp.wait_ge(s_ys[i], 16 * (NE // NB3))
            sp.wait_ge(s_pY, NE)
            beyond = sp.value_load(eidI[0:1, OVER:OVER + 1], min_val=0, max_val=OVER)
            with sp.If(beyond > 0):
                with sp.Fori(0, OVER) as n:
                    sp.wait_ge(s_free, n + 1)
                    sp.wait_ge(s_eid, 1)
                    e = sp.value_load(eidI[0:1, bass.ds(n, 1)], min_val=0, max_val=NE - 1)
                    load_expert(0, e, s_ow, s_ow)
                sp.wait_ge(s_free, OVER + 1)
            with sp.Else():
                sp.wait_ge(s_pY, NE)
            prow_d = pair_d.rearrange("(t j) d -> t j d", j=2)
            for t in range(T5):
                R = tile_rows(t)
                sp.dma_start(ydt[t][0:R, :, :], prow_d[t * P:t * P + R]).then_inc(s_yl[t], 16)
            for t in range(T5):
                R = tile_rows(t)
                sp.wait_ge(s_res, t + 1)
                dst = O["y_prompt"][0, t * P:(t + 1) * P, :] if t < TILES else O["y_sample"][:, 0, :]
                sp.dma_start(dst, x[0:R, t, :]).then_inc(s_out, 16)
            sp.wait_ge(s_out, 16 * (2 + T5))

        @block.gpsimd
        def _(pool):
            pool.wait_ge(s_inv, 1)
            pool.wait_ge(s_prep, 4)
            pool.wait_ge(full, place[("proj", 19, 1)] + 1)
            for n in range(NCH):
                cols = slice(n * CH, (n + 1) * CH)
                inv = small[:, 8:40].rearrange("p (c n) -> p c n", c=4)[:, :, n:n + 1].to_broadcast([P, 4, CH])
                pool.tensor_tensor(Bt[:, :, cols], B1[:, :, cols], inv, ALU.mult).then_inc(s_tilde, 1)
                pool.tensor_tensor(Kt[:, :, cols], PR[:, 4:8, 1 + n * CH:1 + (n + 1) * CH], inv, ALU.mult) \
                    .then_inc(s_tilde, 1)

            chained = [0]

            def link(ins):
                chained[0] += 1
                ins.then_inc(s_pch, 1)
                pool.wait_ge(s_pch, chained[0])

            tt = pool.tensor_tensor

            pool.wait_ge(s_svl, 16 * 7)
            a_, b_, k_, w_, r_ = [sv[:, i, :].unsqueeze(1).to_broadcast([P, 32, HD]) for i in range(5)]
            tt(Stmp, SS, a_, ALU.mult).then_inc(s_sa, 1)
            link(tt(SS, SS, w_, ALU.mult))
            pool.wait_ge(s_ssa, 1)
            link(tt(Stmp, b_, ssa.unsqueeze(2).to_broadcast([P, 32, HD]), ALU.mult))
            link(tt(SS, SS, Stmp, ALU.add))
            link(tt(Stmp, k_, svv.unsqueeze(2).to_broadcast([P, 32, HD]), ALU.mult))
            tt(SS, SS, Stmp, ALU.add).then_inc(s_ss, 1)

            pool.wait_ge(s_idx, 1)
            for i in range(2):
                pool.wait_ge(s_hn[i], 16 * (3 - i))

            def wait(sem, value):
                pool.wait_ge(sem, value)
                pool.wait_ge(s_idx, 1)

            def carried(sem, value, cell=0):
                pool.wait_ge(sem, value)
                return pool.tensor_tensor(scrap[:, cell:cell + 1], scrap[:, 1:2], scrap[:, 1:2], ALU.add)

            def index_in(value):
                carried(s_idc, value)

            pool.memset(scrap, 0.0)

            def gather(i, b):
                pool.tensor_copy(idg[i], tokI[0:BS, bass.ds(b, 1)]).then_inc(s_idc, 1)

            def scatter_index(i, b):
                pool.tensor_copy(ids[i], pidI[0:BS, bass.ds(b, 1)]).then_inc(s_idc, 1)

            def start_gather(i, signal=None):
                pool.indirect_dma_start(xg[i][0:BS], None, hn_d, bass.IndirectOffsetOnAxis(idg[i].bitcast(U32), 0),
                                        bounds_check=NT - 1, oob_is_err=False).then_inc(signal or s_gx[i], 16)

            def start_scatter(i):
                pool.indirect_dma_start(pair_d, bass.IndirectOffsetOnAxis(ids[i].bitcast(U32), 0), yb[i], None,
                                        bounds_check=PAIRS_E - 1, oob_is_err=False).then_inc(s_ys[i], 16)

            for i in range(NB3):
                gather(i, i)
                pool.wait_ge(s_idc, i + 1)
                start_gather(i)
            with pool.Fori(1, NE // NB3) as it:
                for i in range(NB3):
                    wait(s_pX, it * NB3 + (i + 1 - NB3))
                    wait(s_gx[i], it * 16)
                    gather(i, it * NB3 + i)
                    index_in(it * (2 * NB3) + (2 * i + 1 - NB3))
                    start_gather(i)
                    wait(s_vy, it * NB3 + (i + 1 - NB3))
                    wait(s_ay, it * NB3 + (i + 1 - NB3))
                    scatter_index(i, it * NB3 + (i - NB3))
                    index_in(it * (2 * NB3) + (2 * i + 2 - NB3))
                    start_scatter(i)
            last = NE // NB3 - 1
            for i in range(NB3):
                pool.wait_ge(s_vy, NB3 * last + i + 1)
                pool.wait_ge(s_ay, NB3 * last + i + 1)
                pool.wait_ge(s_ys[i], 16 * last)
                scatter_index(i, NB3 * last + i)
                pool.wait_ge(s_idc, 2 * NB3 * last + NB3 + i + 1)
                start_scatter(i)
            pool.wait_ge(s_ys[0], 16 * (NE // NB3))
            pool.wait_ge(s_pX, NE)
            beyond = pool.value_load(eidI[0:1, OVER:OVER + 1], min_val=0, max_val=OVER)
            with pool.If(beyond > 0):
                pool.memset(scrap, 0.0).then_inc(s_free, 1)
                with pool.Fori(0, OVER) as n:
                    wait(s_free, n + 1)
                    pool.tensor_copy(idg[0], tokI[0:BS, bass.ds(n + NE, 1)]).then_inc(s_idc, 1)
                    pool.tensor_copy(ids[0], pidI[0:BS, bass.ds(n + NE, 1)]).then_inc(s_idc, 1)
                    index_in(n * 2 + (2 * NE + 2))
                    start_gather(0, s_ogx)
                    carried(s_oV, n * 3 + 3, 2)
                    carried(s_oA, n * 3 + 3, 3)
                    pool.indirect_dma_start(pair_d, bass.IndirectOffsetOnAxis(ids[0].bitcast(U32), 0), yb[0], None,
                                            bounds_check=PAIRS_E - 1, oob_is_err=False).then_inc(s_osc, 16)
                    carried(s_osc, n * 16 + 16, 4).then_inc(s_free, 1)
            with pool.Else():
                pool.memset(scrap, 0.0)

        @block.tensor
        def _(pe):
            last = [None]

            def mm(out, lhsT, rhs, start=True, stop=True):
                last[0] = pe.matmul(out, lhsT, rhs, start=start, stop=stop, skip_group_check=True)

            def tr(out, in_):
                n = in_.shape[0]
                last[0] = pe.transpose(out, in_, ident[0:n, 0:n])

            def close():
                last[0].then_inc(full, 1)

            pe.wait_ge(s_par, 16 * 14)
            o = reuse(pe, ("par",))
            tr(o[:, 0:42], prow[0:42, :])
            close()
            o = reuse(pe, ("shift_in",))
            for j in range(RW):
                tr(o[:, NS * j:NS * j + NS], srow[0:NS, j * P:(j + 1) * P])
            close()
            for t in range(TILES + 1):
                R = tile_rows(t)
                pe.wait_ge(s_xn, t + 1)
                for i in range(2):
                    o = reuse(pe, ("xT", t, i))
                    xk = x[0:R, t, :].rearrange("p (q k) -> p k q", k=KD)
                    for k in range(4):
                        tr(o[:, k * P:k * P + R], xk[:, 4 * i + k, :])
                    close()

            def project(j):
                grp = j // 4
                key = ("w_in", grp)
                weights_in(pe, key)
                w = weights(key)
                for s in range(2):
                    o = reuse(pe, ("proj", j, s))
                    for k in range(KD):
                        mm(o[:, 0:HALF], w[:, k, (j % 4) * P:(j % 4 + 1) * P], hA[:, k, s * HALF:(s + 1) * HALF],
                           k == 0, k == KD - 1)
                    close()

            def memory_rows_T():
                for t in range(2):
                    pe.wait_ge(s_xn, 6 + t)
                    for i in range(2):
                        o = reuse(pe, ("mT", t, i))
                        xk = memX[:, t, :].rearrange("p (q k) -> p k q", k=KD)
                        for k in range(4):
                            tr(o[:, k * P:(k + 1) * P], xk[:, 4 * i + k, :])
                        close()

            def lora_products():
                pe.wait_ge(s_const, 64)
                pe.wait_ge(s_act, 1)
                for key, b in (("lora_w", 0), ("lora_a", 64)):
                    for c in range(4):
                        for s in range(2):
                            o = reuse(pe, (key, c, s))
                            mm(o[:, 0:HALF], lora[b:b + 64, c * P:(c + 1) * P],
                               PR[b:b + 64, 12, 1 + s * HALF:1 + (s + 1) * HALF])
                            close()

            def memory_products():
                done(pe, ("mT", 1, 1))
                for key, wk in (("mk", ("w_ck",)), ("mv", ("w_cv",))):
                    weights_in(pe, wk)
                    for t in range(2):
                        o = reuse(pe, (key, t))
                        for k in range(KD):
                            mm(o[:, :], memT[:, k, t * P:(t + 1) * P], weights(wk)[:, k, :], k == 0, k == KD - 1)
                        close()
                for t in range(2):
                    done(pe, ("mk", t))
                    o = reuse(pe, ("mkT", t))
                    for h in range(XH):
                        tr(o[:, h * P:(h + 1) * P], mkS[:, t, h * P:(h + 1) * P])
                    close()

            def head_sums(c):
                pe.wait_ge(s_kk, c + 1)
                for s in range(2):
                    o = reuse(pe, ("norm_k", c, s))
                    mm(o[:, 0:HALF], bones, sq[c % 2][:, s * HALF:(s + 1) * HALF])
                    close()
                pe.wait_ge(s_rk, c + 1)
                for s in range(2):
                    o = reuse(pe, ("bonus", c, s))
                    mm(o[:, 0:HALF], bones, B1[:, c, s * HALF:(s + 1) * HALF])
                    close()

            done(pe, ("xT", 4, 1))
            for what, n in FRONT_ORDER:
                if what == "proj":
                    project(n)
                elif what == "mT":
                    memory_rows_T()
                elif what == "lora":
                    lora_products()
                elif what == "mem":
                    memory_products()
                elif what == "sums":
                    head_sums(n)
            pe.wait_ge(s_mix, 14)
            for i in range(4):
                o = reuse(pe, ("shift_out", i))
                for j in range(4 * i, min(4 * i + 4, RW)):
                    tr(o[0:9, (j % 4) * P:(j % 4 + 1) * P], saved[:, j, :])
                close()
            pe.wait_ge(s_prep, 4)
            pe.wait_ge(s_prep, 4)
            for i in range(6):
                o = reuse(pe, ("svec", i))
                for c in range(4):
                    src = (B0[:, c, SEQ:NT], B1[:, c, SEQ:NT], PR[:, 4 + c, 1 + SEQ:1 + NT], wS[:, c, :],
                           PR[:, c, 1 + SEQ:1 + NT], PR[:, 8 + c, 1 + SEQ:1 + NT])[i]
                    tr(o[0:NS, c * P:(c + 1) * P], src)
                close()
            for t in range(TILES):
                o = reuse(pe, ("tokV", t))
                for c in range(4):
                    tr(o[:, c * P:(c + 1) * P], PR[:, 8 + c, 1 + t * P:1 + (t + 1) * P])
                close()

            def by_token(t, _):
                for i, src in enumerate((B0, B1, PR[:, 4:8, :])):
                    o = reuse(pe, ("tok", t, i))
                    off = 1 if i == 2 else 0
                    for c in range(4):
                        tr(o[:, c * P:(c + 1) * P], src[:, c, off + t * P:off + (t + 1) * P])
                    close()

            def chunk_products(t, half):
                lo, hi = t * P, (t + 1) * P
                pe.wait_ge(s_tilde, 4 * (t + 1))
                for h in range(4 * half, 4 * half + 4):
                    c, b = h // 2, 64 * (h % 2)
                    o = reuse(pe, ("AB", t, h))
                    for i, src in enumerate((Bt, Kt)):
                        mm(o[:, i * 256:i * 256 + P], src[b:b + 64, c, lo:hi], B0[b:b + 64, c, lo:hi])
                        mm(o[:, i * 256 + P:i * 256 + 256], src[b:b + 64, c, lo:hi], PR[b:b + 64, c, 1 + lo:1 + hi])
                    close()

            def first_N(t, _):
                for q in range(2):
                    o = reuse(pe, ("N0", t, q))
                    for h in range(4 * q, 4 * q + 4):
                        done(pe, ("AB", t, h))
                        tr(o[:, (h % 4) * P:(h % 4 + 1) * P], ABs[t % 2][:, h, 0, :])
                    close()

            def level(t, k):
                def M(h):
                    return ABs[t % 2][:, h, 0, :] if k == 0 else Mi[k % 2][:, h, :]

                for q in range(2):
                    hs = range(4 * q, 4 * q + 4)
                    if k == 0:
                        done(pe, ("N0", t, q))
                    else:
                        done(pe, ("NN", t, q, k - 1))
                        if k < 5:
                            done(pe, ("MM", t, q, k - 1))
                        if k == 1:
                            pe.wait_ge(s_st, 2 * t + q + 1)
                        else:
                            done(pe, ("XM", t, q, k - 1))
                        o = reuse(pe, ("XM", t, q, k))
                        for h in hs:
                            mm(o[:, (h % 4) * P:(h % 4 + 1) * P], Ni[k % 2][:, h, :], Xi[:, h, :])
                        close()
                    if k < 4:
                        o = reuse(pe, ("MM", t, q, k))
                        for h in hs:
                            mm(o[:, (h % 4) * P:(h % 4 + 1) * P], Ni[k % 2][:, h, :], M(h))
                        close()
                    if k < 5:
                        o = reuse(pe, ("NN", t, q, k))
                        for h in hs:
                            mm(o[:, (h % 4) * P:(h % 4 + 1) * P], M(h), Ni[k % 2][:, h, :])
                        close()

            def last_products(t, _):
                o = reuse(pe, ("akv", t))
                done(pe, ("tokV", t))
                for h in range(H):
                    mm(o[:, h * HD:(h + 1) * HD], ABs[t % 2][:, h, 2, :], tokV[:, t, h * HD:(h + 1) * HD])
                close()
                done(pe, ("akv", t))
                done(pe, ("XM", t, 1, 5))
                o = reuse(pe, ("G", t))
                for h in range(H):
                    mm(o[:, h * HD:(h + 1) * HD], Xi[:, h, :], akv[:, h * HD:(h + 1) * HD])
                close()
                o = reuse(pe, ("WT", t))
                done(pe, ("tok", t, 0))
                for h in range(H):
                    c, b = h // 2, 64 * (h % 2)
                    mm(o[b:b + 64, c * P:(c + 1) * P], tokXs[0][0][:, h * HD:(h + 1) * HD], Xi[:, h, :])
                close()

            def updates(t, u):
                tk, n = 64 * u, 2 * t + u
                done(pe, ("WT", t))
                if n == 0:
                    pe.wait_ge(s_vz, 1)
                elif u == 0:
                    done(pe, ("S", t - 1, 1))
                else:
                    done(pe, ("S", t, 0))
                for e in range(2):
                    o = reuse(pe, ("U", t, u, e))
                    b = 64 * e
                    for c in range(4):
                        mm(o[tk:tk + 64, c * HD:(c + 1) * HD], WT[b:b + 64, c, tk:tk + 64], ST[b:b + 64, n, c, :])
                    close()

            def state(t, u):
                tk = 64 * u
                done(pe, ("tok", t, 2))
                done(pe, ("U", t, u, 1))
                o = reuse(pe, ("S", t, u))
                for h in range(H):
                    c, b = h // 2, 64 * (h % 2)
                    hc = slice(h * HD, (h + 1) * HD)
                    so = o[b:b + 64, c * HD:(c + 1) * HD]
                    mm(so, tokXs[t % 2][2][tk:tk + 64, hc], tokV[tk:tk + 64, t, hc], True, False)
                    mm(so, tokXs[t % 2][1][tk:tk + 64, hc], Ut[tk:tk + 64, hc], False, True)
                close()

            def outputs(t, _):
                lo = 1 + t * P
                o = reuse(pe, ("Y", t))
                for h in range(H):
                    c, b = h // 2, 64 * (h % 2)
                    hc = slice(h * HD, (h + 1) * HD)
                    yo = o[b:b + 64, c * P:(c + 1) * P]
                    mm(yo, tokV[:, t, hc], ABs[t % 2][:, h, 3, :], c == 0, False)
                    mm(yo, Ut[:, hc], ABs[t % 2][:, h, 1, :], False, False)
                    for u in range(2):
                        mm(o[b:b + 64, c * P + 64 * u:c * P + 64 * u + 64], ST[b:b + 64, 2 * t + u, c, :],
                           PR[b:b + 64, c, lo + 64 * u:lo + 64 * u + 64], False, True)
                close()

            def rotated_query(c, s):
                o = reuse(pe, ("rq", c, s))
                mm(o[:, 0:HALF], sel[:, 0, :], SQ[:, c, s * HALF:(s + 1) * HALF])
                close()

            def rotated_key(i, s):
                for key, a in (("rka", 1), ("rkb", 3)):
                    o = reuse(pe, (key, i, s))
                    mm(o[:, 0:HALF], sel[:, a + i, :], SQ[:, 4, s * HALF:(s + 1) * HALF])
                    close()

            def window_values(*_):
                o = reuse(pe, ("vtok",))
                for t in range(TILES):
                    tr(o[:, t * P:(t + 1) * P], SQ[:, 5, t * P:(t + 1) * P])
                close()
                pe.wait_ge(s_rope, 1)
                o = reuse(pe, ("kvout",))
                for i in range(2):
                    tr(o[:, i * HD:(i + 1) * HD], RK[i][0:HD, 3 * P:4 * P])
                    tr(o[0:NS, P + i * HD:P + (i + 1) * HD], RK[i][0:HD, SEQ:NT])
                tr(o[0:NS, 2 * P:3 * P], SQ[:, 5, SEQ:NT])
                close()

            def window_scores(t, _):
                k0 = max(t - 1, 0) * P
                W = (t + 1) * P - k0
                for e in range(2):
                    b = 64 * e
                    for i in range(2):
                        o = reuse(pe, ("s", t, e, i))
                        for n in range(2):
                            mm(o[:, n * W:(n + 1) * W], SQ[b:b + 64, 2 * i + n, t * P:(t + 1) * P],
                               RK[i][b:b + 64, k0:k0 + W])
                        close()

            def window_outputs(t, _):
                done(pe, ("vtok",))
                pe.wait_ge(s_prob, t + 1)
                na = 1 if t == 0 else 2
                sm = SmW[t % 2].rearrange("p (h s) -> p h s", h=H)
                for i in range(4):
                    o = reuse(pe, ("pT", t, i))
                    for n in range(2):
                        for a in range(na):
                            tr(o[:, (2 * n + a) * P:(2 * n + a + 1) * P], sm[:, 2 * i + n, a * P:(a + 1) * P])
                    close()
                done(pe, ("pT", t, 3))
                o = reuse(pe, ("o", t))
                for h in range(H):
                    c, b, g = h // 2, 64 * (h % 2), h // 4
                    for a in range(na):
                        mm(o[b:b + 64, c * P:(c + 1) * P], vtok[:, t + 1 - na + a, g * HD:(g + 1) * HD],
                           PTa[:, h, a, :], a == 0, a == na - 1)
                close()

            steps = {"rq": rotated_query, "rk": rotated_key, "vk": window_values, "ws": window_scores,
                     "wp": window_outputs, "sample": lambda *_: None,
                     "tok": by_token, "AB": chunk_products, "N0": first_N, "level": level, "fin": last_products,
                     "U": updates, "S": state, "Y": outputs}
            for what, t, n in RECUR_ORDER:
                steps[what](t, n)
            o = reuse(pe, ("wkvT",))
            done(pe, ("S", 3, 1))
            for c in range(4):
                tr(o[0:64, c * P:(c + 1) * P], ST[:, 8, c, :])
            close()
            pe.wait_ge(s_ysl, 16)
            o = reuse(pe, ("ysT",))
            for c in range(4):
                tr(o[:, c * NS:(c + 1) * NS], ysr[:, c * P:(c + 1) * P])
            close()
            done(pe, ("ysT",))
            done(pe, ("Y", 3))
            for c in range(4):
                for s in range(2):
                    o = reuse(pe, ("mean", c, s))
                    mm(o[:, 0:HALF], bones, yT[:, c, s * HALF:(s + 1) * HALF])
                    close()
            for c in range(4):
                for s in range(2):
                    o = reuse(pe, ("gate", c, s))
                    mm(o[:, 0:HALF], gup[:, c * P:(c + 1) * P], PR[:, 13, 1 + s * HALF:1 + (s + 1) * HALF])
                    close()
            for e in range(2):
                o = reuse(pe, ("qd", e))
                mm(o[:, 0:32].rearrange("p (c b) -> p c b", c=4), sel[:, 1 + e, :], SQ[:, 0:4, SEQ:NT])
                close()
            for c in range(4):
                pe.wait_ge(s_yc, c + 1)
                for s in range(2):
                    o = reuse(pe, ("var", c, s))
                    mm(o[:, 0:HALF], bones, ysq[:, c, s * HALF:(s + 1) * HALF])
                    close()
            pe.wait_ge(s_cache, 64)
            for i in range(2):
                o = reuse(pe, ("kT", i))
                for m in range(4):
                    tr(o[:, m * P:(m + 1) * P], Kc[:, 4 * i + m, :])
                close()
            done(pe, ("kT", 1))
            done(pe, ("qd", 1))
            for g in range(2):
                o = reuse(pe, ("ss", g))
                for b in range(NS):
                    mm(o[:, 4 * b:4 * b + 4], kTs[64 * g:64 * g + 64, b, :],
                       QD[64 * g:64 * g + 64, b, 2 * g:2 * g + 2, :].rearrange("p c e -> p (c e)"))
                close()
            done(pe, ("o", 3))
            weights_in(pe, ("wo", 1))

            def output_share(t, n, chunks, start):
                R = tile_rows(t)
                o = reuse(pe, ("wo", t, n))
                for c in chunks:
                    mm(o[0:R, :], yT[:, c, t * P:t * P + R],
                       weights(("wo", c // 4), 4)[:, c % 4, n * 512:(n + 1) * 512], start and c == chunks[0],
                       c == 3)

            windows, recurrence = range(4, 8), range(4)
            output_share(0, 0, windows, True)
            done(pe, ("ss", 1))
            o = reuse(pe, ("ssT",))
            tr(o[0:64, 0:P], sT)
            close()
            output_share(0, 1, windows, True)
            output_share(1, 0, windows, True)
            pe.wait_ge(s_prob, 5)
            o = reuse(pe, ("spT",))
            tr(o[:, 0:64], SmW[0][0:64, 0:P])
            close()
            done(pe, ("spT",))
            o = reuse(pe, ("so",))
            for e in range(2):
                for b in range(NS):
                    for g in range(2):
                        mm(o[64 * e:64 * e + 64, 0:32].rearrange("p (c b) -> p c b", c=4)[:, 2 * g:2 * g + 2, b],
                           Vc[:, b, g * HD:(g + 1) * HD],
                           pTs.rearrange("p (b g n e) -> p b g n e", b=NS, g=2, n=2)[:, b, g, :, e])
                close() if e else None
            done(pe, ("so",))
            pe.wait_ge(s_fin, 1)
            weights_in(pe, ("wo", 0))
            def rows_transposed(key, first, t):
                R = tile_rows(t)
                pe.wait_ge(s_xn2, first + t + 1)
                for i in range(2):
                    o = reuse(pe, (key, t, i))
                    xk = xn[t % 2][0:R, :].rearrange("p (q k) -> p k q", k=KD)
                    for k in range(4):
                        tr(o[:, k * P:k * P + R], xk[:, 4 * i + k, :])
                    close()

            for t in range(TILES + 1):
                for n in range(2):
                    if (t, n) not in ((0, 0), (0, 1), (1, 0)):
                        output_share(t, n, windows, True)
                    output_share(t, n, recurrence, False)
                    close()
                if t >= 1:
                    rows_transposed("xT2", 0, t - 1)
            rows_transposed("xT2", 0, TILES)
            weights_in(pe, ("w_cq",))
            done(pe, ("xT2", 4, 1))
            for h in range(XH):
                for s in range(2):
                    o = reuse(pe, ("q", h, s))
                    for k in range(KD):
                        mm(o[:, 0:HALF], weights(("w_cq",))[:, k, h * P:(h + 1) * P],
                           hA[:, k, s * HALF:(s + 1) * HALF], k == 0, k == KD - 1)
                    close()
            done(pe, ("q", 3, 1))

            def prompt_scores(t):
                for i in range(2):
                    o = reuse(pe, ("xs", t, i))
                    for n in range(2):
                        mm(o[:, n * MT:(n + 1) * MT], qT[:, 2 * i + n, t * P:(t + 1) * P], mkT[:, 2 * i + n, :])
                    close()

            def prompt_values(t):
                pe.wait_ge(s_prob, 6 + t)
                sm = Sm[(5 + t) % 2][:, 0:1024].rearrange("p (h s) -> p h s", h=XH)
                for i in range(2):
                    o = reuse(pe, ("xpT", t, i))
                    for n in range(2):
                        for a in range(2):
                            tr(o[:, (2 * n + a) * P:(2 * n + a + 1) * P], sm[:, 2 * i + n, a * P:(a + 1) * P])
                    close()
                done(pe, ("xpT", t, 1))
                o = reuse(pe, ("xo", t))
                for h in range(XH):
                    for a in range(2):
                        mm(o[:, h * P:(h + 1) * P], mv[:, a, h * P:(h + 1) * P], PTc[:, h, a, :], a == 0, a == 1)
                close()

            def keys_T(b):
                pe.wait_ge(s_kvr[b % 4], 16 * (b // 4 + 1))
                for st in range(2):
                    o = reuse(pe, ("ckT", b, st))
                    for h in range(XH):
                        tr(o[:, h * P:(h + 1) * P], kv_ring[b % 4][:, st, h * P:(h + 1) * P])
                    close()

            def sample_scores(b):
                done(pe, ("ckT", b, 1))
                o = reuse(pe, ("cs", b))
                for st in range(2):
                    for h in range(XH):
                        mm(o[:, 4 * st + h:4 * st + h + 1], KT[b % 2][:, h, st, :], qT[:, h, SEQ + b:SEQ + b + 1])
                close()

            for what, n in CROSS_ORDER:
                {"xs": prompt_scores, "xp": prompt_values, "ckT": keys_T, "cs": sample_scores}[what](n)
            done(pe, ("cs", 7))
            o = reuse(pe, ("csT",))
            for st in range(2):
                tr(o[0:32, st * P:(st + 1) * P], csS[:, st, :])
            close()
            pe.wait_ge(s_prob, 10)
            o = reuse(pe, ("cpT",))
            for st in range(2):
                tr(o[:, st * 32:(st + 1) * 32], Sm[1][0:32, st * P:(st + 1) * P])
            close()
            done(pe, ("cpT",))
            o = reuse(pe, ("co",))
            for b in range(NS):
                if b < 4:
                    pe.wait_ge(s_kvr[b], 48)
                elif b == 4:
                    pe.wait_ge(s_late, 64)
                for h in range(XH):
                    for st in range(2):
                        mm(o[:, 4 * b + h:4 * b + h + 1], values_of(b)[:, st, h * P:(h + 1) * P],
                           cpS[:, st, 4 * b + h:4 * b + h + 1], st == 0, st == 1)
            close()
            done(pe, ("co",))
            done(pe, ("xo", 3))
            weights_in(pe, ("w_co",))
            for t in range(TILES + 1):
                R = tile_rows(t)
                for n in range(2):
                    o = reuse(pe, ("wc", t, n))
                    for h in range(XH):
                        mm(o[0:R, :], yT[:, h, t * P:t * P + R], weights(("w_co",), 4)[:, h, n * 512:(n + 1) * 512],
                           h == 0, h == XH - 1)
                    close()
                if t >= 1:
                    rows_transposed("xT3", 5, t - 1)
            rows_transposed("xT3", 5, TILES)
            done(pe, ("xT3", 4, 1))
            pe.wait_ge(s_rw, 16 * 5)
            for t in range(T5):
                R = tile_rows(t)
                o = reuse(pe, ("route", t))
                for k in range(KD):
                    mm(o[0:R, 0:36], hA[:, k, t * P:t * P + R], wr[:, k, :], k == 0, k == KD - 1)
                close()
            pe.wait_ge(s_mk, 1)
            o = reuse(pe, ("ranks",))
            for t in range(T5):
                later = T5 - t
                mm(o[:, (t + 1) * NE:(T5 + 1) * NE].rearrange("p (u e) -> p u e", u=later), onesm,
                   Mk[:, t, :].unsqueeze(1).to_broadcast([P, later, NE]), t == 0, t == T5 - 1)
                mm(o[:, t * NE:(t + 1) * NE], tri, Mk[:, t, :], False, True)
            close()
            pe.wait_ge(s_slot, 1)
            o = reuse(pe, ("slots",))
            for j in range(J):
                mm(o[0:BS, 0:NBLK], in_row[:, j, :], in_block[:, j, :], j == 0, j == J - 1)
            close()
            done(pe, ("slots",))
            bX, bG, bA = banks[0], [banks[2], banks[6]], banks[3]
            bY = [banks[4], banks[5]]

            def rows_T(i, b, r):
                pe.wait_ge(s_gx[i % NB3], r * 32 + (i // NB3 * 16 + 16))
                if b is not None:
                    pe.wait_ge(s_vx, b)
                transposes(i % NB3).then_inc(s_pX, 1)

            def transposes(i):
                xk = xg[i].rearrange("p (q k) -> p k q", k=KD)
                for k in range(KD):
                    n = P if k == 0 else BS
                    ins = pe.transpose(bX[:, k * BS:k * BS + n], xk[0:n, k, :], ident[0:n, 0:n])
                return ins

            def gate_up_products(i):
                for k in range(KD):
                    ins = pe.matmul(bG[i % 2][0:BS, 0:2 * FH].rearrange("p (a f) -> p a f", a=2), xTe[i % 2][:, k, :],
                                    we[i][:, 0:2, k * FH:(k + 1) * FH], start=k == 0, stop=k == KD - 1)
                return ins

            def down_products(i):
                for n in range(2):
                    ins = pe.matmul(bY[n][0:BS, :], actT, we[i][:, 2, n * 512:(n + 1) * 512], start=True, stop=True)
                return ins

            def gate_up(i, b, r):
                pe.wait_ge(s_wgu[i], r * 32 + 32)
                pe.wait_ge(s_vx, b + 1)
                gate_up_products(i).then_inc(s_pG, 1)

            def act_T(b):
                pe.wait_ge(s_vm, b + 1)
                pe.transpose(bA[:, 0:P], act_f, ident).then_inc(s_pA, 1)

            def down(i, b, r, first=False):
                pe.wait_ge(s_aa, b + 1)
                pe.wait_ge(s_wd[i], r * 16 + 16)
                if not first:
                    pe.wait_ge(s_vy, b)
                    pe.wait_ge(s_ay, b)
                down_products(i).then_inc(s_pY, 1)

            rows_T(0, None, 0)
            rows_T(1, 1, 0)
            gate_up(0, 0, 0)
            rounds = NE // NW

            def pe_round(it, first, final):
                for i in range(NW):
                    b = it * NW + i
                    if not (final and i == NW - 1):
                        gate_up((i + 1) % NW, b + 1, it if i < NW - 1 else it + 1)
                    act_T(b)
                    if not (final and i >= NW - 2):
                        rows_T((i + 2) % NW, b + 2, it if i < NW - 2 else it + 1)
                    down(i, b, it, first and i == 0)

            pe_round(0, True, False)
            with pe.Fori(1, rounds - 1) as it:
                pe_round(it, False, False)
            pe_round(rounds - 1, False, True)
            pe.wait_ge(s_vx, NE)
            pe.wait_ge(s_vy, NE)
            pe.wait_ge(s_ay, NE)
            beyond = pe.value_load(eidI[0:1, OVER:OVER + 1], min_val=0, max_val=OVER)
            with pe.If(beyond > 0):
                with pe.Fori(0, OVER) as n:
                    pe.wait_ge(s_ogx, n * 16 + 16)
                    transposes(0).then_inc(s_oP, 1)
                    pe.wait_ge(s_oV, n * 3 + 1)
                    pe.wait_ge(s_ow, n * 48 + 48)
                    gate_up_products(0).then_inc(s_oP, 1)
                    pe.wait_ge(s_oV, n * 3 + 2)
                    pe.transpose(bA[:, 0:P], act_f, ident).then_inc(s_oP, 1)
                    pe.wait_ge(s_oA, n * 3 + 2)
                    down_products(0).then_inc(s_oP, 1)
            with pe.Else():
                pe.wait_ge(s_vx, NE)

        @block.scalar
        def _(act):
            chain = [0]

            def link(ins):
                chain[0] += 1
                ins.then_inc(a_ch, 1)
                act.wait_ge(a_ch, chain[0])

            act.wait_ge(s_eps, 1)
            for t in range(TILES + 1):
                R = tile_rows(t)
                act.wait_ge(s_x[t], 16)
                ms = small[0:R, t:t + 1]
                link(act.activation(junk[0:R, :], x[0:R, t, :], ACT.Square, accum_out=ms))
                act.activation(ms, ms, ACT.Sqrt, scale=1.0 / D, bias=small[0:R, 41:42]).then_inc(s_sq, 1)
            act.wait_ge(s_mem, 16)
            for t in range(2):
                ms = small[:, 5 + t:6 + t]
                link(act.activation(junk, memX[:, t, :], ACT.Square, accum_out=ms))
                act.activation(ms, ms, ACT.Sqrt, scale=1.0 / D, bias=small[:, 41:42]).then_inc(s_sq, 1)
            def from_psum(keys, write):
                for key in keys:
                    o = filled(act, key)
                    write(key, o).then_inc(evac["a"], 1)

            def projected(key, o):
                _, j, s = key
                dst = PR[:, j, 1 + s * HALF:1 + (s + 1) * HALF] if j < RW else SQ[:, j - RW, s * HALF:(s + 1) * HALF]
                return act.copy(dst, o[:, 0:HALF])

            def lora_sigmoid(key, o):
                name, c, s = key
                dst, bias = (sg, "w_decay0") if name == "lora_w" else (aa, "a0")
                return act.activation(dst[:, c, s * HALF:(s + 1) * HALF], o[:, 0:HALF], ACT.Sigmoid,
                                      bias=pcol(bias, c))

            def memory(key, o):
                name, t = key
                if name == "mkT":
                    return act.copy(mkT[:, :, t * P:(t + 1) * P], o[:, :].rearrange("p (h s) -> p h s", h=XH))
                return act.copy((mkS if name == "mk" else mv)[:, t, :], o[:, :])

            for what, n in FRONT_ORDER:
                if what == "proj":
                    from_psum([("proj", n, s) for s in range(2)], projected)
                elif what == "lora_in":
                    act.wait_ge(s_mix, 2)
                    link(act.activation(PR[0:64, 12, 1:1 + NT], PR[0:64, 12, 1:1 + NT], ACT.Tanh))
                    act.activation(PR[:, 13, 1:1 + NT], PR[:, 13, 1:1 + NT], ACT.Sigmoid).then_inc(s_act, 1)
                elif what == "lora":
                    from_psum([(key, c, s) for key in ("lora_w", "lora_a") for c in range(4) for s in range(2)],
                              lora_sigmoid)
                elif what == "mem":
                    from_psum([(key, t) for key in ("mk", "mv", "mkT") for t in range(2)], memory)
                elif what == "sums":
                    from_psum([("norm_k", n, s) for s in range(2)],
                              lambda key, o: act.activation(sq[n % 2][:, key[2] * HALF:(key[2] + 1) * HALF],
                                                            o[:, 0:HALF], ACT.Sqrt))
                    act.wait_ge(s_cs, n + 1)
                    act.activation(wS[:, n, :], sg[:, n, SEQ:NT], ACT.Exp, scale=-KAPPA)
                    act.activation(csum[n % 2][:, 0:SEQ], csum[n % 2][:, 0:SEQ], ACT.Exp, scale=-KAPPA) \
                        .then_inc(s_ep, 1)
                    act.activation(tail[n % 2][:, 0:SEQ], tail[n % 2][:, 0:SEQ], ACT.Exp, scale=-KAPPA) \
                        .then_inc(s_ep, 1)
            act.wait_ge(s_prep, 4)
            for i in range(4):
                o = filled(act, ("shift_out", i))
                n = min(4, RW - 4 * i) * P
                act.copy(shiftO[:, i * 512:i * 512 + n], o[0:9, 0:n]).then_inc(evac["a"], 1)
            for i in range(6):
                o = filled(act, ("svec", i))
                act.copy(svt6[:, i, :], o[0:NS, :]).then_inc(evac["a"], 1)
            act.wait_ge(s_shout, 32)
            for t in range(TILES):
                o = filled(act, ("tokV", t))
                act.copy(tokV[:, t, :], o[:, :]).then_inc(evac["a"], 1)
            def exps(n, rows, heads, W, sink):
                act.wait_ge(s_max, n + 1)
                stat = stats[n % 2]
                sm = (SmW if n < 5 else Sm)[n % 2][0:rows, 0:heads * (2048 // H if heads == H else 256)] \
                    .rearrange("p (h s) -> p h s", h=heads)
                if sink:
                    link(act.activation(stat[0:rows, 24:24 + heads], stat[0:rows, 24:24 + heads], ACT.Exp))
                for h in range(heads):
                    ins = act.activation(sm[:, h, 0:W], sm[:, h, 0:W], ACT.Exp, bias=stat[0:rows, 8 + h:9 + h],
                                         accum_out=stat[0:rows, 16 + h:17 + h])
                ins.then_inc(s_exp, 1)

            for what, t, n in RECUR_ORDER:
                if what == "vk":
                    o = filled(act, ("vtok",))
                    act.copy(vtok, o[:, :].rearrange("p (t n) -> p t n", t=4)).then_inc(evac["a"], 1)
                    o = filled(act, ("kvout",))
                    link(act.copy(kvO[:, 0:P], o[:, 0:P]))
                    act.copy(kvO[0:NS, P:3 * P], o[0:NS, P:3 * P]).then_inc(evac["a"], 1)
                elif what == "ws":
                    exps(t, P, H, P if t == 0 else 2 * P, True)
                elif what == "wp":
                    na = 1 if t == 0 else 2
                    for i in range(4):
                        o = filled(act, ("pT", t, i))
                        act.copy(PTa[:, 2 * i:2 * i + 2, 0:na, :],
                                 o[:, :].rearrange("p (n a q) -> p n a q", n=2, a=2)[:, :, 0:na, :]) \
                            .then_inc(evac["a"], 1)
                    o = filled(act, ("o", t))
                    if t == 0:
                        act.wait_ge(s_sso, 16)
                    act.copy(yT[:, 4:8, t * P:(t + 1) * P], o[:, :].rearrange("p (c q) -> p c q", c=4)) \
                        .then_inc(evac["a"], 1)
                elif what == "tok":
                    for i in range(3):
                        o = filled(act, ("tok", t, i))
                        act.copy(tokXs[t % 2][i], o[:, :]).then_inc(evac["a"], 1)
                elif what == "N0":
                    for q in range(2):
                        o = filled(act, ("N0", t, q))
                        act.copy(Ni[0][:, 4 * q:4 * q + 4, :], o[:, :].rearrange("p (h t) -> p h t", h=4)) \
                            .then_inc(evac["a"], 1)
                elif what == "level":
                    for q in range(2):
                        for key, dst in (("MM", Mi), ("NN", Ni)):
                            if (key, t, q, n) in rank and rank[(key, t, q, n)][0] == "a":
                                o = filled(act, (key, t, q, n))
                                act.copy(dst[(n + 1) % 2][:, 4 * q:4 * q + 4, :],
                                         o[:, :].rearrange("p (h t) -> p h t", h=4)).then_inc(evac["a"], 1)
                elif what == "fin":
                    o = filled(act, ("WT", t))
                    act.copy(WT, o[:, :].rearrange("p (c t) -> p c t", c=4)).then_inc(evac["a"], 1)
                elif what == "Y":
                    o = filled(act, ("Y", t))
                    if t == 0:
                        act.wait_ge(s_bv, 4)
                    act.copy(yT[:, 0:4, t * P:(t + 1) * P], o[:, :].rearrange("p (c t) -> p c t", c=4)) \
                        .then_inc(evac["a"], 1)
            o = filled(act, ("wkvT",))
            act.copy(wkvO, o[0:64, :]).then_inc(evac["a"], 1)
            act.wait_ge(s_kvw, 32)
            act.wait_ge(s_newkv, 32)
            for c in range(4):
                for s in range(2):
                    o = filled(act, ("gate", c, s))
                    act.copy(gateS[:, c, s * HALF:(s + 1) * HALF], o[:, 0:HALF]).then_inc(evac["a"], 1)
            for c in range(4):
                for s in range(2):
                    o = filled(act, ("var", c, s))
                    act.activation(ydev[:, c, s * HALF:(s + 1) * HALF], o[:, 0:HALF], ACT.Sqrt, scale=1.0 / HD,
                                   bias=small[:, 40:41]).then_inc(evac["a"], 1)
            for i in range(2):
                o = filled(act, ("kT", i))
                act.copy(kTs[:, 4 * i:4 * i + 4, :], o[:, :].rearrange("p (b s) -> p b s", b=4)) \
                    .then_inc(evac["a"], 1)
            exps(4, 64, 1, P, True)

            def row_norms(first, sem):
                for t in range(TILES + 1):
                    R = tile_rows(t)
                    act.wait_ge(evac["v"], sem[t])
                    ms = small[0:R, t:t + 1]
                    link(act.activation(junk[0:R, :], x[0:R, t, :], ACT.Square, accum_out=ms))
                    act.activation(ms, ms, ACT.Sqrt, scale=1.0 / D, bias=small[0:R, 41:42]).then_inc(s_sq2, 1)

            row_norms(0, [rank[("wo", t, 1)][1] for t in range(5)])
            for h in range(XH):
                for s in range(2):
                    o = filled(act, ("q", h, s))
                    act.copy(qT[:, h, s * HALF:(s + 1) * HALF], o[:, 0:HALF]).then_inc(evac["a"], 1)
            for what, n in CROSS_ORDER:
                if what == "xs":
                    exps(5 + n, P, XH, MT, False)
                elif what == "xp":
                    for i in range(2):
                        o = filled(act, ("xpT", n, i))
                        act.copy(PTc[:, 2 * i:2 * i + 2, :, :], o[:, :].rearrange("p (n a q) -> p n a q", n=2, a=2)) \
                            .then_inc(evac["a"], 1)
                    o = filled(act, ("xo", n))
                    act.copy(yT[:, 0:4, n * P:(n + 1) * P], o[:, :].rearrange("p (c q) -> p c q", c=4)) \
                        .then_inc(evac["a"], 1)
                elif what == "ckT":
                    for st in range(2):
                        o = filled(act, ("ckT", n, st))
                        act.copy(KT[n % 2][:, :, st, :], o[:, :].rearrange("p (h s) -> p h s", h=XH)) \
                            .then_inc(evac["a"], 1)
            exps(9, 32, 1, MT, False)
            row_norms(5, [rank[("wc", t, 1)][1] for t in range(5)])
            act.wait_ge(s_exp1, 1)
            act.activation(Ta[:, :, 0:4], Ta[:, :, 0:4], ACT.Exp).then_inc(s_exp2, 1)
            act.wait_ge(s_exp1, 2)
            act.activation(ee, ee, ACT.Exp).then_inc(s_exp2, 1)
            bG, bA, bY = [banks[2], banks[6]], banks[3], banks[5]

            def act_block(i, b, r, first=False):
                act.wait_ge(s_pG, b + 1)
                act.activation(silu, bG[i % 2][0:BS, 0:FH], ACT.Silu).then_inc(s_as, 1)
                act.wait_ge(s_pA, b + 1)
                act.copy(actT, bA[:, 0:BS]).then_inc(s_aa, 1)
                act.wait_ge(s_pY, b + 1)
                if not first:
                    act.wait_ge(s_ys[i], r * 16)
                act.copy(yb[i][:, 512:1024], bY[0:BS, :]).then_inc(s_ay, 1)

            for i in range(NB3):
                act_block(i, i, 0, True)
            with act.Fori(1, NE // NB3) as it:
                for i in range(NB3):
                    act_block(i, it * NB3 + i, it)
            beyond = act.value_load(eidI[0:1, OVER:OVER + 1], min_val=0, max_val=OVER)
            with act.If(beyond > 0):
                act.wait_ge(s_ys[0], 16 * (NE // NB3))
                with act.Fori(0, OVER) as n:
                    act.wait_ge(s_oP, n * 4 + 2)
                    act.activation(silu, bG[0][0:BS, 0:FH], ACT.Silu).then_inc(s_oA, 1)
                    act.wait_ge(s_oP, n * 4 + 3)
                    act.copy(actT, bA[:, 0:BS]).then_inc(s_oA, 1)
                    act.wait_ge(s_oP, n * 4 + 4)
                    act.copy(yb[0][:, 512:1024], bY[0:BS, :]).then_inc(s_oA, 1)
            with act.Else():
                act.wait_ge(s_pY, NE)
            for t in range(T5):
                R = tile_rows(t)
                act.wait_ge(s_comb, t + 1)
                ms = small[0:R, t:t + 1]
                link(act.activation(junk[0:R, :], x[0:R, t, :], ACT.Square, accum_out=ms))
                act.activation(ms, ms, ACT.Sqrt, scale=1.0 / D, bias=small[0:R, 41:42]).then_inc(s_sq3, 1)

        @block.vector
        def _(dve):
            chain = [0]

            def link(ins):
                chain[0] += 1
                ins.then_inc(v_ch, 1)
                dve.wait_ge(v_ch, chain[0])

            tt, ts, stt = dve.tensor_tensor, dve.tensor_scalar, dve.scalar_tensor_tensor
            link(dve.memset(PR[:, :, 0:1], 0.0))
            link(dve.memset(small[:, 40:41], GN_EPS))
            dve.memset(small[:, 41:42], EPS).then_inc(s_eps, 1)
            o = filled(dve, ("par",))
            dve.tensor_copy(par[:, 0:42], o[:, 0:42]).then_inc(evac["v"], 1)
            o = filled(dve, ("shift_in",))
            dve.tensor_copy(shiftS, o[:, 0:RW * NS].rearrange("p (j n) -> p j n", j=RW)).then_inc(evac["v"], 1)

            def first_rows(t):
                R = tile_rows(t) if t < 5 else P
                rows = x[0:R, t, :] if t < 5 else memX[:, t - 5, :]
                dve.wait_ge(s_sq, t + 1)
                ms = small[0:R, t:t + 1]
                link(dve.reciprocal(ms, ms))
                ts(rows, rows, ms, None, ALU.mult).then_inc(s_xn, 1)

            def first_gained(t):
                R = tile_rows(t)
                for i in range(2):
                    o = filled(dve, ("xT", t, i))
                    g = gains[:, 0, 4 * i:4 * i + 4].unsqueeze(2).to_broadcast([P, 4, R])
                    tt(hA[:, 4 * i:4 * i + 4, t * P:t * P + R],
                       o[:, :].rearrange("p (k n) -> p k n", k=4)[:, :, 0:R], g, ALU.mult) \
                        .then_inc(evac["v"], 1)

            first_rows(0)
            for t in range(1, 5):
                first_rows(t)
                first_gained(t - 1)
            first_gained(4)
            first_rows(5)
            first_rows(6)

            def mix(n, j):
                done(dve, ("proj", j, 1))
                link(dve.tensor_copy(saved[:, j, :], PR[:, j, SEQ:SEQ + 9]))
                d = diffs[n % 2]
                tt(d[:, 0:SEQ], PR[:, j, 0:SEQ], PR[:, j, 1:1 + SEQ], ALU.subtract)
                link(tt(d[:, SEQ:NT], shiftS[:, j, :], PR[:, j, 1 + SEQ:1 + NT], ALU.subtract))
                ins = stt(PR[:, j, 1:1 + NT], d, pcol("mu_shift", j), PR[:, j, 1:1 + NT], ALU.mult, ALU.add)
                ins.then_inc(s_mix, 1)

            def memory_gained():
                for t in range(2):
                    for i in range(2):
                        o = filled(dve, ("mT", t, i))
                        g = gains[:, 1, 4 * i:4 * i + 4].unsqueeze(2).to_broadcast([P, 4, P])
                        tt(memT[:, 4 * i:4 * i + 4, t * P:(t + 1) * P],
                           o[:, :].rearrange("p (k n) -> p k n", k=4), g, ALU.mult).then_inc(evac["v"], 1)
                link(dve.memset(reset, 1.0))
                link(dve.memset(reset.rearrange("p (n t) -> p n t", t=CH)[:, :, 0:1], 0.0))
                link(ts(small[:, 48:52], par[:, PARC["k_a"]:PARC["k_a"] + 4], -1.0, 1.0, ALU.mult, ALU.add))

            def chunked(a):
                return a[:, 0:SEQ].rearrange("p (n t) -> p n t", t=CH)

            def before_sums(c, mixed):
                dve.wait_ge(s_mix, mixed)
                R_, K_ = PR[:, c, 1:1 + NT], PR[:, 4 + c, 1:1 + NT]
                kk, cs = B0[:, c, :], csum[c % 2]
                done(dve, ("lora_a", c, 1))
                link(ts(kk, K_, pcol("k_k", c), None, ALU.mult))
                tt(sq[c % 2], kk, kk, ALU.mult).then_inc(s_kk, 1)
                link(ts(tmp[8], aa[:, c, :], pcol("k_a", c), small[:, 48 + c:49 + c], ALU.mult, ALU.add))
                link(tt(K_, K_, tmp[8], ALU.mult))
                stt(B1[:, c, :], R_, pcol("r_k", c), K_, ALU.mult, ALU.mult).then_inc(s_rk, 1)
                link(dve.tensor_tensor_scan(cs[:, 0:SEQ], reset, sg[:, c, 0:SEQ], 0.0, ALU.mult, ALU.add))
                tt(chunked(tail[c % 2]), chunked(cs)[:, :, CH - 1:CH].to_broadcast([P, NCH, CH]), chunked(cs),
                   ALU.subtract).then_inc(s_cs, 1)

            def after_sums(c):
                R_, K_ = PR[:, c, 1:1 + NT], PR[:, 4 + c, 1:1 + NT]
                kk, b, norm = B0[:, c, :], B1[:, c, :], sq[c % 2]
                decay, left = csum[c % 2], tail[c % 2]
                done(dve, ("norm_k", c, 1))
                link(ts(norm, norm, L2_EPS, None, ALU.max))
                link(dve.reciprocal(norm, norm))
                link(tt(kk, kk, norm, ALU.mult))
                for s in range(2):
                    o = filled(dve, ("bonus", c, s))
                    dve.tensor_copy(yT[:, c, s * HALF:(s + 1) * HALF], o[:, 0:HALF]).then_inc(evac["v"], 1)
                link(tt(b, kk, aa[:, c, :], ALU.mult))
                dve.wait_ge(s_ep, 2 * c + 1)
                dve.tensor_copy(PC[:, c, :], chunked(decay)[:, :, CH - 1])
                tt(R_[:, 0:SEQ], R_[:, 0:SEQ], decay[:, 0:SEQ], ALU.mult)
                stt(chunked(kk)[:, :, 1:CH], chunked(kk)[:, :, 1:CH], -1.0, chunked(decay)[:, :, 0:CH - 1],
                    ALU.mult, ALU.mult)
                ts(chunked(kk)[:, :, 0:1], chunked(kk)[:, :, 0:1], -1.0, None, ALU.mult)
                ts(kk[:, SEQ:NT], kk[:, SEQ:NT], -1.0, None, ALU.mult)
                dve.wait_ge(s_ep, 2 * c + 2)
                tt(b[:, 0:SEQ], b[:, 0:SEQ], left[:, 0:SEQ], ALU.mult)
                tt(K_[:, 0:SEQ], K_[:, 0:SEQ], left[:, 0:SEQ], ALU.mult).then_inc(s_prep, 1)
                dve.wait_ge(s_prep, c + 1)

            dve.wait_ge(evac["v"], 2)
            mixed = 0
            for what, n in FRONT_ORDER:
                if what == "proj" and n < RW:
                    mix(mixed, n)
                    mixed += 1
                elif what == "mT":
                    memory_gained()
                elif what == "pre":
                    before_sums(n, mixed)
                elif what == "post":
                    after_sums(n)
            dve.reciprocal(small[:, 8:40].rearrange("p (c n) -> p c n", c=4), PC).then_inc(s_inv, 1)
            done(dve, ("tokV", 3))
            done(dve, ("svec", 5))
            for c in range(4):
                V_ = PR[:, 8 + c, 1:1 + NT]
                tt(V_, V_, yT[:, c, :], ALU.mult).then_inc(s_bv, 1)
            dve.memset(ST[:, 0, :, :], 0.0).then_inc(s_vz, 1)
            dve.wait_ge(s_vz, 1)

            def softmax(n, rows, heads, W, sink):
                sm = (SmW if n < 5 else Sm)[n % 2][0:rows, 0:heads * 256].rearrange("p (h s) -> p h s", h=heads)[:, :, 0:W]
                stat = stats[n % 2]
                mx, neg, snk = stat[0:rows, 0:heads], stat[0:rows, 8:8 + heads], stat[0:rows, 24:24 + heads]
                link(dve.tensor_reduce(mx, sm, X, ALU.max))
                if sink is not None:
                    link(tt(mx, mx, sink, ALU.max))
                    link(tt(snk, sink, mx, ALU.subtract))
                ts(neg, mx, -1.0, None, ALU.mult).then_inc(s_max, 1)

            def normalise(n, rows, heads, W, sink):
                sm = (SmW if n < 5 else Sm)[n % 2][0:rows, 0:heads * 256].rearrange("p (h s) -> p h s", h=heads)[:, :, 0:W]
                stat = stats[n % 2]
                sums, snk = stat[0:rows, 16:16 + heads], stat[0:rows, 24:24 + heads]
                dve.wait_ge(s_exp, n + 1)
                if sink is not None:
                    link(tt(sums, sums, snk, ALU.add))
                link(dve.reciprocal(sums, sums))
                tt(sm, sm, sums.unsqueeze(2).to_broadcast([rows, heads, W]), ALU.mult).then_inc(s_prob, 1)

            def window_tile(t):
                W = P if t == 0 else 2 * P
                sm = SmW[t % 2].rearrange("p (h s) -> p h s", h=H)
                band = swamask[:, 2 * P - W:].unsqueeze(1).to_broadcast([P, 2, W])
                for e in range(2):
                    for i in range(2):
                        o = filled(dve, ("s", t, e, i))
                        stt(sm[:, 4 * i + e:4 * i + e + 3:2, 0:W], o[:, 0:2 * W].rearrange("p (n s) -> p n s", n=2),
                            HD ** -0.5, band, ALU.mult, ALU.add).then_inc(evac["v"], 1)
                done(dve, ("s", t, 1, 1))
                softmax(t, P, H, W, sinks[:, 0:H])

            for what, t, n in RECUR_ORDER:
                hs = slice(n * HALF, (n + 1) * HALF)
                if what == "sample" and n == 0:
                    dve.wait_ge(s_sa, 1)
                    dve.tensor_reduce(ssa, Stmp, X, ALU.add).then_inc(s_ssa, 1)
                elif what == "sample":
                    dve.wait_ge(s_ss, 1)
                    link(tt(Stmp, SS, sv[:, 4, :].unsqueeze(1).to_broadcast([P, 32, HD]), ALU.mult))
                    dve.tensor_reduce(sy, Stmp, X, ALU.add).then_inc(s_ss, 1)
                elif what == "rq":
                    o = filled(dve, ("rq", t, n))
                    tt(ropeT, o[:, 0:HALF], sinT[:, hs], ALU.mult).then_inc(evac["v"], 1)
                    link(tt(SQ[:, t, hs], SQ[:, t, hs], cosT[:, hs], ALU.mult))
                    done(dve, ("rq", t, n))
                    link(tt(SQ[:, t, hs], SQ[:, t, hs], ropeT, ALU.add))
                elif what == "rk":
                    o = filled(dve, ("rka", t, n))
                    tt(RK[t][:, hs], o[:, 0:HALF], cosT[:, hs], ALU.mult).then_inc(evac["v"], 1)
                    o = filled(dve, ("rkb", t, n))
                    tt(ropeT, o[:, 0:HALF], sinT[:, hs], ALU.mult).then_inc(evac["v"], 1)
                    done(dve, ("rkb", t, n))
                    link(tt(RK[t][:, hs], RK[t][:, hs], ropeT, ALU.add))
                elif what == "vk":
                    dve.memset(small[:, 43:44], 0.0).then_inc(s_rope, 1)
                    dve.wait_ge(s_sink, 32)
                elif what == "ws":
                    window_tile(t)
                elif what == "wp":
                    normalise(t, P, H, P if t == 0 else 2 * P, sinks)
                elif what == "AB":
                    if t == 1 and n == 0:
                        dve.wait_ge(s_ss, 2)
                        dve.wait_ge(s_svd, 32)
                    for h in range(4 * n, 4 * n + 4):
                        o = filled(dve, ("AB", t, h))
                        tt(ABs[t % 2][:, h, :, :], o[:, :].rearrange("p (a t) -> p a t", a=4), maskAB, ALU.mult) \
                            .then_inc(evac["v"], 1)
                elif what == "N0":
                    for q in range(2):
                        for h in range(4 * q, 4 * q + 4):
                            done(dve, ("AB", t, h))
                        if t > 0:
                            done(dve, ("G", t - 1))
                            done(dve, ("WT", t - 1))
                        idb = ident.unsqueeze(1).to_broadcast([P, 4, P])
                        tt(Xi[:, 4 * q:4 * q + 4, :], ABs[t % 2][:, 4 * q:4 * q + 4, 0, :], idb, ALU.add) \
                            .then_inc(s_st, 1)
                    dve.wait_ge(s_st, 2 * t + 2)
                elif what == "level":
                    for q in range(2):
                        qs = slice(4 * q, 4 * q + 4)
                        if n > 0:
                            o = filled(dve, ("XM", t, q, n))
                            tt(Xi[:, qs, :], Xi[:, qs, :], o[:, :].rearrange("p (h t) -> p h t", h=4), ALU.add) \
                                .then_inc(evac["v"], 1)
                        if n < 5 and rank[("NN", t, q, n)][0] == "v":
                            o = filled(dve, ("NN", t, q, n))
                            dve.tensor_copy(Ni[(n + 1) % 2][:, qs, :], o[:, :].rearrange("p (h t) -> p h t", h=4)) \
                                .then_inc(evac["v"], 1)
                elif what == "fin":
                    for key, dst in (("akv", akv), ("G", Gt)):
                        o = filled(dve, (key, t))
                        dve.tensor_copy(dst, o[:, :]).then_inc(evac["v"], 1)
                    done(dve, ("G", t))
                elif what == "U":
                    tk, m = 64 * n, 2 * t + n
                    if m > 0:
                        done(dve, ("S", m // 2 if m % 2 else m // 2 - 1, (m + 1) % 2))
                    link(tt(ST[:, m + 1, :, :], ST[:, m, :, :],
                            PC[:, :, m:m + 1].to_broadcast([P, 4, HD]), ALU.mult))
                    for e in range(2):
                        o = filled(dve, ("U", t, n, e))
                        of = [a[tk:tk + 64, :].rearrange("p (c e i) -> p c e i", e=2, i=HD)[:, :, e, :]
                              for a in (Ut, Gt)]
                        tt(of[0], o[tk:tk + 64, 0:256].rearrange("p (c i) -> p c i", c=4), of[1], ALU.add) \
                            .then_inc(evac["v"], 1)
                elif what == "S":
                    m = 2 * t + n
                    o = filled(dve, ("S", t, n))
                    tt(ST[:, m + 1, :, :], ST[:, m + 1, :, :], o[:, 0:256].rearrange("p (c i) -> p c i", c=4),
                       ALU.add).then_inc(evac["v"], 1)
            o = filled(dve, ("ysT",))
            dve.tensor_copy(yT[:, 0:4, SEQ:NT], o[:, 0:4 * NS].rearrange("p (c n) -> p c n", c=4)) \
                .then_inc(evac["v"], 1)
            for c in range(4):
                for s in range(2):
                    o = filled(dve, ("mean", c, s))
                    hs = slice(s * HALF, (s + 1) * HALF)
                    stt(yT[:, c, hs], o[:, 0:HALF], -1.0 / HD, yT[:, c, hs], ALU.mult, ALU.add) \
                        .then_inc(evac["v"], 1)
                done(dve, ("mean", c, 1))
                tt(ysq[:, c, :], yT[:, c, :], yT[:, c, :], ALU.mult).then_inc(s_yc, 1)
            for e in range(2):
                o = filled(dve, ("qd", e))
                dve.tensor_copy(QD[:, :, :, e], o[:, 0:32].rearrange("p (c b) -> p b c", c=4)).then_inc(evac["v"], 1)

            def deviation_divided(c):
                done(dve, ("var", c, 1))
                link(dve.reciprocal(ydev[:, c, :], ydev[:, c, :]))
                link(tt(yT[:, c, :], yT[:, c, :], ydev[:, c, :], ALU.mult))
                link(ts(yT[:, c, :], yT[:, c, :], pcol("ln_x_w", c), pcol("ln_x_b", c), ALU.mult, ALU.add))
                link(tt(yT[:, c, :], yT[:, c, :], PR[:, 8 + c, 1:1 + NT], ALU.add))

            deviation_divided(0)
            deviation_divided(1)
            for g in range(2):
                o = filled(dve, ("ss", g))
                dve.tensor_copy(sT.rearrange("p (b g m) -> p b g m", b=NS, g=2)[:, :, g, :],
                                o[:, 0:32].rearrange("p (b m) -> p b m", b=NS)).then_inc(evac["v"], 1)
            o = filled(dve, ("ssT",))
            ts(SmW[0][0:64, 0:P], o[0:64, 0:P], HD ** -0.5, None, ALU.mult).then_inc(evac["v"], 1)
            done(dve, ("ssT",))
            softmax(4, 64, 1, P, sinks[0:64, H:H + 1])
            deviation_divided(2)
            normalise(4, 64, 1, P, sinks)
            o = filled(dve, ("spT",))
            dve.tensor_copy(pTs, o[:, 0:64]).then_inc(evac["v"], 1)
            deviation_divided(3)
            done(dve, ("gate", 3, 1))
            for c in range(4):
                ins = tt(yT[:, c, :], yT[:, c, :], gateS[:, c, :], ALU.mult)
            ins.then_inc(s_fin, 1)
            o = filled(dve, ("so",))
            dve.tensor_copy(yT[:, 4:8, SEQ:NT], o[:, 0:32].rearrange("p (c b) -> p c b", c=4)) \
                .then_inc(evac["v"], 1)


            def residual(key, first, gi, hkey):
                for t in range(TILES + 1):
                    R = tile_rows(t)
                    if key == "wo":
                        dve.wait_ge(s_xr[t], 16)
                    for n in range(2):
                        o = filled(dve, (key, t, n))
                        ns = slice(n * 512, (n + 1) * 512)
                        tt(x[0:R, t, ns], x[0:R, t, ns], o[0:R, :], ALU.add).then_inc(evac["v"], 1)
                    if t >= 1:
                        gained(hkey, t - 1, gi)
                    dve.wait_ge(s_sq2, first + t + 1)
                    ms = small[0:R, t:t + 1]
                    link(dve.reciprocal(ms, ms))
                    if t >= 2 and key == "wc":
                        dve.wait_ge(s_hn[t % 2], 16 * (t // 2))
                    ts(xn[t % 2][0:R, :], x[0:R, t, :], ms, None, ALU.mult).then_inc(s_xn2, 1)
                gained(hkey, 4, gi)

            def gained(hkey, t, gi):
                R = tile_rows(t)
                for i in range(2):
                    o = filled(dve, (hkey, t, i))
                    g = gains[:, gi, 4 * i:4 * i + 4].unsqueeze(2).to_broadcast([P, 4, R])
                    tt(hA[:, 4 * i:4 * i + 4, t * P:t * P + R],
                       o[:, :].rearrange("p (k n) -> p k n", k=4)[:, :, 0:R], g, ALU.mult).then_inc(evac["v"], 1)

            dve.wait_ge(s_kvw, 32)
            residual("wo", 0, 2, "xT2")
            for what, n in CROSS_ORDER:
                if what == "xs":
                    sm = Sm[(5 + n) % 2][:, 0:1024].rearrange("p (h s) -> p h s", h=XH)
                    for i in range(2):
                        o = filled(dve, ("xs", n, i))
                        ts(sm[:, 2 * i:2 * i + 2, :], o[:, :].rearrange("p (n s) -> p n s", n=2), P ** -0.5, None,
                           ALU.mult).then_inc(evac["v"], 1)
                    done(dve, ("xs", n, 1))
                    softmax(5 + n, P, XH, MT, None)
                    if n > 0:
                        normalise(4 + n, P, XH, MT, None)
                    if n == TILES - 1:
                        normalise(5 + n, P, XH, MT, None)
                elif what == "cs":
                    o = filled(dve, ("cs", n))
                    dve.tensor_copy(csS[:, :, 4 * n:4 * n + 4], o[:, 0:8].rearrange("p (a h) -> p a h", a=2)) \
                        .then_inc(evac["v"], 1)
            o = filled(dve, ("csT",))
            ts(Sm[1][0:32, 0:MT], o[0:32, 0:MT], P ** -0.5, None, ALU.mult).then_inc(evac["v"], 1)
            done(dve, ("csT",))
            softmax(9, 32, 1, MT, None)
            normalise(9, 32, 1, MT, None)
            o = filled(dve, ("cpT",))
            dve.tensor_copy(cpS, o[:, 0:64].rearrange("p (a n) -> p a n", a=2)).then_inc(evac["v"], 1)
            o = filled(dve, ("co",))
            dve.tensor_copy(yT[:, 0:4, SEQ:NT], o[:, 0:4 * NS].rearrange("p (b h) -> p h b", h=XH)) \
                .then_inc(evac["v"], 1)
            residual("wc", 5, 3, "xT3")
            link(dve.memset(Lg, 0.0))
            dve.memset(onesm, 1.0)
            link(dve.memset(zer, 1.0))
            for t in range(T5):
                R = tile_rows(t)
                o = filled(dve, ("route", t))
                tt(Lg[0:R, t, :], o[0:R, 0:36], rbias[0:R, :], ALU.add).then_inc(evac["v"], 1)
            done(dve, ("route", 4))

            def wide(a, n):
                return a.unsqueeze(2).to_broadcast([P, T5, n])

            def first_max(src, n, top, out):
                io = iota[:, 0:n].unsqueeze(1).to_broadcast([P, T5, n])
                link(dve.tensor_reduce(top, src, X, ALU.max))
                link(tt(out, src, wide(top, n), ALU.is_lt))
                link(stt(out, out, 100.0, io, ALU.mult, ALU.add))
                link(dve.tensor_reduce(mi, out, X, ALU.min))
                link(tt(out, io, wide(mi, n), ALU.is_equal))

            lg, le = Lg[:, :, 0:4], Lg[:, :, 4:36]
            first_max(lg, 4, gmx, ohg)
            tt(Ta[:, :, 0:4], lg, wide(gmx, 4), ALU.subtract).then_inc(s_exp1, 1)
            dve.wait_ge(s_exp2, 1)
            link(dve.tensor_reduce(psel, Ta[:, :, 0:4], X, ALU.add))
            link(dve.reciprocal(psel, psel))
            link(ts(ohg, ohg, -NEG, NEG, ALU.mult, ALU.add))
            for t in range(T5):
                tt(Le[:, t, :].rearrange("p (g e) -> p g e", g=4), le[:, t, :].rearrange("p (g e) -> p g e", g=4),
                   ohg[:, t, :].unsqueeze(2).to_broadcast([P, 4, 8]), ALU.add)
            link(dve.memset(small[:, 44:45], 0.0))
            first_max(Le, NE, m1, oh[0])
            link(stt(Le, oh[0], NEG, Le, ALU.mult, ALU.add))
            first_max(Le, NE, m2, oh[1])
            tt(ee, m2, m1, ALU.subtract).then_inc(s_exp1, 1)
            for j in range(2):
                link(tt(oh[j], oh[j], wide(valid, NE), ALU.mult))
            tt(Mk, oh[0], oh[1], ALU.add).then_inc(s_mk, 1)
            dve.wait_ge(s_exp2, 2)
            link(ts(m1, ee, 1.0, None, ALU.add))
            link(dve.reciprocal(m1, m1))
            link(tt(cw[0], m1, psel, ALU.mult))
            link(tt(cw[1], cw[0], ee, ALU.mult))
            o = filled(dve, ("ranks",))
            dve.tensor_copy(RC, o[:, 0:6 * NE]).then_inc(evac["v"], 1)
            done(dve, ("ranks",))
            cnt_e = RC[:, T5 * NE:]
            link(ts(nb, cnt_e, float(BS - 1), None, ALU.add))
            link(dve.tensor_copy(nbI, nb))
            link(ts(nbI, nbI, BSHIFT, None, ALU.arith_shift_right))
            link(dve.tensor_copy(nb, nbI))
            link(ts(nb, nb, -1.0, 0.0, ALU.add, ALU.max))
            link(dve.tensor_tensor_scan(cum, zer, nb, 0.0, ALU.mult, ALU.add))
            link(tt(nb, cum, nb, ALU.subtract))
            link(stt(nb, nb, float(NE - 1), iota[:, 0:NE], ALU.add, ALU.subtract))
            rk = RC[:, 0:T5 * NE].rearrange("p (t e) -> p t e", t=T5)
            link(ts(far, rk, float(BS), None, ALU.is_ge))
            link(tt(far, far, nb.unsqueeze(1).to_broadcast([P, T5, NE]), ALU.mult))
            link(tt(far, far, iota[:, 0:NE].unsqueeze(1).to_broadcast([P, T5, NE]), ALU.add))
            link(stt(slot_all, far, float(BS), rk, ALU.mult, ALU.add))
            link(ts(mi, valid, -1e6, 1e6, ALU.mult, ALU.add))
            for j in range(2):
                sj = slot[:, j * T5:(j + 1) * T5]
                link(tt(Ta, oh[j], slot_all, ALU.mult))
                link(dve.tensor_reduce(sj, Ta, X, ALU.add))
                link(tt(sj, sj, mi, ALU.add))
            link(dve.tensor_copy(slot_blockI, slot))
            link(ts(slot_blockI, slot_blockI, BSHIFT, None, ALU.arith_shift_right))
            link(dve.tensor_copy(slot_block, slot_blockI))
            link(stt(slot, slot_block, float(-BS), slot, ALU.mult, ALU.add))
            tt(in_block, iota[:, 0:NBLK].unsqueeze(1).to_broadcast([P, J, NBLK]),
               slot_block.unsqueeze(2).to_broadcast([P, J, NBLK]), ALU.is_equal)
            link(tt(in_row, iota[:, 0:BS].unsqueeze(1).to_broadcast([P, J, BS]),
                    slot.unsqueeze(2).to_broadcast([P, J, BS]), ALU.is_equal))
            tt(in_row, in_row, pair_no1.unsqueeze(2).to_broadcast([P, J, BS]), ALU.mult).then_inc(s_slot, 1)
            link(tt(big, cum.unsqueeze(1).to_broadcast([P, OVER, NE]),
                    iota[:, 0:OVER].unsqueeze(2).to_broadcast([P, OVER, NE]), ALU.is_le))
            link(dve.tensor_reduce(eid[:, 0:OVER], big, X, ALU.add))
            link(ts(eid[:, 0:OVER], eid[:, 0:OVER], float(NE - 1), None, ALU.min))
            link(dve.tensor_copy(eid[:, OVER:OVER + 1], cum[:, NE - 1:NE]))
            dve.tensor_copy(eidI, eid).then_inc(s_eid, 1)
            o = filled(dve, ("slots",))
            link(ts(none[0:BS], o[0:BS, 0:NBLK], 0.5, 1e6, ALU.is_lt, ALU.mult))
            stt(pid[0:BS], o[0:BS, 0:NBLK], -1.0, none[0:BS], ALU.add, ALU.add).then_inc(evac["v"], 1)
            done(dve, ("slots",))
            link(dve.tensor_copy(pidI[0:BS], pid[0:BS]))
            ts(tokI[0:BS], pidI[0:BS], 1, None, ALU.arith_shift_right).then_inc(s_idx, 1)
            bX, bG, bY = banks[0], [banks[2], banks[6]], banks[4]

            def rows_gained(i):
                g = gains[:, 3, :].unsqueeze(2).to_broadcast([P, KD, BS])
                return tt(xTe[i % 2], bX[:, 0:KD * BS].rearrange("p (k n) -> p k n", k=KD), g, ALU.mult)

            def rows_out(i, b):
                dve.wait_ge(s_pX, b + 1)
                rows_gained(i).then_inc(s_vx, 1)

            def dve_block(i, b, r, first, nxt):
                dve.wait_ge(s_as, b + 1)
                tt(act_e, silu, bG[i % 2][0:BS, FH:2 * FH], ALU.mult).then_inc(s_vm, 1)
                if nxt:
                    rows_out(i, b + 2)
                dve.wait_ge(s_pY, b + 1)
                if not first:
                    dve.wait_ge(s_ys[i], r * 16)
                dve.tensor_copy(yb[i][:, 0:512], bY[0:BS, :]).then_inc(s_vy, 1)

            rows_out(0, 0)
            rows_out(1, 1)
            rounds = NE // NB3
            for i in range(NB3):
                dve_block(i, i, 0, True, True)
            with dve.Fori(1, rounds - 1) as it:
                for i in range(NB3):
                    dve_block(i, it * NB3 + i, it, False, True)
            for i in range(NB3):
                dve_block(i, (rounds - 1) * NB3 + i, rounds - 1, False, i < NB3 - 2)
            beyond = dve.value_load(eidI[0:1, OVER:OVER + 1], min_val=0, max_val=OVER)
            with dve.If(beyond > 0):
                dve.wait_ge(s_ys[0], 16 * (NE // NB3))
                with dve.Fori(0, OVER) as n:
                    dve.wait_ge(s_oP, n * 4 + 1)
                    rows_gained(0).then_inc(s_oV, 1)
                    dve.wait_ge(s_oA, n * 3 + 1)
                    tt(act_e, silu, bG[0][0:BS, FH:2 * FH], ALU.mult).then_inc(s_oV, 1)
                    dve.wait_ge(s_oP, n * 4 + 4)
                    dve.tensor_copy(yb[0][:, 0:512], bY[0:BS, :]).then_inc(s_oV, 1)
            with dve.Else():
                dve.wait_ge(s_pY, NE)
            def combined(t):
                R = tile_rows(t)
                dve.wait_ge(s_yl[t], 16)
                link(stt(x[0:R, t, :], ydt[t][0:R, 0, :], cw[0][0:R, t:t + 1], x[0:R, t, :], ALU.mult, ALU.add))
                stt(x[0:R, t, :], ydt[t][0:R, 1, :], cw[1][0:R, t:t + 1], x[0:R, t, :], ALU.mult, ALU.add) \
                    .then_inc(s_comb, 1)

            def final_rows(t):
                R = tile_rows(t)
                dve.wait_ge(s_sq3, t + 1)
                ms = small[0:R, t:t + 1]
                link(dve.reciprocal(ms, ms))
                stt(x[0:R, t, :], x[0:R, t, :], ms, gfin[0:R, :], ALU.mult, ALU.mult).then_inc(s_res, 1)

            combined(0)
            for t in range(1, T5):
                combined(t)
                final_rows(t - 1)
            final_rows(T5 - 1)


_INS = ['x_prompt', 'x_sample', 'mem_prompt', 'state_rwkv_shift', 'state_rwkv_wkv', 'cache_swa_k', 'cache_swa_v',
        'cache_mem_k', 'cache_mem_v', 'norm_mix', 'w_in', 'mu_shift', 'w_decay0', 'w_decay_up', 'a0', 'w_a_up',
        'w_g_up', 'k_k', 'k_a', 'r_k', 'ln_x_w', 'ln_x_b', 'attn_sink', 'w_out', 'norm_cross', 'norm_mem', 'w_cq',
        'w_ck', 'w_cv', 'w_co', 'norm_ffn', 'w_group_router', 'b_group_router', 'w_expert_router',
        'b_expert_router', 'w_exp_gate', 'w_exp_up', 'w_exp_down', 'norm_final']
_OUTS = [('y_prompt', (1, 512, 1024)), ('y_sample', (8, 1, 1024)), ('prompt_shift', (1, 1, 1792)),
         ('prompt_wkv', (1, 1, 8, 64, 64)), ('prompt_swa_k', (1, 1, 128, 2, 64)),
         ('prompt_swa_v', (1, 1, 128, 2, 64)), ('prompt_mem_k', (1, 1, 256, 4, 128)),
         ('prompt_mem_v', (1, 1, 256, 4, 128)), ('sample_shift', (1, 8, 1792)), ('sample_wkv', (1, 8, 8, 64, 64)),
         ('sample_swa_k', (1, 8, 128, 2, 64)), ('sample_swa_v', (1, 8, 128, 2, 64))]


def tables():
    i = np.arange(P)
    ident = np.eye(P, dtype=np.float32)
    bones = (i[:, None] // HD == i[None, :] // HD).astype(np.float32)
    strict = bones * (i[:, None] < i[None, :])
    incl = bones * (i[:, None] <= i[None, :])
    diff = i[:, None] + P - np.arange(2 * P)[None, :]
    band = np.where((diff >= 0) & (diff < P), 0.0, NEG)
    tri = (i[:, None] < i[None, :]).astype(np.float32)
    swap = ((i[:, None] ^ 32) == i[None, :]).astype(np.float32)
    dup = [((i[:, None] // HD == g) & (i[:, None] % HD == i[None, :] % HD)).astype(np.float32) for g in range(2)]
    dsw = [((i[:, None] // HD == g) & ((i[:, None] % HD) ^ 32 == i[None, :] % HD)).astype(np.float32)
           for g in range(2)]
    pos = np.concatenate([np.arange(SEQ), np.full(NS, 1024)]).astype(np.float32)
    inv = (np.float32(10000.0) ** (-np.arange(32, dtype=np.float32) * np.float32(2.0) / np.float32(64)))
    ang = (pos[None, :] * inv.astype(np.float32)[:, None]).astype(np.float32)
    cos = np.tile(np.cos(ang), (4, 1))
    sin = np.tile(np.concatenate([-np.sin(ang), np.sin(ang)]), (2, 1))
    misc = np.zeros((P, MISC), np.float32)
    misc[:, 0:COUNT] = np.arange(COUNT)
    tok = np.arange(TILES + 1)[None, :] * P + i[:, None]
    misc[:, COUNT:COUNT + 10] = (2 * tok[:, None, :] + np.arange(2)[:, None] + 1).reshape(P, 10)
    misc[:, COUNT + 10:COUNT + 15] = tok < NT
    parts = [ident, bones, strict, incl, strict, incl, band, tri, swap, dup[0], dup[1], dsw[0], dsw[1], cos, sin, misc]
    return np.concatenate(parts, axis=1).astype(np.float32)


def kernel(**inputs):
    import concourse.bacc as _bacc
    from concourse.bass_utils import run_bass_kernel_spmd as _run

    nc = _bacc.Bacc("TRN2", target_bir_lowering=False, num_devices=1)
    arrays, A, O = {}, {}, {}
    for name in _INS:
        a = np.ascontiguousarray(inputs[name])
        arrays[f"in_{name}"] = a
        A[name] = nc.dram_tensor(f"in_{name}", a.shape, mybir.dt.from_np(a.dtype), kind="ExternalInput").ap()
    c = tables()
    arrays["in_tables"] = c
    A["c_tables"] = nc.dram_tensor("in_tables", c.shape, F32, kind="ExternalInput").ap()
    for name, shape in _OUTS:
        O[name] = nc.dram_tensor(f"out_{name}", shape, F32, kind="ExternalOutput").ap()
    small_kernel(nc, A, O)
    r = _run(nc, [arrays], core_ids=[0])
    return tuple(r.results[0][f"out_{name}"] for name, _ in _OUTS)
```
